# Optimizing a Trainium2 kernel written in Bass

```python
import jax, jax.numpy as jnp
from jax import lax
import numpy as np
import math

D_MODEL = 1024
BATCH = 1
SEQ = 256
DEPTH = 1

N_META = 16
HEAD_DIM = 64
ATTN_HEADS = (D_MODEL // 2) // HEAD_DIM
KV_HEADS = 2
GQA_GROUP = ATTN_HEADS // KV_HEADS
ATTN_WIDTH = ATTN_HEADS * HEAD_DIM
KV_WIDTH = KV_HEADS * HEAD_DIM
LRU_WIDTH = D_MODEL // 2
LRU_BLOCKS = 8
LRU_BLOCK = LRU_WIDTH // LRU_BLOCKS
LRU_C = 8.0
CONV_WIDTH = 4
WINDOW = 128
BLOCK = 128
PAD = BLOCK - N_META
MIX_WIDTH = ATTN_WIDTH + LRU_WIDTH
IN_WIDTH = ATTN_WIDTH + 2 * KV_WIDTH + 2 * LRU_WIDTH
D_FF = 4 * D_MODEL
EPS = 1e-6
NEG = -1e30


def rmsnorm(x, g):
    xf = x.astype(jnp.float32)
    y = xf * lax.rsqrt(jnp.mean(xf * xf, axis=-1, keepdims=True) + EPS)
    return (y * g.astype(jnp.float32)).astype(x.dtype)

def causal_depthwise_conv(x, w, b):
    c = x.shape[-1]
    y = lax.conv_general_dilated(
        x, w[:, None, :].astype(x.dtype), window_strides=(1,),
        padding=[(CONV_WIDTH - 1, 0)],
        dimension_numbers=("NWC", "WIO", "NWC"), feature_group_count=c)
    return y + b.astype(x.dtype)

def rg_lru(x, w_a, b_a, w_x, b_x, lam):
    bsz, t, _ = x.shape
    xb = x.reshape(bsz, t, LRU_BLOCKS, LRU_BLOCK)
    gate_r = jnp.einsum("btnc,ncd->btnd", xb, w_a).reshape(bsz, t, LRU_WIDTH) + b_a
    gate_i = jnp.einsum("btnc,ncd->btnd", xb, w_x).reshape(bsz, t, LRU_WIDTH) + b_x
    r = jax.nn.sigmoid(gate_r.astype(jnp.float32))
    i = jax.nn.sigmoid(gate_i.astype(jnp.float32))
    log_a = -LRU_C * r * jax.nn.softplus(-lam.astype(jnp.float32))
    a = jnp.exp(log_a)
    mult = jnp.sqrt(-jnp.expm1(2.0 * log_a))
    u = mult * (i * x.astype(jnp.float32))

    def combine(left, right):
        a_l, b_l = left
        a_r, b_r = right
        return a_l * a_r, a_r * b_l + b_r

    _, h = lax.associative_scan(combine, (a, u), axis=1)
    return h

def sliding_window_attention_with_sinks(q, k, v, sinks):
    bsz, t, _, _ = q.shape
    pad_cfg = ((0, 0), (PAD, 0), (0, 0), (0, 0))
    qp, kp, vp = jnp.pad(q, pad_cfg), jnp.pad(k, pad_cfg), jnp.pad(v, pad_cfg)
    tp = t + PAD
    nb = tp // BLOCK
    qb = qp.reshape(bsz, nb, BLOCK, KV_HEADS, GQA_GROUP, HEAD_DIM)
    kb = kp.reshape(bsz, nb, BLOCK, KV_HEADS, HEAD_DIM)
    vb = vp.reshape(bsz, nb, BLOCK, KV_HEADS, HEAD_DIM)
    blk_pad = ((0, 0), (1, 0), (0, 0), (0, 0), (0, 0))
    kk = jnp.concatenate([jnp.pad(kb, blk_pad)[:, :-1], kb], axis=2)
    vv = jnp.concatenate([jnp.pad(vb, blk_pad)[:, :-1], vb], axis=2)
    scale = HEAD_DIM ** -0.5
    s = jnp.einsum("bnqkgd,bnskd->bnkgqs", qb, kk,
                   preferred_element_type=jnp.float32) * scale
    blk = jnp.arange(nb)[:, None] * BLOCK
    qpos = blk + jnp.arange(BLOCK)[None, :]
    kpos = blk - BLOCK + jnp.arange(2 * BLOCK)[None, :]
    diff = qpos[:, :, None] - kpos[:, None, :]
    valid = (diff >= 0) & (diff < WINDOW) & (kpos[:, None, :] >= PAD)
    s = jnp.where(valid[None, :, None, None], s, NEG)
    sink = sinks.astype(jnp.float32).reshape(1, 1, KV_HEADS, GQA_GROUP, 1, 1)
    m = jnp.maximum(jnp.max(s, axis=-1, keepdims=True), sink)
    p = jnp.exp(s - m)
    denom = jnp.sum(p, axis=-1, keepdims=True) + jnp.exp(sink - m)
    o = jnp.einsum("bnkgqs,bnskd->bnqkgd", (p / denom).astype(v.dtype), vv)
    return o.reshape(bsz, tp, ATTN_WIDTH)[:, PAD:]

def first_inputs(seed: int = 0) -> dict:
    key = jax.random.key(seed)
    ks = jax.random.split(key, 20)
    f32 = jnp.float32

    def nrm(k, shape, scale):
        return jax.random.normal(k, shape, f32) * scale

    u = jax.random.uniform(ks[10], (DEPTH, LRU_WIDTH), f32, 0.9, 0.999)
    a0 = u ** (1.0 / LRU_C)
    lru_lambda = jnp.log(a0) - jnp.log1p(-a0)
    return {
        "x": nrm(ks[0], (BATCH, SEQ, D_MODEL), 1.0),
        "meta_tokens": nrm(ks[1], (N_META, D_MODEL), 1.0),
        "g_pre_mix": 1.0 + nrm(ks[2], (DEPTH, D_MODEL), 0.05),
        "w_in": nrm(ks[3], (DEPTH, D_MODEL, IN_WIDTH), D_MODEL ** -0.5),
        "conv_w": nrm(ks[4], (DEPTH, CONV_WIDTH, LRU_WIDTH), CONV_WIDTH ** -0.5),
        "conv_b": nrm(ks[5], (DEPTH, LRU_WIDTH), 0.01),
        "w_a": nrm(ks[6], (DEPTH, LRU_BLOCKS, LRU_BLOCK, LRU_BLOCK), LRU_BLOCK ** -0.5),
        "b_a": nrm(ks[7], (DEPTH, LRU_WIDTH), 0.01),
        "w_x": nrm(ks[8], (DEPTH, LRU_BLOCKS, LRU_BLOCK, LRU_BLOCK), LRU_BLOCK ** -0.5),
        "b_x": nrm(ks[9], (DEPTH, LRU_WIDTH), 0.01),
        "lru_lambda": lru_lambda,
        "attn_sinks": nrm(ks[11], (DEPTH, ATTN_HEADS), 0.5),
        "w_out": nrm(ks[12], (DEPTH, MIX_WIDTH, D_MODEL), MIX_WIDTH ** -0.5),
        "g_post_mix": 1.0 + nrm(ks[13], (DEPTH, D_MODEL), 0.05),
        "g_pre_ffn": 1.0 + nrm(ks[14], (DEPTH, D_MODEL), 0.05),
        "w_ff1": nrm(ks[15], (DEPTH, D_MODEL, D_FF), D_MODEL ** -0.5),
        "w_ff2": nrm(ks[16], (DEPTH, D_FF, D_MODEL), D_FF ** -0.5),
        "g_post_ffn": 1.0 + nrm(ks[17], (DEPTH, D_MODEL), 0.05),
    }

def first_block(x, meta_tokens, g_pre_mix, w_in, conv_w, conv_b, w_a, b_a, w_x, b_x,
              lru_lambda, attn_sinks, w_out, g_post_mix, g_pre_ffn, w_ff1, w_ff2,
              g_post_ffn):
    bsz = x.shape[0]
    meta = jnp.broadcast_to(meta_tokens[None].astype(x.dtype), (bsz, N_META, D_MODEL))
    h = jnp.concatenate([meta, x], axis=1)
    t = h.shape[1]
    split_at = [ATTN_WIDTH, ATTN_WIDTH + KV_WIDTH, ATTN_WIDTH + 2 * KV_WIDTH,
                ATTN_WIDTH + 2 * KV_WIDTH + LRU_WIDTH]
    for l in range(DEPTH):
        u = rmsnorm(h, g_pre_mix[l])
        z = u @ w_in[l]
        q, k, v, xr, yr = jnp.split(z, split_at, axis=-1)
        attn = sliding_window_attention_with_sinks(
            q.reshape(bsz, t, ATTN_HEADS, HEAD_DIM),
            k.reshape(bsz, t, KV_HEADS, HEAD_DIM),
            v.reshape(bsz, t, KV_HEADS, HEAD_DIM),
            attn_sinks[l])
        xr = causal_depthwise_conv(xr, conv_w[l], conv_b[l])
        hr = rg_lru(xr, w_a[l], b_a[l], w_x[l], b_x[l], lru_lambda[l])
        rec = (jax.nn.gelu(yr.astype(jnp.float32)) * hr).astype(h.dtype)
        mix = jnp.concatenate([attn.astype(h.dtype), rec], axis=-1) @ w_out[l]
        h = h + rmsnorm(mix, g_post_mix[l])
        u = rmsnorm(h, g_pre_ffn[l])
        f = jnp.square(jax.nn.relu(u @ w_ff1[l])) @ w_ff2[l]
        h = h + rmsnorm(f, g_post_ffn[l])
    return h[:, N_META:]


HEAD_DIM_2 = 128
N_HEADS_MOBA = 8
N_HEADS_GDN = 8
MOBA_WIDTH = N_HEADS_MOBA * HEAD_DIM_2
GDN_WIDTH = N_HEADS_GDN * HEAD_DIM_2
MOBA_BLOCK = 256
MOBA_TOPK = 3
MOBA_Q_CHUNK = 32
GDN_CHUNK = 64
ROPE_THETA = 10000.0
D_FF_2 = -(-8 * D_MODEL // (3 * 256)) * 256
PLE_DIM = 256

IN_SIZES = (MOBA_WIDTH, MOBA_WIDTH, MOBA_WIDTH, 3 * GDN_WIDTH, GDN_WIDTH,
            N_HEADS_GDN, N_HEADS_GDN, D_MODEL, D_MODEL)
IN_SPLITS = tuple(int(s) for s in np.cumsum(IN_SIZES)[:-1])
IN_WIDTH_2 = int(sum(IN_SIZES))


def rms_norm(x, w):
    xf = x.astype(jnp.float32)
    y = xf * lax.rsqrt(jnp.mean(xf * xf, axis=-1, keepdims=True) + EPS)
    return (y * w.astype(jnp.float32)).astype(x.dtype)

def l2_norm(x):
    xf = x.astype(jnp.float32)
    return xf * lax.rsqrt(jnp.sum(xf * xf, axis=-1, keepdims=True) + EPS)

def rope_tables(seq):
    inv = 1.0 / (ROPE_THETA ** (jnp.arange(0, HEAD_DIM_2, 2, dtype=jnp.float32) / HEAD_DIM_2))
    ang = jnp.arange(seq, dtype=jnp.float32)[:, None] * inv[None, :]
    return jnp.cos(ang), jnp.sin(ang)

def apply_rope(x, cos, sin):
    x1, x2 = jnp.split(x.astype(jnp.float32), 2, axis=-1)
    out = jnp.concatenate([x1 * cos - x2 * sin, x2 * cos + x1 * sin], axis=-1)
    return out.astype(x.dtype)

def causal_depthwise_conv_2(x, w):
    c = x.shape[-1]
    return lax.conv_general_dilated(
        x, w[:, None, :].astype(x.dtype), window_strides=(1,),
        padding=[(CONV_WIDTH - 1, 0)], dimension_numbers=("NWC", "WIO", "NWC"),
        feature_group_count=c)

def moba_attention(q, k, v):
    b, h, s, hd = q.shape
    nb = -(-s // MOBA_BLOCK)
    pad = nb * MOBA_BLOCK - s
    n_sel = min(MOBA_TOPK, nb)
    scale = hd ** -0.5
    k_blocks = jnp.pad(k, ((0, 0), (0, 0), (0, pad), (0, 0))).reshape(b, h, nb, MOBA_BLOCK, hd)
    v_blocks = jnp.pad(v, ((0, 0), (0, 0), (0, pad), (0, 0))).reshape(b, h, nb, MOBA_BLOCK, hd)
    k_mean = jnp.mean(k_blocks.astype(jnp.float32), axis=3)
    blk_ids = jnp.arange(nb)
    n_chunks = s // MOBA_Q_CHUNK

    def one_chunk(c):
        start = c * MOBA_Q_CHUNK
        q_c = lax.dynamic_slice_in_dim(q, start, MOBA_Q_CHUNK, axis=2)
        q_blk = start // MOBA_BLOCK
        gate = jnp.einsum("bhcd,bhnd->bhcn", q_c.astype(jnp.float32), k_mean)
        gate = jnp.where(blk_ids < q_blk, gate, -jnp.inf)
        _, sel = lax.top_k(gate, n_sel)
        sel_valid = sel < q_blk
        idx = sel.reshape(b, h, MOBA_Q_CHUNK * n_sel, 1, 1)
        k_sel = jnp.take_along_axis(k_blocks, idx, axis=2).reshape(
            b, h, MOBA_Q_CHUNK, n_sel, MOBA_BLOCK, hd)
        v_sel = jnp.take_along_axis(v_blocks, idx, axis=2).reshape(
            b, h, MOBA_Q_CHUNK, n_sel, MOBA_BLOCK, hd)
        s_past = jnp.einsum("bhcd,bhcknd->bhckn", q_c, k_sel).astype(jnp.float32) * scale
        s_past = jnp.where(sel_valid[..., None], s_past, -jnp.inf)
        s_past = s_past.reshape(b, h, MOBA_Q_CHUNK, n_sel * MOBA_BLOCK)
        k_own = lax.dynamic_index_in_dim(k_blocks, q_blk, axis=2, keepdims=False)
        v_own = lax.dynamic_index_in_dim(v_blocks, q_blk, axis=2, keepdims=False)
        s_own = jnp.einsum("bhcd,bhnd->bhcn", q_c, k_own).astype(jnp.float32) * scale
        q_pos = start + jnp.arange(MOBA_Q_CHUNK)
        k_pos = q_blk * MOBA_BLOCK + jnp.arange(MOBA_BLOCK)
        s_own = jnp.where(k_pos[None, :] <= q_pos[:, None], s_own, -jnp.inf)
        probs = jax.nn.softmax(jnp.concatenate([s_past, s_own], axis=-1), axis=-1)
        p_past = probs[..., : n_sel * MOBA_BLOCK].reshape(
            b, h, MOBA_Q_CHUNK, n_sel, MOBA_BLOCK).astype(v.dtype)
        p_own = probs[..., n_sel * MOBA_BLOCK:].astype(v.dtype)
        return (jnp.einsum("bhckn,bhcknd->bhcd", p_past, v_sel)
                + jnp.einsum("bhcn,bhnd->bhcd", p_own, v_own))

    out = lax.map(one_chunk, jnp.arange(n_chunks))
    return out.transpose(1, 2, 0, 3, 4).reshape(b, h, s, hd)

def gated_delta_rule(q, k, v, g, beta):
    b, h, s, dk = q.shape
    dv = v.shape[-1]
    L = GDN_CHUNK
    nc = s // L
    f32 = jnp.float32
    q = q.astype(f32) * (dk ** -0.5)
    k = k.astype(f32)
    v = v.astype(f32)
    q = q.reshape(b, h, nc, L, dk)
    k = k.reshape(b, h, nc, L, dk)
    v = v.reshape(b, h, nc, L, dv)
    g = g.astype(f32).reshape(b, h, nc, L)
    beta = beta.astype(f32).reshape(b, h, nc, L)
    gc = jnp.cumsum(g, axis=-1)
    causal = jnp.tril(jnp.ones((L, L), dtype=bool))
    strict = jnp.tril(jnp.ones((L, L), dtype=bool), k=-1)
    decay = jnp.exp(jnp.where(causal, gc[..., :, None] - gc[..., None, :], -jnp.inf))
    k_beta = k * beta[..., None]
    a_low = jnp.where(strict, jnp.einsum("bhnid,bhnjd->bhnij", k_beta, k) * decay, 0.0)
    t_mat = a_low + jnp.eye(L, dtype=f32)
    rhs = jnp.concatenate([v * beta[..., None], k_beta * jnp.exp(gc)[..., None]], axis=-1)
    sol = lax.linalg.triangular_solve(t_mat, rhs, left_side=True, lower=True, unit_diagonal=True)
    u = sol[..., :dv]
    w = sol[..., dv:]
    attn = jnp.where(causal, jnp.einsum("bhnid,bhnjd->bhnij", q, k) * decay, 0.0)

    def step(state, inp):
        q_i, k_i, u_i, w_i, g_i, a_i = inp
        v_new = u_i - jnp.einsum("bhld,bhde->bhle", w_i, state)
        o = (jnp.einsum("bhld,bhde->bhle", q_i * jnp.exp(g_i)[..., None], state)
             + jnp.einsum("bhlm,bhme->bhle", a_i, v_new))
        g_last = g_i[..., -1]
        state = (state * jnp.exp(g_last)[..., None, None]
                 + jnp.einsum("bhld,bhle->bhde", k_i * jnp.exp(g_last[..., None] - g_i)[..., None], v_new))
        return state, o

    xs = tuple(jnp.moveaxis(t, 2, 0) for t in (q, k, u, w, gc, attn))
    state0 = jnp.zeros((b, h, dk, dv), dtype=f32)
    _, o = lax.scan(step, state0, xs)
    return jnp.moveaxis(o, 0, 2).reshape(b, h, s, dv)

def second_inputs(seed: int = 0) -> dict:
    key = jax.random.key(seed)
    ks = jax.random.split(key, 24)
    f32 = jnp.float32

    def nrm(k, shape, scale):
        return jax.random.normal(k, shape, f32) * scale

    def gain(k, n):
        return 1.0 + 0.1 * jax.random.normal(k, (DEPTH, n), f32)

    dt = jnp.exp(jax.random.uniform(ks[7], (DEPTH, N_HEADS_GDN), f32,
                                    math.log(1e-3), math.log(1e-1)))
    return {
        "x": nrm(ks[0], (BATCH, SEQ, D_MODEL), 1.0),
        "p": nrm(ks[1], (DEPTH, BATCH, SEQ, PLE_DIM), 1.0),
        "ln_pre_mix": gain(ks[2], D_MODEL),
        "w_in": nrm(ks[3], (DEPTH, D_MODEL, IN_WIDTH_2), D_MODEL ** -0.5),
        "conv_w": nrm(ks[4], (DEPTH, CONV_WIDTH, 3 * GDN_WIDTH), CONV_WIDTH ** -0.5),
        "a_log": jnp.log(jax.random.uniform(ks[5], (DEPTH, N_HEADS_GDN), f32, 1.0, 16.0)),
        "dt_bias": jnp.log(jnp.expm1(dt)),
        "gdn_norm": gain(ks[6], HEAD_DIM_2),
        "w_proj_a": nrm(ks[8], (DEPTH, MOBA_WIDTH, D_MODEL), MOBA_WIDTH ** -0.5),
        "w_proj_b": nrm(ks[9], (DEPTH, GDN_WIDTH, D_MODEL), GDN_WIDTH ** -0.5),
        "w_out": nrm(ks[10], (DEPTH, D_MODEL, D_MODEL), D_MODEL ** -0.5),
        "ln_post_mix": gain(ks[11], D_MODEL),
        "ln_pre_ffn": gain(ks[12], D_MODEL),
        "w_ffn_gate": nrm(ks[13], (DEPTH, D_MODEL, D_FF_2), D_MODEL ** -0.5),
        "w_ffn_up": nrm(ks[14], (DEPTH, D_MODEL, D_FF_2), D_MODEL ** -0.5),
        "w_ffn_down": nrm(ks[15], (DEPTH, D_FF_2, D_MODEL), D_FF_2 ** -0.5),
        "ln_post_ffn": gain(ks[16], D_MODEL),
        "w_ple": nrm(ks[17], (DEPTH, PLE_DIM, D_MODEL), PLE_DIM ** -0.5),
        "ln_ple": gain(ks[18], D_MODEL),
        "w_ple_gate": nrm(ks[19], (DEPTH, D_MODEL, D_MODEL), D_MODEL ** -0.5),
    }

def second_block(x, p, ln_pre_mix, w_in, conv_w, a_log, dt_bias, gdn_norm, w_proj_a, w_proj_b,
              w_out, ln_post_mix, ln_pre_ffn, w_ffn_gate, w_ffn_up, w_ffn_down, ln_post_ffn,
              w_ple, ln_ple, w_ple_gate):
    b, s, _ = x.shape
    cos, sin = rope_tables(s)

    def to_heads(t, n):
        return t.reshape(b, s, n, HEAD_DIM_2).transpose(0, 2, 1, 3)

    def from_heads(t):
        return t.transpose(0, 2, 1, 3).reshape(b, s, -1)

    h = x
    for i in range(DEPTH):
        u = rms_norm(h, ln_pre_mix[i])
        proj = u @ w_in[i]
        q_a, k_a, v_a, qkv_b, z_b, b_b, a_b, gate_a, gate_b = jnp.split(proj, IN_SPLITS, axis=-1)

        qa = apply_rope(to_heads(q_a, N_HEADS_MOBA), cos, sin)
        ka = apply_rope(to_heads(k_a, N_HEADS_MOBA), cos, sin)
        va = to_heads(v_a, N_HEADS_MOBA)
        y_a = from_heads(moba_attention(qa, ka, va))

        qkv_b = jax.nn.silu(causal_depthwise_conv_2(qkv_b, conv_w[i]))
        q_b, k_b, v_b = jnp.split(qkv_b, 3, axis=-1)
        qb = l2_norm(to_heads(q_b, N_HEADS_GDN))
        kb = l2_norm(to_heads(k_b, N_HEADS_GDN))
        vb = to_heads(v_b, N_HEADS_GDN)
        g_log = -jnp.exp(a_log[i].astype(jnp.float32)) * jax.nn.softplus(
            a_b.astype(jnp.float32) + dt_bias[i].astype(jnp.float32))
        beta = jax.nn.sigmoid(b_b.astype(jnp.float32))
        o_b = gated_delta_rule(qb, kb, vb, g_log.transpose(0, 2, 1), beta.transpose(0, 2, 1))
        o_b = o_b.transpose(0, 2, 1, 3).astype(h.dtype)
        z = z_b.reshape(b, s, N_HEADS_GDN, HEAD_DIM_2)
        y_b = (rms_norm(o_b, gdn_norm[i]) * jax.nn.silu(z)).reshape(b, s, GDN_WIDTH)

        merged = (jax.nn.sigmoid(gate_a) * (y_a @ w_proj_a[i])
                  + jax.nn.sigmoid(gate_b) * (y_b @ w_proj_b[i]))
        h = h + rms_norm(merged @ w_out[i], ln_post_mix[i])

        f = rms_norm(h, ln_pre_ffn[i])
        f = (jax.nn.silu(f @ w_ffn_gate[i]) * (f @ w_ffn_up[i])) @ w_ffn_down[i]
        h = h + rms_norm(f, ln_post_ffn[i])

        e = rms_norm(p[i].astype(h.dtype) @ w_ple[i], ln_ple[i])
        h = h + jax.nn.sigmoid(h @ w_ple_gate[i]) * e
    return h


def setup_inputs(seed=0):
    out = dict(first_inputs(seed))
    for name, value in second_inputs(seed + 1).items():
        if name != "x":
            out[name + "_2"] = value
    return out


def reference(
    x, meta_tokens, g_pre_mix, w_in, conv_w, conv_b, w_a, b_a, w_x, b_x, lru_lambda, attn_sinks,
    w_out, g_post_mix, g_pre_ffn, w_ff1, w_ff2, g_post_ffn, p_2, ln_pre_mix_2, w_in_2, conv_w_2,
    a_log_2, dt_bias_2, gdn_norm_2, w_proj_a_2, w_proj_b_2, w_out_2, ln_post_mix_2,
    ln_pre_ffn_2, w_ffn_gate_2, w_ffn_up_2, w_ffn_down_2, ln_post_ffn_2, w_ple_2, ln_ple_2,
    w_ple_gate_2,
):
    x = first_block(
        x, meta_tokens, g_pre_mix, w_in, conv_w, conv_b, w_a, b_a, w_x, b_x, lru_lambda,
        attn_sinks, w_out, g_post_mix, g_pre_ffn, w_ff1, w_ff2, g_post_ffn,
    )
    return second_block(
        x, p_2, ln_pre_mix_2, w_in_2, conv_w_2, a_log_2, dt_bias_2, gdn_norm_2, w_proj_a_2,
        w_proj_b_2, w_out_2, ln_post_mix_2, ln_pre_ffn_2, w_ffn_gate_2, w_ffn_up_2,
        w_ffn_down_2, ln_post_ffn_2, w_ple_2, ln_ple_2, w_ple_gate_2,
    )


_drawn_inputs = setup_inputs


def setup_inputs(seed=0):
    import zlib

    import numpy as np

    out = dict(_drawn_inputs(seed))
    spreads = {}
    factors = {'b_a': 30.738, 'b_x': 8.0, 'attn_sinks': 8.0}
    for name, (base, spread) in spreads.items():
        noise = np.random.default_rng([zlib.crc32(name.encode()), seed]).standard_normal(out[name].shape)
        drawn = base * np.exp(spread * noise) if base else spread * noise
        out[name] = __import__('jax').numpy.asarray(drawn.astype(out[name].dtype))
    for name, factor in factors.items():
        out[name] = (out[name] * factor).astype(out[name].dtype)
    return out
```

```python
from contextlib import ExitStack

import numpy as np

import concourse.bass as bass
from concourse import mybir

F32 = mybir.dt.float32
F32R = mybir.dt.float32r
ALU = mybir.AluOpType
ACT = mybir.ActivationFunctionType
AX = mybir.AxisListType.X

P = 128
D = 1024
KC = D // P
S = 256
META = 16
T1 = S + META
NT = S // P
EPS = 1e-6
NEG = -1e30
QH, KVH, HD1 = 8, 2, 64
WINDOW = 128
LRU = 512
LT = LRU // P
FF1_TILES = 16
HEADS2 = 8
PAIRS = HEADS2 // 2
LEVELS = 7
FF2_TILES = 11
PLE = 256
REGION = 16128
SC1 = HD1 ** -0.5
SC2 = P ** -0.5
IN2_Q, IN2_K, IN2_V, IN2_CONV, IN2_Z, IN2_B, IN2_GA, IN2_GB = (
    0, 1024, 2048, 3072, 6144, 7168, 7184, 8208)

C_IDENT, C_TRI, C_MUP, C_MLOW, C_LEV, C_MOBA, C_WIN0, C_WIN1, C_COS, C_SIN, C_END = (
    0, 128, 256, 384, 512, 1408, 1792, 1936, 2192, 2448, 2704)


def constant_table():
    c = np.zeros((P, C_END), np.float32)
    r, k = np.arange(P)[:, None], np.arange(P)[None, :]
    c[:, C_IDENT:C_TRI] = r == k
    c[:, C_TRI:C_MUP] = r <= k
    c[:, C_MUP:C_MLOW] = np.where(r <= k, 0.0, NEG)
    c[:, C_MLOW:C_LEV] = np.where(k < r, 0.0, NEG)
    for n in range(LEVELS):
        b = 1 << n
        c[:, C_LEV + n * P:C_LEV + (n + 1) * P] = (r // (2 * b) == k // (2 * b)) & (r % (2 * b) >= b) & (k % (2 * b) < b)
    diag = np.where(k <= r, 0.0, NEG)
    c[:, C_MOBA + P:C_MOBA + 2 * P] = diag
    c[:, C_MOBA + 2 * P:C_MOBA + 3 * P] = diag
    k0 = np.arange(P + META)[None, :]
    gap = META + r - k0
    c[:, C_WIN0:C_WIN1] = np.where((gap >= 0) & (gap < WINDOW), 0.0, NEG)
    gap = P + r - np.arange(2 * P)[None, :]
    c[:, C_WIN1:C_COS] = np.where((gap >= 0) & (gap < WINDOW), 0.0, NEG)
    half = P // 2
    inv = (1.0 / (np.float32(10000.0) ** (np.arange(0, P, 2, dtype=np.float32) / np.float32(P)))).astype(np.float32)
    ang = (np.arange(S, dtype=np.float32)[None, :] * inv[:, None]).astype(np.float32)
    c[:half, C_COS:C_SIN] = c[half:, C_COS:C_SIN] = np.cos(ang)
    c[:half, C_SIN:C_END] = -np.sin(ang)
    c[half:, C_SIN:C_END] = np.sin(ang)
    return c


RING = 4
UNITS = 4
(P_KV, P_XR, P_YR0, P_Q, P_YR1, P_OUT1, P_FF1, P_MOBA, P_GDN, P_GATEB, P_PROJA, P_PROJB, P_OUT2, P_FF2, P_PLE,
 P_PGATE, P_ALL) = (0, 1, 3, 4, 6, 7, 11, 43, 59, 75, 79, 83, 87, 91, 124, 125, 129)


def panel_plan():
    plan = [("cols", "kv")] + [("cols", "fm")] * 6 + [("rows", "acc")] * 4
    plan += [("cols", "fm")] + [("cols", "fm"), ("rows", "acc")] * 15 + [("rows", "acc")]
    plan += ([("cols", "fm")] * 3 + [("rows", "tok")]) * PAIRS
    plan += ([("cols", "fm")] * 3 + [("rows", "tok")]) * PAIRS
    plan += [("cols", "fm")] * 12 + [("rows", "acc")] * 4
    plan += [("cols", "fm")] * 2 + [("cols", "fm"), ("rows", "acc"), ("cols", "fm")] * 10 + [("rows", "acc")]
    plan += [("rows", "acc")] * 5
    assert len(plan) == P_ALL
    return plan


PLAN = panel_plan()
SLOT = [p % RING if p < P_FF2 else (p - P_FF2) % 3 if p < P_PLE else (p - P_PLE) % RING for p in range(P_ALL)]
LOADS = [16 * sum(SLOT[q] == SLOT[p] for q in range(p + 1)) for p in range(P_ALL)]
REUSE = [max((q for q in range(p) if SLOT[q] == SLOT[p]), default=-1) for p in range(P_ALL)]


def bank_counts():
    n, before = [0, 0], []
    for layout, to in PLAN:
        for j in range(2):
            before.append(tuple(n))
            if to == "fm":
                n[j] += 1
            elif to == "kv" and j == 0:
                n[0] += 1
            elif to == "tok" and j == 1:
                n[0] += 1
                n[1] += 1
    return before


EMPTIED = bank_counts()
EMPTIED0 = [e[0] for e in EMPTIED] + [0] * 64
EMPTIED1 = [e[1] for e in EMPTIED] + [0] * 64


def along(table, at, stride, i):
    if isinstance(i, int):
        return table[at + stride * i]
    step = table[at + stride] - table[at]
    return i * step + table[at]


class Chain:

    def __init__(self, eng, sem):
        self.eng, self.sem, self.n = eng, sem, 0

    def mark(self, ins):
        ins.then_inc(self.sem, 1)
        self.n = self.n + 1

    def wait(self):
        self.eng.wait_ge(self.sem, self.n)

    def link(self, ins):
        self.mark(ins)
        self.wait()


def rounds(eng, n, chain=None, per=0):
    base = chain.n if chain else 0
    with eng.Fori(0, n) as i:
        if chain:
            chain.n = i * per + base
        yield i
    if chain:
        chain.n = base + n * per


MOBA_WEAVE = [16, 8, 16, 8, 16]
GDN_WEAVE = [12, 8, 4, 4, 2] + [2] * 12 + [2, 3, 2, 2, 1]
assert sum(MOBA_WEAVE) == 64 and sum(GDN_WEAVE) == 64


def finished(weave):
    done, out = 0, []
    for n in weave:
        out.append(range(done // 8, (done + n) // 8))
        done += n
    return out


def build(nc, A):
    ctx = ExitStack()
    with ctx:
        def sb(name, shape, dt=F32):
            return ctx.enter_context(nc.sbuf_tensor(name, shape, dt))

        def sem(name):
            return ctx.enter_context(nc.semaphore(name))

        acc = ctx.enter_context(nc.psum_tensor("acc", [P, 4, 512], F32))
        fm = ctx.enter_context(nc.psum_tensor("fm", [P, 2, 512], F32))
        ma = ctx.enter_context(nc.psum_tensor("ma", [P, 512], F32))
        mb = ctx.enter_context(nc.psum_tensor("mb", [P, 512], F32))

        w_raw = sb("w_raw", [P, RING, 2048])
        wh = sb("wh", [P, UNITS, 1024], F32R)
        wl = sb("wl", [P, UNITS, 1024], F32R)
        h = sb("h", [P, NT, D])
        xTh = sb("xTh", [P, KC, T1], F32R)
        xTl = sb("xTl", [P, KC, T1], F32R)
        yTh = sb("yTh", [P, KC, S], F32R)
        yTl = sb("yTl", [P, KC, S], F32R)
        y2 = sb("y2", [P, 2 * KC * S], F32R)
        gain = sb("gain", [P, 2, D])
        cst = sb("cst", [P, C_END])
        ones = sb("ones", [P, P])
        zero_r = sb("zero_r", [P, P])
        eps = sb("eps", [P, 1])
        st = sb("st", [P, 32])
        R = sb("R", [P, REGION])

        def carve(state, *shape):
            n = int(np.prod(shape))
            a = R[:, state[0]:state[0] + n]
            state[0] += n
            assert state[0] <= REGION, state
            if len(shape) == 2:
                return a.rearrange("p (a b) -> p a b", a=shape[0])
            if len(shape) == 3:
                return a.rearrange("p (a b c) -> p a b c", a=shape[0], b=shape[1])
            return a

        c1 = [0]
        u = carve(c1, NT, D)
        meta = carve(c1, D)
        xr_pad = carve(c1, LT, T1 + 3)
        xc = carve(c1, LT, T1)
        r_g = carve(c1, LT, T1)
        i_g = carve(c1, LT, T1)
        th_ = carve(c1, LT, T1)
        a_ = carve(c1, LT, T1)
        a2 = carve(c1, LT, T1)
        gy = carve(c1, LT, S)
        qT1 = carve(c1, 4, S)
        kT1 = carve(c1, KVH, T1)
        v1 = carve(c1, 3, P)
        o1 = carve(c1, QH * HD1)
        wa_bd = carve(c1, LT, P)
        wx_bd = carve(c1, LT, P)
        cwb = carve(c1, LT, 8)
        lam_t = carve(c1, 8, LT)
        sink = carve(c1, QH)
        cp = [NT * D + D]
        p1 = carve(cp, QH, S)
        pT1 = carve(cp, QH, 2, P)
        sm1 = carve(cp, QH, S)
        cf = [NT * D + D]
        hid_t = carve(cf, 2, S)
        hid_q = carve(cf, 2, S)
        hid_h = y2[:, 0:4 * S].rearrange("p (a b c) -> p a b c", a=2, b=2)
        hid_l = y2[:, 4 * S:8 * S].rearrange("p (a b c) -> p a b c", a=2, b=2)
        c2 = [NT * D]
        ybh = y2[:, 0:KC * S].rearrange("p (k n) -> p k n", k=KC)
        ybl = y2[:, KC * S:2 * KC * S].rearrange("p (k n) -> p k n", k=KC)
        ga = carve(c2, KC, S)
        g_all = carve(c2, 7, 2, HEADS2)
        cw_all = carve(c2, 4, 24)
        ab_w = carve(c2, KC, 16)
        ab_h = y2[:, 0:KC * 16].rearrange("p (k n) -> p k n", k=KC)
        ab_l = y2[:, KC * 16:2 * KC * 16].rearrange("p (k n) -> p k n", k=KC)
        ab = carve(c2, 2, 16)
        dt_row = carve(c2, 2, HEADS2)
        tmp16 = carve(c2, 8, 16)
        gnorm = carve(c2, P)
        sc = carve(c2, 6, 2, 2)
        cw = carve(c2, 4, 6)
        raw = carve(c2, 6, S + 3)
        zr = carve(c2, NT, S)
        c3 = [c2[0]]
        qk = carve(c3, 4, S)
        qr = carve(c3, 4, S)
        rot = carve(c3, 4, S)
        va = carve(c3, NT, S)
        sm2 = carve(c3, 2, 384)
        p2 = carve(c3, 2, 384)
        pT2 = carve(c3, 2, 384)
        c4 = [c2[0]]
        cv = carve(c4, 6, S)
        c5 = [0]
        rk = carve(c5, 4 * S)
        sq = rk
        kbe = carve(c5, 2, P)
        kdec = carve(c5, 2, P)
        vb = carve(c5, 4, P)
        dt_ = carve(c4, 4, P)
        dl_ = carve(c4, 4, P)
        eg = carve(c4, 2, P)
        attnT = carve(c4, 4, P)
        A_ = carve(c4, 4, P)
        gb = carve(c4, 4, P)
        C_ = carve(c4, 2, 512)
        X_, XT_ = dl_, dt_
        P_ = carve(c4, 4, P)
        u0 = carve(c4, 2, P)
        nwT = carve(c4, 2, P)
        S1 = carve(c4, 2, P)
        vn = carve(c4, 2, P)
        qeg = carve(c4, 2, P)
        y_ = gb
        sz = carve(c4, NT, S)
        c6 = [c2[0]]
        gate_s = carve(c6, 2, S)
        hid2 = carve(c6, 2, S)
        hid2_h = y2[:, 0:2 * S].rearrange("p (j n) -> p j n", j=2)
        hid2_l = y2[:, 2 * S:4 * S].rearrange("p (j n) -> p j n", j=2)
        gb_s = gain[:, :, :].rearrange("p a (m n) -> p (a m) n", n=S)
        p_in = carve(c6, NT, PLE)
        e_row = ga.rearrange("p a b -> p (a b)").rearrange("p (t n) -> p t n", t=NT)
        junk = sb("junk", [P, D])

        ident = cst[:, C_IDENT:C_TRI]
        tri = cst[:, C_TRI:C_MUP]

        w_loaded = [sem(f"w_loaded{n}") for n in range(RING)]
        w_hi, w_lo, unit_done = sem("w_hi"), sem("w_lo"), sem("unit_done")
        emptied = [sem("fm0_emptied"), sem("fm1_emptied")]
        x_loaded, cst_loaded, small1, small2 = (sem(n) for n in ("x_loaded", "cst_loaded", "small1_loaded", "small2_loaded"))
        small3 = sem("block_diag_loaded")
        gain_loaded = [sem("gain0_loaded"), sem("gain1_loaded")]
        gain_used = sem("gain_used")
        filled = sem("pool_filled")
        act_chain, dve_chain = sem("act_chain"), sem("dve_chain")
        stat = sem("norm_root_ready")
        u_ready = sem("u_ready")
        ut_ps = sem("uT_in_psum")
        ut_hi, ut_lo = sem("uT_hi_ready"), sem("uT_lo_ready")
        h_ready = sem("h_ready")
        v1_out = sem("v1_ready")
        lam_e, sp_ready, xc_ready = sem("lam_exp_ready"), sem("softplus_ready"), sem("conv_ready")
        r_ps, r_act, tanh_out, a_out, m2_out, mult_out = (
            sem(n) for n in ("lru_gates_in_psum", "lru_gates_ready", "lru_tanh_ready", "lru_a_ready",
                             "lru_mult2_ready", "lru_mult_ready"))
        rec_out, rec_hi, rec_lo = sem("rec_ready"), sem("rec_hi_ready"), sem("rec_lo_ready")
        s1_ps, s1_max, s1_exp, p1T_ps, p1T_out, o1_ps, o1_out, o1T_ps, o1T_hi, o1T_lo = (
            sem(n) for n in ("attn1_scores", "attn1_max", "attn1_exp", "attn1_pT", "attn1_pT_ready", "attn1_o",
                             "attn1_o_ready", "attn1_oT", "attn1_oT_hi", "attn1_oT_lo"))
        s1_sink = sem("attn1_sink_exp")
        hid_a, hid_s, hid_hi, hid_lo = (sem(n) for n in ("hid_relu", "hid_square", "hid_hi", "hid_lo"))
        ab_hi, ab_ps, ab_out, ab_act, g_ready, gc_ps, gc_act, gc_ready = (
            sem(n) for n in ("ab_w_hi", "ab_in_psum", "ab_ready", "ab_act", "g_ready", "gc_in_psum", "gc_exp", "gc_ready"))
        ab_lo = sem("ab_w_lo")
        rot_out, rope_out, s2_ps, s2_max, s2_exp, s2_p, p2T_ps, p2T_a, p2T_v, o2_ps, o2_hi, o2_lo = (
            sem(n) for n in ("rope_halves", "rope_ready", "moba_scores", "moba_max", "moba_exp", "moba_p", "moba_pT",
                             "moba_pT0_ready", "moba_pT1_ready", "moba_o", "moba_o_hi", "moba_o_lo"))
        cv_out, silu_out, sq_out, ssq_ps, rk_out, qkn_out, gb_out, gcb_ps, t12_out, dt_out, dl_out = (
            sem(n) for n in ("gdn_conv", "gdn_silu", "gdn_squares", "gdn_square_sums", "gdn_inv_norms", "gdn_qk_ready",
                             "gdn_g_rows", "gdn_gc_rows", "gdn_exponents", "gdn_decay_up", "gdn_decay_low"))
        vT_ps, kT_ps, qkg_ps, kv_out, pre_out, c0_ps, lv_c, lv_p, lv_pe, lv_z, lv_x = (
            sem(n) for n in ("gdn_v_rows", "gdn_k_rows", "gdn_qk_products", "gdn_kv_scaled", "gdn_matrices", "gdn_c0T",
                             "inv_c_ready", "inv_p_in_psum", "inv_p_ready", "inv_z_in_psum", "inv_x_ready"))
        c0_out = sem("gdn_c0_ready")
        vb_out = sem("gdn_vb_ready")
        uw_ps, u0_out, nw_out, so_ps, S1_out, vn_ps, vn_out, o_ps, og_out, y_out, yT_ps, yb_hi, yb_lo = (
            sem(n) for n in ("gdn_u_w", "gdn_u0", "gdn_nwT", "gdn_state_ps", "gdn_state", "gdn_vnew_ps", "gdn_vnew",
                             "gdn_o_ps", "gdn_o_root", "gdn_y", "gdn_yT_ps", "gdn_yT_hi", "gdn_yT_lo"))
        sig_a, sig_b, mg_out, mg_hi, mg_lo = (sem(n) for n in ("gate_a_sig", "gate_b_sig", "merged", "merged_hi", "merged_lo"))
        swi_a, swi_m, swi_hi, swi_lo = (sem(n) for n in ("ffn2_silu", "ffn2_hidden", "ffn2_hid_hi", "ffn2_hid_lo"))
        p_loaded, e_out = sem("ple_loaded"), sem("ple_rows_ready")
        fin_sig, fin_out, stored = sem("final_sigmoid"), sem("out_ready"), sem("out_stored")

        def raw_unit(slot, j, layout):
            if layout == "cols":
                return w_raw[:, slot, :].rearrange("p (k n) -> p k n", k=KC)[:, :, j * P:(j + 1) * P]
            return w_raw[:, slot, j * 1024:(j + 1) * 1024]

        def split_view(buf, ring, layout):
            if layout == "cols":
                return buf[:, ring, :].rearrange("p (k n) -> p k n", k=KC)
            return buf[:, ring, :]

        block = ctx.enter_context(nc.Block())

        @block.sync
        def _(sp):
            w_in, w_in2 = A["w_in"][0], A["w_in_2"][0]

            def cols(w, off, n, m):
                src = w[:, off:off + 256 * n].rearrange("(k p) (m n) -> m p k n", p=P, n=256)
                return src[bass.ds(m, 1)].rearrange("a p k n -> p (a k) n")

            def rows(w, m):
                src = w.rearrange("(m k p) n -> m p k n", k=2, p=P)
                return src[bass.ds(m, 1)].rearrange("a p k n -> p (a k) n")

            def tokcols(w, off, n, m):
                return cols(w, off, n, m)

            def load(p, src, stride=0, i=0):
                if isinstance(i, int):
                    last = REUSE[p + stride * i]
                    if last >= 0:
                        sp.wait_ge(w_lo, 2 * last + 2)
                else:
                    sp.wait_ge(w_lo, along([2 * q + 2 for q in REUSE], p, stride, i))
                k = 8 if src.shape[-1] == 256 else 2
                dst = w_raw[:, SLOT[p], :].rearrange("p (k n) -> p k n", k=k)
                sp.dma_start(dst, src).then_inc(w_loaded[SLOT[p]], 16)

            sp.dma_start(u[:, :, :], A["x"][0].rearrange("(t p) d -> p t d", p=P)).then_inc(x_loaded, 16)
            sp.dma_start(meta[0:META, :], A["meta_tokens"]).then_inc(x_loaded, 16)
            load(P_KV, cols(w_in, 512, 1, 0))
            for m in range(2):
                load(P_XR + m, cols(w_in, 768, 2, m))
            load(P_YR0, cols(w_in, 1280, 2, 0))
            for m in range(2):
                load(P_Q + m, cols(w_in, 0, 2, m))
            load(P_YR1, cols(w_in, 1280, 2, 1))
            for n, m in enumerate((2, 3, 0, 1)):
                load(P_OUT1 + n, rows(A["w_out"][0], m))
            w1, w2 = A["w_ff1"][0], A["w_ff2"][0]
            load(P_FF1, cols(w1, 0, 16, 0))
            for i in rounds(sp, 7):
                load(P_FF1 + 1, cols(w1, 0, 16, i * 2 + 1), 4, i)
                load(P_FF1 + 2, rows(w2, i * 2), 4, i)
                load(P_FF1 + 3, cols(w1, 0, 16, i * 2 + 2), 4, i)
                load(P_FF1 + 4, rows(w2, i * 2 + 1), 4, i)
            load(P_FF1 + 29, cols(w1, 0, 16, 15))
            load(P_FF1 + 30, rows(w2, 14))
            load(P_FF1 + 31, rows(w2, 15))
            for i in rounds(sp, PAIRS):
                for n, off in enumerate((IN2_Q, IN2_K, IN2_GA, IN2_V)):
                    load(P_MOBA + n, cols(w_in2, off, 4, i), 4, i)
            for i in rounds(sp, PAIRS):
                for n, off in enumerate((IN2_CONV, IN2_CONV + D, IN2_CONV + 2 * D, IN2_Z)):
                    load(P_GDN + n, cols(w_in2, off, 4, i), 4, i)
            for m in range(4):
                load(P_GATEB + m, cols(w_in2, IN2_GB, 4, m))
            for n, w in enumerate((A["w_proj_a_2"][0], A["w_proj_b_2"][0])):
                for m in range(4):
                    load(P_PROJA + 4 * n + m, cols(w, 0, 4, m))
            for m in range(4):
                load(P_OUT2 + m, rows(A["w_out_2"][0], m))
            wg, wu, wd = A["w_ffn_gate_2"][0], A["w_ffn_up_2"][0], A["w_ffn_down_2"][0]
            load(P_FF2, cols(wg, 0, 11, 0))
            load(P_FF2 + 1, cols(wu, 0, 11, 0))
            for i in rounds(sp, 5):
                for n in range(2):
                    load(P_FF2 + 2 + 3 * n, cols(wg, 0, 11, i * 2 + (n + 1)), 6, i)
                    load(P_FF2 + 3 + 3 * n, rows(wd, i * 2 + n), 6, i)
                    load(P_FF2 + 4 + 3 * n, cols(wu, 0, 11, i * 2 + (n + 1)), 6, i)
            load(P_FF2 + 32, rows(wd, 10))
            load(P_PLE, rows(A["w_ple_2"][0], 0))
            for m in range(4):
                load(P_PGATE + m, rows(A["w_ple_gate_2"][0], m))
            for t in range(NT):
                sp.wait_ge(fin_out, t + 1)
                sp.dma_start(A["out"][0].rearrange("(t p) d -> t p d", p=P)[t], u[:, t, :]).then_inc(stored, 16)
            sp.wait_ge(stored, 16 * NT)

        GAINS = ["g_pre_mix", "g_post_mix", "g_pre_ffn", "g_post_ffn", "ln_pre_mix_2", "ln_post_mix_2",
                 "ln_pre_ffn_2", "ln_post_ffn_2", "ln_ple_2"]

        @block.gpsimd
        def _(pool):
            pool.memset(eps[:, :], EPS).then_inc(filled, 1)
            pool.memset(ones[:, :], 1.0).then_inc(filled, 1)
            pool.memset(zero_r[:, :], 0.0).then_inc(filled, 1)
            pool.memset(xr_pad[:, :, 0:3], 0.0).then_inc(filled, 1)
            pool.memset(wa_bd[:, :, :], 0.0).then_inc(filled, 1)
            pool.memset(wx_bd[:, :, :], 0.0).then_inc(filled, 1)
            pool.dma_start(gain[:, 0, :], A[GAINS[0]][0].partition_broadcast(P)).then_inc(gain_loaded[0], 16)
            pool.dma_start(cst[:, :], A["cst"]).then_inc(cst_loaded, 16)
            pool.dma_start(gain[:, 1, :], A[GAINS[1]][0].partition_broadcast(P)).then_inc(gain_loaded[1], 16)
            with nc.allow_non_contiguous_dma(reason="per-channel vectors"):
                for tap in range(4):
                    pool.dma_start(cwb[:, :, tap], A["conv_w"][0, tap].rearrange("(m p) -> p m", p=P)).then_inc(small1, 16)
                for n, name in enumerate(("conv_b", "b_a", "b_x", "lru_lambda")):
                    pool.dma_start(cwb[:, :, 4 + n], A[name][0].rearrange("(m p) -> p m", p=P)).then_inc(small1, 16)
                for b in range(2):
                    sinks = A["attn_sinks"][0].rearrange("(m b) -> b m", b=2)[b].partition_broadcast(P)
                    pool.dma_start(sink[:, 4 * b:4 * b + 4], sinks).then_inc(small1, 16)
            pool.wait_ge(filled, 6)
            for dst, name in ((wa_bd, "w_a"), (wx_bd, "w_x")):
                src = A[name][0].rearrange("(m b) c d -> b c m d", b=2)
                for b in range(2):
                    pool.dma_start(dst[64 * b:64 * b + 64, :, 64 * b:64 * b + 64], src[b]).then_inc(small3, 16)
            def gain_free(n):
                if n % 2 == 0:
                    pool.wait_ge(u_ready, n + 1)
                else:
                    pool.wait_ge(gain_used, n // 2)

            for n in range(2, 5):
                gain_free(n)
                pool.dma_start(gain[:, n % 2, :], A[GAINS[n]][0].partition_broadcast(P)).then_inc(gain_loaded[n % 2], 16)
            pool.wait_ge(h_ready, 4)
            with nc.allow_non_contiguous_dma(reason="per-channel vectors"):
                for tap in range(4):
                    pool.dma_start(cw_all[:, tap, :], A["conv_w_2"][0, tap].rearrange("(m p) -> p m", p=P)).then_inc(small2, 16)
                pool.dma_start(ab_w, A["w_in_2"][0][:, IN2_B:IN2_B + 16].rearrange("(k p) n -> p k n", p=P)).then_inc(small2, 16)
            pool.dma_start(dt_row[:, 0, :], A["dt_bias_2"][0].partition_broadcast(P)).then_inc(small2, 16)
            pool.dma_start(dt_row[:, 1, :], A["a_log_2"][0].partition_broadcast(P)).then_inc(small2, 16)
            pool.dma_start(gnorm, A["gdn_norm_2"][0].partition_broadcast(P)).then_inc(small2, 16)
            pool.memset(raw[:, :, 0:3], 0.0).then_inc(filled, 1)
            pool.wait_ge(mg_lo, 2)
            for n in range(5, 9):
                gain_free(n)
                pool.dma_start(gain[:, n % 2, :], A[GAINS[n]][0].partition_broadcast(P)).then_inc(gain_loaded[n % 2], 16)
                if n == 6:
                    pool.wait_ge(ut_lo, 9)
                    pool.dma_start(p_in, A["p_2"][0, 0].rearrange("(t p) n -> p t n", p=P)).then_inc(p_loaded, 16)

        @block.scalar
        def _(act):
            ch = Chain(act, act_chain)

            def hi(pu, stride=0, i=0):
                p, j = pu // 2, pu % 2
                if p >= P_ALL:
                    return
                layout = PLAN[p][0]
                if not isinstance(i, int):
                    assert stride % (2 * UNITS) == 0 or stride == 12
                    assert PLAN[(pu + stride) // 2] == PLAN[p]
                if isinstance(i, int):
                    pu, i, stride = pu + stride * i, 0, 0
                    p, layout = pu // 2, PLAN[pu // 2][0]
                if j == 0:
                    act.wait_ge(w_loaded[SLOT[p]], along(LOADS, p, stride // 2, i))
                if pu >= UNITS or not isinstance(i, int):
                    act.wait_ge(unit_done, i * stride + (pu - UNITS + 1))
                act.activation(split_view(wh, pu % UNITS, layout), raw_unit(SLOT[p], j, layout), ACT.Copy).then_inc(w_hi, 1)

            def unit_wait(pu, stride=0, i=0):
                act.wait_ge(unit_done, i * stride + (pu + 1))

            def root(n, cols, width=D):
                act.activation(st[:, 4:4 + cols], st[:, 0:cols], ACT.Sqrt, bias=eps[:, 0:1], scale=1.0 / width).then_inc(stat, 1)

            def norm(n, src, off):
                for t in range(NT):
                    act.wait_ge(h_ready, 2 * n + t + 1)
                    ch.link(act.activation(junk[:, :], src[:, t, :], ACT.Square, accum_out=st[:, t:t + 1]))
                root(n, NT)

            def acc_stat(last_unit):
                act.wait_ge(unit_done, last_unit + 1)
                for t in range(NT):
                    ch.link(act.activation(junk[:, :], acc[:, 2 * t:2 * t + 2, :].rearrange("p b n -> p (b n)"), ACT.Square,
                                           accum_out=st[:, t:t + 1]))
                root(0, NT)

            act.wait_ge(x_loaded, 32)
            act.wait_ge(filled, 4)
            for t in range(NT):
                ch.link(act.activation(junk[:, :], u[:, t, :], ACT.Square, accum_out=st[:, t:t + 1]))
            ch.link(act.activation(junk[0:META, :], meta[0:META, :], ACT.Square, accum_out=st[0:META, 2:3]))
            act.activation(st[:, 4:6], st[:, 0:2], ACT.Sqrt, bias=eps[:, 0:1], scale=1.0 / D)
            act.activation(st[0:META, 6:7], st[0:META, 2:3], ACT.Sqrt, bias=eps[0:META, 0:1], scale=1.0 / D).then_inc(stat, 1)
            act.wait_ge(small1, 16 * 10)
            ch.link(act.activation(lam_t[:, 0, :], cwb[:, :, 7], ACT.Abs))
            act.activation(lam_t[:, 1, :], lam_t[:, 0, :], ACT.Exp, scale=-1.0).then_inc(lam_e, 1)
            for n in range(4):
                hi(n)
            act.wait_ge(ut_ps, 1)
            act.activation(xTh[:, :, 0:META], ma[:, 0:KC * META].rearrange("p (k n) -> p k n", k=KC), ACT.Copy).then_inc(ut_hi, 1)
            for t in range(NT):
                act.wait_ge(ut_ps, t + 2)
                act.activation(xTh[:, :, META + t * P:META + (t + 1) * P],
                               acc[:, 2 * t:2 * t + 2, :].rearrange("p b (k n) -> p (b k) n", n=P), ACT.Copy).then_inc(ut_hi, 1)
            unit_wait(0)
            for v in range(KVH):
                for half in range(2):
                    ins = act.activation(kT1[64 * half:64 * half + 64, v, :], fm[64 * v:64 * v + 64, 0, 0:T1], ACT.Copy)
            ins.then_inc(emptied[0], 1)
            hi(4)
            unit_wait(1)
            act.activation(v1[:, 0:2, :], ma[:, 0:256].rearrange("p (a b) -> p a b", a=2), ACT.Copy)
            act.activation(v1[0:META, 2, :], ma[0:META, 256:384], ACT.Copy).then_inc(v1_out, 1)
            hi(5)
            act.wait_ge(filled, 4)
            for m in range(LT):
                unit_wait(2 + m)
                act.activation(xr_pad[:, m, 3:3 + T1], fm[:, m % 2, 0:T1], ACT.Copy).then_inc(emptied[m % 2], 1)
                hi(6 + m)
            for m in range(2):
                unit_wait(6 + m)
                act.activation(gy[:, m, :], fm[:, m % 2, 0:S], ACT.Gelu_apprx_tanh).then_inc(emptied[m % 2], 1)
                hi(10 + m)
            for m in range(LT):
                act.wait_ge(r_ps, m + 1)
                act.activation(r_g[:, m, :], acc[:, m, 0:T1], ACT.Sigmoid, bias=cwb[:, m, 5:6])
                act.activation(i_g[:, m, :], (ma, mb)[m % 2][:, 0:T1], ACT.Sigmoid, bias=cwb[:, m, 6:7]).then_inc(r_act, 1)
            act.wait_ge(sp_ready, 1)
            act.wait_ge(r_act, LT)
            for m in range(LT):
                act.activation(th_[:, m, :], r_g[:, m, :], ACT.Tanh, scale=lam_t[:, 6, m:m + 1]).then_inc(tanh_out, 1)
            for m in range(LT):
                act.activation(a_[:, m, :], r_g[:, m, :], ACT.Exp, scale=lam_t[:, 7, m:m + 1]).then_inc(a_out, 1)
            act.wait_ge(a_out, LT)
            act.activation(a2, a_, ACT.Square).then_inc(a_out, 1)
            for m in range(4):
                unit_wait(8 + m)
                act.activation(qT1[:, m, :], fm[:, m % 2, 0:S], ACT.Copy).then_inc(emptied[m % 2], 1)
                hi(12 + m)
            act.wait_ge(m2_out, 1)
            act.activation(a2, th_, ACT.Sqrt).then_inc(mult_out, 1)
            for m in range(2):
                unit_wait(12 + m)
                act.activation(gy[:, 2 + m, :], fm[:, m % 2, 0:S], ACT.Gelu_apprx_tanh).then_inc(emptied[m % 2], 1)
                hi(16 + m)
            act.wait_ge(rec_out, 1)
            act.activation(yTh[:, 4:8, :], gy, ACT.Copy).then_inc(rec_hi, 1)
            for b in range(2):
                nk = (P + META, 2 * P)[b]
                act.wait_ge(s1_max, b + 1)
                for hh in range(QH):
                    act.activation(p1[:, hh, 0:nk], sm1[:, hh, 0:nk], ACT.Exp, bias=st[:, 16 + hh:17 + hh],
                                   accum_out=st[:, 8 + hh:9 + hh]).then_inc(s1_exp, 1)
                act.activation(st[:, 24:32], st[:, 24:32], ACT.Exp).then_inc(s1_sink, 1)
                act.wait_ge(p1T_ps, 2 * b + 1)
                act.activation(pT1[:, 0:4, :, :], acc[:, 0:2, :].rearrange("p b (h c n) -> p (b h) c n", h=2, c=2), ACT.Copy).then_inc(p1T_out, 1)
                act.wait_ge(o1T_ps, b + 1)
                act.activation(yTh[:, 0:4, b * P:(b + 1) * P], mb[:, :].rearrange("p (k n) -> p k n", k=4), ACT.Copy).then_inc(o1T_hi, 1)
            for n in range(14, 22):
                hi(n + 4)
            acc_stat(21)
            norm(0, h, META)

            def norm_hi(base, off):
                for t in range(NT):
                    act.wait_ge(ut_ps, base + t + 1)
                    act.activation(xTh[:, :, off + t * P:off + (t + 1) * P],
                                   acc[:, 2 * t:2 * t + 2, :].rearrange("p b (k n) -> p (b k) n", n=P), ACT.Copy).then_inc(ut_hi, 1)

            norm_hi(3, 0)

            def ffn1_hidden(fu, par, n0, stride=0, i=0):
                for j in range(2):
                    unit_wait(fu + j, stride, i)
                    act.activation(hid_t[:, j, :], fm[:, j, 0:S], ACT.Relu).then_inc(emptied[j], 1)
                    hi(fu + j + 4, stride, i)
                for j in range(2):
                    act.wait_ge(hid_s, i * (stride // 2) + (2 * n0 + j + 1))
                    act.activation(hid_h[:, par, j, :], hid_q[:, j, :], ACT.Copy).then_inc(hid_hi, 1)

            def acc_units(fu, stride=0, i=0):
                for j in range(2):
                    hi(fu + j + 4, stride, i)

            F = 2 * P_FF1
            ffn1_hidden(F, 0, 0)
            for i in rounds(act, 7):
                ffn1_hidden(F + 2, 1, 1, 8, i)
                acc_units(F + 4, 8, i)
                ffn1_hidden(F + 6, 0, 2, 8, i)
                acc_units(F + 8, 8, i)
            ffn1_hidden(F + 58, 1, 15)
            acc_units(F + 60)
            acc_units(F + 62)
            acc_stat(F + 63)
            norm(1, h, 0)
            norm_hi(5, 0)
            act.wait_ge(small2, 16 * 8)
            act.activation(ab_h, ab_w, ACT.Copy).then_inc(ab_hi, 1)
            act.activation(dt_row[:, 1, :], dt_row[:, 1, :], ACT.Exp).then_inc(ab_act, 1)
            act.wait_ge(ab_out, 1)
            act.activation(g_all[:, 0, :, :], ma[:, 0:32].rearrange("p (t n) -> p t n", t=2)[:, :, 0:8], ACT.Sigmoid).then_inc(ab_act, 1)
            ch.link(act.activation(tmp16[:, 1, :], tmp16[:, 0, :], ACT.Abs))
            act.activation(tmp16[:, 2, :], tmp16[:, 1, :], ACT.Exp, scale=-1.0).then_inc(ab_act, 1)

            def moba_unit(c, fu, stride, a, pair):
                unit_wait(fu, stride, a)
                if c < 4:
                    act.wait_ge(rope_out, pair) if not (isinstance(pair, int) and pair == 0) else None
                    act.activation(qk[:, c, :], fm[:, c % 2, 0:S], ACT.Copy).then_inc(emptied[c % 2], 1)
                elif c < 6:
                    act.activation(ga[:, bass.ds(pair * 2 + (c - 4), 1), :].rearrange("p a n -> p (a n)"),
                                   fm[:, c % 2, 0:S], ACT.Copy).then_inc(emptied[c % 2], 1)
                elif c == 7:
                    for t in range(NT):
                        act.activation(va[:, t, :], fm[:, t, 0:S], ACT.Copy).then_inc(emptied[t], 1)
                hi(fu + 4, stride, a)

            def gdn_unit(c, fu, stride, a, pair):
                unit_wait(fu, stride, a)
                if not (isinstance(pair, int) and pair == 0):
                    act.wait_ge(cv_out, pair)
                if c < 6:
                    act.activation(raw[:, c, 3:3 + S], fm[:, c % 2, 0:S], ACT.Copy).then_inc(emptied[c % 2], 1)
                elif c == 7:
                    for t in range(NT):
                        act.activation(zr[:, t, :], fm[:, t, 0:S], ACT.Copy).then_inc(emptied[t], 1)
                hi(fu + 4, stride, a)

            def gateb_unit(c, fu, stride, a, pair):
                unit_wait(fu, stride, a)
                act.activation(gb_s[:, c, :], fm[:, c % 2, 0:S], ACT.Copy).then_inc(emptied[c % 2], 1)
                hi(fu + 4, stride, a)

            def moba_stage(s, a):
                if s == 0:
                    act.wait_ge(emptied[0], along(EMPTIED0, 2 * P_MOBA + 4, 8, a))
                    act.wait_ge(emptied[1], along(EMPTIED1, 2 * P_MOBA + 4, 8, a))
                    act.activation(rot[0:64, :, :], qk[64:128, :, :], ACT.Copy)
                    act.activation(rot[64:128, :, :], qk[0:64, :, :], ACT.Copy).then_inc(rot_out, 1)
                if s == 2:
                    act.wait_ge(s2_max, a + 1)
                    for n, (lo_, hi_) in enumerate(((0, 256), (256, 384))):
                        for j in range(2):
                            ins = act.activation(p2[:, j, lo_:hi_], sm2[:, j, lo_:hi_], ACT.Exp,
                                                 bias=st[:, 16 + 2 * n + j:17 + 2 * n + j], accum_out=st[:, 8 + 2 * n + j:9 + 2 * n + j])
                    ins.then_inc(s2_exp, 1)
                if s == 3:
                    act.wait_ge(p2T_ps, a + 1)
                    act.activation(pT2[:, 0, :], acc[:, 2, 0:384], ACT.Copy).then_inc(p2T_a, 1)
                if s == 4:
                    act.wait_ge(o2_ps, a + 1)
                    act.activation(yTh[:, bass.ds(a * 2, 2), :], ma[:, :].rearrange("p (j n) -> p j n", j=2), ACT.Copy).then_inc(o2_hi, 1)

            def gdn_stage(s, a):
                if s == 0:
                    act.wait_ge(cv_out, a + 1)
                    act.activation(cv, cv, ACT.Silu)
                    act.wait_ge(emptied[0], along(EMPTIED0, 2 * P_GDN + 8, 8, a))
                    act.wait_ge(emptied[1], along(EMPTIED1, 2 * P_GDN + 8, 8, a))
                    act.activation(sz, zr, ACT.Silu).then_inc(silu_out, 1)
                    act.wait_ge(silu_out, a + 1)
                    act.activation(sq, cv[:, 0:4, :].rearrange("p a b -> p (a b)"), ACT.Square).then_inc(sq_out, 1)
                if s == 1:
                    act.wait_ge(ssq_ps, a + 1)
                    ch.link(act.activation(rk, acc[:, 0:2, :].rearrange("p b n -> p (b n)"), ACT.Ln, bias=eps[:, 0:1]))
                    act.activation(rk, rk, ACT.Exp, scale=-0.5).then_inc(rk_out, 1)
                if s == 2:
                    act.wait_ge(t12_out, a + 1)
                    act.activation(eg, acc[:, 2, 256:512].rearrange("p (j n) -> p j n", j=2), ACT.Exp)
                    for pr in range(4):
                        c, j = pr // 2, pr % 2
                        act.activation(dt_[:, pr, :], dt_[:, pr, :], ACT.Exp, bias=sc[:, 2, c, j:j + 1])
                        ins = act.activation(dl_[:, pr, :], dl_[:, pr, :], ACT.Exp, bias=sc[:, 1, c, j:j + 1])
                    ins.then_inc(dt_out, 1)
                    act.wait_ge(vT_ps, a + 1)
                    for pr in range(4):
                        c, j = pr // 2, pr % 2
                        ins = act.activation(vb[:, pr, :], acc[:, 3, pr * P:(pr + 1) * P], ACT.Copy, scale=sc[:, 0, c, j:j + 1])
                    ins.then_inc(vb_out, 1)
                if s == 3:
                    act.wait_ge(kT_ps, a + 1)
                    for j in range(2):
                        act.activation(kdec[:, j, :], acc[:, 0, j * P:(j + 1) * P], ACT.Copy, scale=sc[:, 4, 0, j:j + 1])
                        ins = act.activation(kbe[:, j, :], acc[:, 0, (2 + j) * P:(3 + j) * P], ACT.Copy, scale=sc[:, 3, 1, j:j + 1])
                    ins.then_inc(kv_out, 1)
                if 5 <= s < 17 and s % 2 == 1:
                    lv = (s - 5) // 2
                    act.wait_ge(lv_p, a * 6 + (lv + 1))
                    act.activation(P_, acc[:, 0, :].rearrange("p (r n) -> p r n", r=4), ACT.Copy).then_inc(lv_pe, 1)
                if s == 17:
                    act.wait_ge(uw_ps, a + 1)
                    act.activation(u0, acc[:, 3, 0:256].rearrange("p (j n) -> p j n", j=2), ACT.Copy).then_inc(u0_out, 1)
                if s == 18:
                    act.wait_ge(so_ps, a + 1)
                    act.activation(S1, acc[:, 1, 0:256].rearrange("p (j n) -> p j n", j=2), ACT.Copy).then_inc(S1_out, 1)
                if s == 19:
                    act.wait_ge(vn_ps, a + 1)
                    act.activation(vn, acc[:, 3, 256:512].rearrange("p (j n) -> p j n", j=2), ACT.Copy).then_inc(vn_out, 1)
                if s == 20:
                    act.wait_ge(o_ps, a + 1)
                    for pr in range(4):
                        ins = act.activation(junk[:, pr * P:(pr + 1) * P], acc[:, 2, pr * P:(pr + 1) * P], ACT.Square, accum_out=st[:, pr:pr + 1])
                    ch.link(ins)
                    ch.link(act.activation(st[:, 4:8], st[:, 0:4], ACT.Ln, bias=eps[:, 0:1], scale=1.0 / P))
                    act.activation(st[:, 4:8], st[:, 4:8], ACT.Exp, scale=-0.5).then_inc(og_out, 1)
                if s == 21:
                    act.wait_ge(yT_ps, a + 1)
                    dst = ybh[:, bass.ds(a * 2, 2), :].rearrange("p j (c n) -> p j c n", c=2)
                    act.activation(dst, acc[:, 0, :].rearrange("p (c j n) -> p j c n", c=2, j=2), ACT.Copy).then_inc(yb_hi, 1)

            def pair_round(weave, stage, unit, fu, a, pair, mine=0):
                before = ch.n
                for s, done in enumerate(finished(weave)):
                    stage(s, a)
                    for c in done:
                        unit(c, fu + c, 8, a, pair)
                return ch.n - before if isinstance(ch.n, int) else None

            M, G = 2 * P_MOBA, 2 * P_GDN
            for c in range(8):
                moba_unit(c, M + c, 8, 0, 0)
            act.wait_ge(gc_ps, 1)
            gcs = mb[:, 0:32].rearrange("p (v c h) -> p v c h", v=2, c=2)
            act.activation(g_all[:, 1, :, :], gcs[:, 0], ACT.Copy)
            act.activation(g_all[:, 2, :, :], gcs[:, 0], ACT.Copy, scale=-1.0)
            act.activation(g_all[:, 3, :, :], gcs[:, 0], ACT.Exp).then_inc(gc_act, 1)
            act.wait_ge(gc_ready, 1)
            act.activation(g_all[:, 4, :, :], g_all[:, 6, :, :], ACT.Exp).then_inc(gc_act, 1)
            for i in rounds(act, 3, ch, 0):
                pair_round(MOBA_WEAVE, moba_stage, moba_unit, M + 8, i, i + 1)
            pair_round(MOBA_WEAVE, moba_stage, gdn_unit, M + 8, 3, 0)
            for i in rounds(act, 3, ch, 3):
                pair_round(GDN_WEAVE, gdn_stage, gdn_unit, G + 8, i, i + 1)
            pair_round(GDN_WEAVE, gdn_stage, gateb_unit, G + 8, 3, 0)
            act.activation(ga, ga, ACT.Sigmoid).then_inc(sig_a, 1)
            act.wait_ge(emptied[0], EMPTIED0[2 * P_PROJA])
            act.wait_ge(emptied[1], EMPTIED1[2 * P_PROJA])
            act.activation(gb_s, gb_s, ACT.Sigmoid).then_inc(sig_b, 1)
            for n in range(16):
                hi(2 * P_PROJA + n + 4)
            for q in range(2):
                act.wait_ge(mg_out, 4 * q + 4)
                act.activation(yTh[:, 4 * q:4 * q + 4, :], gb_s[:, 4 * q:4 * q + 4, :], ACT.Copy).then_inc(mg_hi, 1)
            for n in range(8):
                hi(2 * P_OUT2 + n + 4)
            acc_stat(2 * P_OUT2 + 7)
            norm(2, h, 0)
            norm_hi(7, 0)
            F2 = 2 * P_FF2

            def silu_gate(fu, stride=0, i=0, k=0):
                for j in range(2):
                    unit_wait(fu + j, stride, i)
                    if k > 0:
                        act.wait_ge(swi_m, i * (stride // 3) + 2 * (k - 1) + j + 1)
                    act.activation(gate_s[:, j, :], fm[:, j, 0:S], ACT.Silu).then_inc(swi_a, 1)
                    hi(fu + j + 4, stride, i)

            def hid2_hi(fu, stride=0, i=0, k=0):
                for j in range(2):
                    act.wait_ge(swi_m, i * (stride // 3) + 2 * k + j + 1)
                    act.activation(hid2_h[:, j, :], hid2[:, j, :], ACT.Copy).then_inc(swi_hi, 1)
                    hi(fu + j + 4, stride, i)

            silu_gate(F2)
            hid2_hi(F2 + 2)
            for i in rounds(act, 4):
                for n in range(2):
                    silu_gate(F2 + 4 + 6 * n, 12, i, n + 1)
                    acc_units(F2 + 6 + 6 * n, 12, i)
                    hid2_hi(F2 + 8 + 6 * n, 12, i, n + 1)
            for n in range(2):
                silu_gate(F2 + 4 + 6 * n + 48, 0, 0, n + 9)
                acc_units(F2 + 6 + 6 * n + 48)
                hid2_hi(F2 + 8 + 6 * n + 48, 0, 0, n + 9)
            acc_units(F2 + 64)
            acc_stat(F2 + 65)
            act.wait_ge(ut_ps, 10)
            act.activation(xTh[:, 0:2, 0:S].rearrange("p k (t n) -> p t k n", t=2), ma[:, :].rearrange("p (t k n) -> p t k n", t=2, k=2), ACT.Copy).then_inc(ut_hi, 1)
            for n in range(2):
                hi(2 * P_PLE + n + 4)
            acc_stat(2 * P_PLE + 1)
            norm_hi(10, 0)
            for n in range(8):
                hi(2 * P_PGATE + n + 4)
            act.wait_ge(unit_done, 2 * P_ALL)
            for t in range(NT):
                act.activation(u[:, t, :], acc[:, 2 * t:2 * t + 2, :].rearrange("p b n -> p (b n)"), ACT.Sigmoid).then_inc(fin_sig, 1)

        @block.vector
        def _(dve):
            ch = Chain(dve, dve_chain)
            link = ch.link
            TT, TS, STT = dve.tensor_tensor, dve.tensor_scalar, dve.scalar_tensor_tensor

            def lo(pu, stride=0, i=0):
                p, j = pu // 2, pu % 2
                if p >= P_ALL:
                    return
                if isinstance(i, int):
                    pu, i, stride = pu + stride * i, 0, 0
                    p = pu // 2
                layout = PLAN[p][0]
                dve.wait_ge(w_hi, i * stride + (pu + 1))
                TT(split_view(wl, pu % UNITS, layout), raw_unit(SLOT[p], j, layout),
                   split_view(wh, pu % UNITS, layout).bitcast(F32), ALU.subtract).then_inc(w_lo, 1)

            def log1p(y, z, t, out):
                link(TS(t, y, 2.0, None, ALU.add))
                link(dve.reciprocal(t, t))
                link(TT(z, y, t, ALU.mult))
                link(TT(t, z, z, ALU.mult))
                link(TS(out, t, 1.0 / 19, None, ALU.mult))
                for c in (17, 15, 13, 11, 9, 7, 5, 3):
                    link(STT(out, out, 1.0 / c, t, ALU.add, ALU.mult))
                link(STT(out, out, 1.0, z, ALU.add, ALU.mult))
                link(TS(out, out, 2.0, None, ALU.mult))

            def norm_rows(n, src, g, off, base):
                dve.wait_ge(stat, n)
                link(dve.reciprocal(st[:, 4:6], st[:, 4:6]))
                dve.wait_ge(gain_loaded[g % 2], 16 * (g // 2 + 1))
                for t in range(NT):
                    STT(u[:, t, :], src[:, t, :], st[:, 4 + t:5 + t], gain[:, g % 2, :], ALU.mult, ALU.mult).then_inc(u_ready, 1)

            def norm_lo(base, off):
                for t in range(NT):
                    dve.wait_ge(ut_hi, base + t + 1)
                    TT(xTl[:, :, off + t * P:off + (t + 1) * P],
                       acc[:, 2 * t:2 * t + 2, :].rearrange("p b (k n) -> p (b k) n", n=P),
                       xTh[:, :, off + t * P:off + (t + 1) * P].bitcast(F32), ALU.subtract).then_inc(ut_lo, 1)

            def residual(n, g):
                dve.wait_ge(stat, n)
                link(dve.reciprocal(st[:, 4:6], st[:, 4:6]))
                dve.wait_ge(gain_loaded[g % 2], 16 * (g // 2 + 1))
                for t in range(NT):
                    ins = STT(u[:, t, :], acc[:, 2 * t:2 * t + 2, :].rearrange("p b n -> p (b n)"), st[:, 4 + t:5 + t],
                              gain[:, g % 2, :], ALU.mult, ALU.mult)
                    if t == 0:
                        link(ins)
                    else:
                        ins.then_inc(gain_used, 1)
                        dve.wait_ge(gain_used, g // 2 + 1)
                    TT(h[:, t, :], h[:, t, :], u[:, t, :], ALU.add).then_inc(h_ready, 1)

            dve.wait_ge(stat, 1)
            dve.wait_ge(filled, 4)
            dve.reciprocal(st[0:META, 6:7], st[0:META, 6:7])
            link(dve.reciprocal(st[:, 4:6], st[:, 4:6]))
            dve.wait_ge(gain_loaded[0], 16)
            dve.wait_ge(x_loaded, 32)
            for t in range(NT):
                link(dve.tensor_copy(h[:, t, :], u[:, t, :]))
            STT(meta[0:META, :], meta[0:META, :], st[0:META, 6:7], gain[0:META, 0, :], ALU.mult, ALU.mult).then_inc(u_ready, 1)
            for t in range(NT):
                STT(u[:, t, :], h[:, t, :], st[:, 4 + t:5 + t], gain[:, 0, :], ALU.mult, ALU.mult).then_inc(u_ready, 1)
            for n in range(4):
                lo(n)
            dve.wait_ge(ut_hi, 1)
            TT(xTl[:, :, 0:META], ma[:, 0:KC * META].rearrange("p (k n) -> p k n", k=KC), xTh[:, :, 0:META].bitcast(F32),
               ALU.subtract).then_inc(ut_lo, 1)
            norm_lo(1, META)
            dve.wait_ge(lam_e, 1)
            log1p(lam_t[:, 1, :], lam_t[:, 2, :], lam_t[:, 3, :], lam_t[:, 4, :])
            link(TS(lam_t[:, 5, :], cwb[:, :, 7], -1.0, 0.0, ALU.mult, ALU.max))
            link(TT(lam_t[:, 4, :], lam_t[:, 4, :], lam_t[:, 5, :], ALU.add))
            TS(lam_t[:, 6, :], lam_t[:, 4, :], 8.0, None, ALU.mult)
            TS(lam_t[:, 7, :], lam_t[:, 4, :], -8.0, None, ALU.mult).then_inc(sp_ready, 1)
            lo(4)
            lo(5)
            for q in range(2):
                lo(6 + 2 * q)
                lo(7 + 2 * q)
                dve.wait_ge(emptied[0], 2 + q)
                dve.wait_ge(emptied[1], 1 + q)
                for m in (2 * q, 2 * q + 1):
                    ins = TS(xc[:, m, :], xr_pad[:, m, 0:T1], cwb[:, m, 0:1], cwb[:, m, 4:5], ALU.mult, ALU.add)
                link(ins)
                for tap in range(1, 4):
                    for m in (2 * q, 2 * q + 1):
                        ins = STT(xc[:, m, :], xr_pad[:, m, tap:tap + T1], cwb[:, m, tap:tap + 1], xc[:, m, :], ALU.mult, ALU.add)
                    if tap < 3:
                        link(ins)
                ins.then_inc(xc_ready, 1)
            lo(10)
            lo(11)
            dve.wait_ge(r_act, LT)
            dve.wait_ge(xc_ready, 2)
            link(TT(xc, i_g, xc, ALU.mult))
            dve.wait_ge(tanh_out, LT)
            dve.wait_ge(a_out, LT + 1)
            STT(th_, a2, 1.0, th_, ALU.add, ALU.mult).then_inc(m2_out, 1)
            for n in range(12, 16):
                lo(n)
            dve.wait_ge(mult_out, 1)
            link(TT(xc, a2, xc, ALU.mult))
            for m in range(LT):
                ins = dve.tensor_tensor_scan(r_g[:, m, :], a_[:, m, :], xc[:, m, :], 0.0, ALU.mult, ALU.add)
            link(ins)
            lo(16)
            lo(17)
            dve.wait_ge(emptied[0], EMPTIED0[14])
            dve.wait_ge(emptied[1], EMPTIED1[14])
            TT(gy, gy, r_g[:, :, META:T1], ALU.mult).then_inc(rec_out, 1)
            dve.wait_ge(rec_hi, 1)
            TT(yTl[:, 4:8, :], gy, yTh[:, 4:8, :].bitcast(F32), ALU.subtract).then_inc(rec_lo, 1)
            dve.wait_ge(small1, 16 * 10)
            for b in range(2):
                nk = (P + META, 2 * P)[b]
                mask = cst[:, (C_WIN0, C_WIN1)[b]:(C_WIN0, C_WIN1)[b] + nk]
                dve.wait_ge(s1_ps, b + 1)
                dve.wait_ge(cst_loaded, 16)
                sc_ps = acc[:, :, :].rearrange("p b (h n) -> p (b h) n", h=2)
                link(STT(sm1[:, :, 0:nk], sc_ps[:, :, 0:nk], SC1, mask.unsqueeze(1).to_broadcast([P, QH, nk]), ALU.mult, ALU.add))
                if b:
                    dve.wait_ge(s1_exp, QH * b)
                link(dve.tensor_reduce(st[:, 16:24], sm1[:, :, 0:nk], AX, ALU.max))
                link(TT(st[:, 16:24], st[:, 16:24], sink, ALU.max))
                link(TT(st[:, 24:32], sink, st[:, 16:24], ALU.subtract))
                TS(st[:, 16:24], st[:, 16:24], -1.0, None, ALU.mult).then_inc(s1_max, 1)
                dve.wait_ge(s1_sink, b + 1)
                dve.wait_ge(s1_exp, QH * (b + 1))
                link(TT(st[:, 8:16], st[:, 8:16], st[:, 24:32], ALU.add))
                link(dve.reciprocal(st[:, 8:16], st[:, 8:16]))
                dve.wait_ge(p1T_ps, 2 * b + 2)
                dve.tensor_copy(pT1[:, 4:8, :, :], acc[:, 2:4, :].rearrange("p b (h c n) -> p (b h) c n", h=2, c=2)).then_inc(p1T_out, 1)
                dve.wait_ge(o1_ps, b + 1)
                TT(o1.rearrange("p (m b n) -> p m b n", m=4, b=2), ma[:, :].rearrange("p (m b n) -> p m b n", m=4, b=2),
                   st[:, 8:16].rearrange("p (b m) -> p m b", b=2).unsqueeze(3).to_broadcast([P, 4, 2, HD1]), ALU.mult).then_inc(o1_out, 1)
                dve.wait_ge(o1T_hi, b + 1)
                TT(yTl[:, 0:4, b * P:(b + 1) * P], mb[:, :].rearrange("p (k n) -> p k n", k=4),
                   yTh[:, 0:4, b * P:(b + 1) * P].bitcast(F32), ALU.subtract).then_inc(o1T_lo, 1)
            for n in range(18, 26):
                lo(n)
            dve.wait_ge(ut_lo, 3)
            residual(2, 1)
            norm_rows(3, h, 2, 0, 3)
            norm_lo(3, 0)

            def ffn1_hidden(fu, par, n0, stride=0, i=0):
                for j in range(2):
                    lo(fu + j + 4, stride, i)
                    dve.wait_ge(emptied[j], along(AFTER[j], fu + j, stride, i))
                    if n0:
                        dve.wait_ge(hid_lo, i * (stride // 2) + 2 * n0 + j - 1)
                    TT(hid_q[:, j, :], hid_t[:, j, :], hid_t[:, j, :], ALU.mult).then_inc(hid_s, 1)
                for j in range(2):
                    k = i * (stride // 2) + 2 * n0 + j + 1
                    dve.wait_ge(hid_hi, k)
                    TT(hid_l[:, par, j, :], hid_q[:, j, :], hid_h[:, par, j, :].bitcast(F32), ALU.subtract).then_inc(hid_lo, 1)

            def acc_units(fu, stride=0, i=0):
                for j in range(2):
                    lo(fu + j + 4, stride, i)

            F = 2 * P_FF1
            AFTER = [[EMPTIED[min(n + 1, 2 * P_ALL - 1)][b] for n in range(2 * P_ALL)] for b in range(2)]
            ffn1_hidden(F, 0, 0)
            for i in rounds(dve, 7):
                ffn1_hidden(F + 2, 1, 1, 8, i)
                acc_units(F + 4, 8, i)
                ffn1_hidden(F + 6, 0, 2, 8, i)
                acc_units(F + 8, 8, i)
            ffn1_hidden(F + 58, 1, 15)
            acc_units(F + 60)
            acc_units(F + 62)
            residual(4, 3)
            norm_rows(5, h, 4, 0, 5)
            norm_lo(5, 0)
            dve.wait_ge(ab_hi, 1)
            TT(ab_l, ab_w, ab_h.bitcast(F32), ALU.subtract).then_inc(ab_lo, 1)
            dve.wait_ge(ab_ps, 1)
            x_dt = tmp16[:, 0, :].rearrange("p (t n) -> p t n", t=2)
            TT(x_dt, ma[:, 0:32].rearrange("p (t n) -> p t n", t=2)[:, :, 8:16],
               dt_row[:, 0, :].unsqueeze(1).to_broadcast([P, 2, 8]), ALU.add).then_inc(ab_out, 1)
            dve.wait_ge(ab_act, 3)
            log1p(tmp16[:, 2, :], tmp16[:, 3, :], tmp16[:, 4, :], tmp16[:, 5, :])
            link(STT(tmp16[:, 5, :], tmp16[:, 0, :], 0.0, tmp16[:, 5, :], ALU.max, ALU.add))
            STT(g_all[:, 5, :, :], tmp16[:, 5, :].rearrange("p (t n) -> p t n", t=2), -1.0,
                dt_row[:, 1, :].unsqueeze(1).to_broadcast([P, 2, 8]), ALU.mult, ALU.mult).then_inc(g_ready, 1)

            def pair_unit(c, fu, stride, a, pair):
                lo(fu + 4, stride, a)

            def moba_stage(s, a):
                if s == 0:
                    cosb = cst[:, C_COS:C_SIN].unsqueeze(1).to_broadcast([P, 4, S])
                    sinb = cst[:, C_SIN:C_END].unsqueeze(1).to_broadcast([P, 4, S])
                    dve.wait_ge(rot_out, a + 1)
                    TT(qr, qk, cosb, ALU.mult)
                    link(TT(rot, rot, sinb, ALU.mult))
                    TT(qr, qr, rot, ALU.add).then_inc(rope_out, 1)
                if s == 1:
                    dve.wait_ge(s2_ps, a + 1)
                    mask = cst[:, C_MOBA:C_WIN0].unsqueeze(1).to_broadcast([P, 2, 384])
                    link(STT(sm2, acc[:, 0:2, 0:384], SC2, mask, ALU.mult, ALU.add))
                    dve.tensor_reduce(st[:, 16:18], sm2[:, :, 0:256], AX, ALU.max)
                    link(dve.tensor_reduce(st[:, 18:20], sm2[:, :, 256:384], AX, ALU.max))
                    TS(st[:, 16:20], st[:, 16:20], -1.0, None, ALU.mult).then_inc(s2_max, 1)
                if s == 2:
                    dve.wait_ge(s2_exp, a + 1)
                    link(dve.reciprocal(st[:, 8:12], st[:, 8:12]))
                    for n, (lo_, hi_) in enumerate(((0, 256), (256, 384))):
                        for j in range(2):
                            ins = TS(p2[:, j, lo_:hi_], p2[:, j, lo_:hi_], st[:, 8 + 2 * n + j:9 + 2 * n + j], None, ALU.mult)
                    ins.then_inc(s2_p, 1)
                if s == 3:
                    dve.wait_ge(p2T_ps, a + 1)
                    dve.tensor_copy(pT2[:, 1, :], acc[:, 3, 0:384]).then_inc(p2T_v, 1)
                if s == 4:
                    dve.wait_ge(o2_hi, a + 1)
                    TT(yTl[:, bass.ds(a * 2, 2), :], ma[:, :].rearrange("p (j n) -> p j n", j=2),
                       yTh[:, bass.ds(a * 2, 2), :].bitcast(F32), ALU.subtract).then_inc(o2_lo, 1)

            def rows4(x):
                return x.rearrange("p (r n) -> p r n", r=4)

            def spread(x):
                return x.unsqueeze(1).to_broadcast([P, 4, P])

            def level_mask(n):
                return spread(cst[:, C_LEV + n * P:C_LEV + (n + 1) * P])

            def gdn_stage(s, a):
                if s == 0:
                    dve.wait_ge(gc_act, 2)
                    dve.tensor_copy(sc, g_all[:, 0:6, :, bass.ds(a * 2, 2)])
                    link(dve.tensor_copy(cw.rearrange("p t (k j) -> p t k j", k=3),
                                         cw_all.rearrange("p t (k h) -> p t k h", k=3)[:, :, :, bass.ds(a * 2, 2)]))
                    gsrc = sc[:, 5, :, :].rearrange("p c j -> p (c j)").unsqueeze(2).to_broadcast([P, 4, P])
                    dve.tensor_copy(gb, gsrc).then_inc(gb_out, 1)
                    dve.wait_ge(emptied[0], along(EMPTIED0, 2 * P_GDN + 8, 8, a))
                    dve.wait_ge(emptied[1], along(EMPTIED1, 2 * P_GDN + 8, 8, a))
                    dve.wait_ge(filled, 7)
                    for m in range(6):
                        ins = TS(cv[:, m, :], raw[:, m, 0:S], cw[:, 0, m:m + 1], None, ALU.mult)
                    link(ins)
                    for tap in range(1, 4):
                        for m in range(6):
                            ins = STT(cv[:, m, :], raw[:, m, tap:tap + S], cw[:, tap, m:m + 1], cv[:, m, :], ALU.mult, ALU.add)
                        if tap < 3:
                            link(ins)
                    ins.then_inc(cv_out, 1)
                if s == 1:
                    dve.wait_ge(rk_out, a + 1)
                    q4 = cv[:, 0:4, :].rearrange("p a b -> p (a b)")
                    TT(q4, q4, rk, ALU.mult).then_inc(qkn_out, 1)
                if s == 2:
                    dve.wait_ge(gcb_ps, a + 1)
                    TT(dt_, rows4(acc[:, 2, :]), spread(cst[:, C_MUP:C_MLOW]), ALU.add)
                    TT(dl_, spread(cst[:, C_MLOW:C_LEV]), rows4(acc[:, 2, :]), ALU.subtract).then_inc(t12_out, 1)
                if s == 3:
                    dve.wait_ge(qkg_ps, a + 1)
                    dve.wait_ge(dt_out, a + 1)
                    qkg = acc[:, 1:3, :].rearrange("p b (r n) -> p (b r) n", r=2)
                    STT(attnT, qkg[:, :, 0:P], SC2, dt_, ALU.mult, ALU.mult)
                    for pr in range(4):
                        ins = STT(A_[:, pr, :], qkg[:, pr, P:2 * P], sc[:, 0, pr // 2, pr % 2:pr % 2 + 1], dl_[:, pr, :], ALU.mult, ALU.mult)
                    link(ins)
                    link(TT(rows4(C_[:, 0, :]), A_, level_mask(0), ALU.mult))
                    TT(rows4(C_[:, 1, :]), A_, level_mask(1), ALU.mult)
                    TT(X_, spread(ident), rows4(C_[:, 0, :]), ALU.subtract).then_inc(c0_out, 1)
                    STT(qeg, cv[:, 0:2, P:2 * P], SC2, eg, ALU.mult, ALU.mult)
                if s == 4:
                    dve.wait_ge(c0_ps, a + 1)
                    TT(XT_, spread(ident), rows4(acc[:, 3, :]), ALU.subtract).then_inc(lv_x, 1)
                if 5 <= s < 17 and s % 2 == 1:
                    lv = (s - 5) // 2 + 1
                    if lv < 6:
                        if lv > 1:
                            dve.wait_ge(lv_p, a * 6 + (lv - 1))
                        TT(rows4(C_[:, (lv + 1) % 2, :]), A_, level_mask(lv + 1), ALU.mult).then_inc(lv_c, 1)
                if 5 <= s < 17 and s % 2 == 0:
                    lv = (s - 5) // 2 + 1
                    dve.wait_ge(lv_z, a * 6 + lv)
                    if lv < 6:
                        TT(X_, X_, rows4(acc[:, 2, :]), ALU.subtract)
                    TT(XT_, XT_, rows4(acc[:, 1, :]), ALU.subtract).then_inc(lv_x, 1)
                if s == 17:
                    dve.wait_ge(uw_ps, a + 1)
                    TS(nwT, acc[:, 0, 0:256].rearrange("p (j n) -> p j n", j=2), -1.0, None, ALU.mult).then_inc(nw_out, 1)
                if s == 20:
                    dve.wait_ge(og_out, a + 1)
                    for pr in range(4):
                        ins = STT(y_[:, pr, :], acc[:, 2, pr * P:(pr + 1) * P], st[:, 4 + pr:5 + pr], gnorm, ALU.mult, ALU.mult)
                    link(ins)
                    TT(y_, y_, sz.rearrange("p t (j n) -> p (t j) n", j=2), ALU.mult).then_inc(y_out, 1)
                if s == 21:
                    dve.wait_ge(yb_hi, a + 1)
                    dst = ybl[:, bass.ds(a * 2, 2), :].rearrange("p j (c n) -> p j c n", c=2)
                    hi_ = ybh[:, bass.ds(a * 2, 2), :].rearrange("p j (c n) -> p j c n", c=2).bitcast(F32)
                    TT(dst, acc[:, 0, :].rearrange("p (c j n) -> p j c n", c=2, j=2), hi_, ALU.subtract).then_inc(yb_lo, 1)

            def pair_round(weave, stage, fu, a):
                for s, done in enumerate(finished(weave)):
                    stage(s, a)
                    for c in done:
                        pair_unit(c, fu + c, 8, a, None)

            M, G = 2 * P_MOBA, 2 * P_GDN
            for c in range(8):
                pair_unit(c, M + c, 8, 0, 0)
            dve.wait_ge(gc_act, 1)
            gcs = mb[:, 0:32].rearrange("p (v c h) -> p v c h", v=2, c=2)
            TT(g_all[:, 3, :, :], g_all[:, 3, :, :], g_all[:, 0, :, :], ALU.mult)
            TT(g_all[:, 6, :, :], gcs[:, 1], g_all[:, 1, :, :], ALU.subtract).then_inc(gc_ready, 1)
            for i in rounds(dve, 3, ch, 4):
                pair_round(MOBA_WEAVE, moba_stage, M + 8, i)
            pair_round(MOBA_WEAVE, moba_stage, M + 8, 3)
            for i in rounds(dve, 3, ch, 7):
                pair_round(GDN_WEAVE, gdn_stage, G + 8, i)
            pair_round(GDN_WEAVE, gdn_stage, G + 8, 3)
            dve.wait_ge(sig_a, 1)
            for m in range(KC):
                pu = 2 * P_PROJA + m
                dve.wait_ge(unit_done, pu + 1)
                TT(ga[:, m, :], ga[:, m, :], fm[:, m % 2, 0:S], ALU.mult).then_inc(emptied[m % 2], 1)
                lo(pu + 4)
            dve.wait_ge(sig_b, 1)
            dve.wait_ge(emptied[0], EMPTIED0[2 * P_PROJB])
            dve.wait_ge(emptied[1], EMPTIED1[2 * P_PROJB])
            for m in range(KC):
                pu = 2 * P_PROJB + m
                dve.wait_ge(unit_done, pu + 1)
                ins = TT(gb_s[:, m, :], gb_s[:, m, :], fm[:, m % 2, 0:S], ALU.mult)
                ins.then_inc(emptied[m % 2], 1)
                dve.wait_ge(emptied[m % 2], AFTER[m % 2][pu])
                TT(gb_s[:, m, :], gb_s[:, m, :], ga[:, m, :], ALU.add).then_inc(mg_out, 1)
                lo(pu + 4)
            for q in range(2):
                dve.wait_ge(mg_hi, q + 1)
                TT(yTl[:, 4 * q:4 * q + 4, :], gb_s[:, 4 * q:4 * q + 4, :], yTh[:, 4 * q:4 * q + 4, :].bitcast(F32), ALU.subtract).then_inc(mg_lo, 1)
            for n in range(8):
                lo(2 * P_OUT2 + n + 4)
            residual(6, 5)
            norm_rows(7, h, 6, 0, 7)
            norm_lo(7, 0)
            F2 = 2 * P_FF2

            def gate_units(fu, stride=0, i=0):
                for j in range(2):
                    lo(fu + j + 4, stride, i)

            def hid2_mul(fu, stride=0, i=0, k=0):
                for j in range(2):
                    n = i * (stride // 3) + 2 * k + j + 1
                    dve.wait_ge(swi_a, n)
                    dve.wait_ge(unit_done, i * stride + (fu + j + 1))
                    if k:
                        dve.wait_ge(swi_lo, n - 2)
                    TT(hid2[:, j, :], gate_s[:, j, :], (ma, mb)[j][:, 0:S], ALU.mult).then_inc(swi_m, 1)
                    lo(fu + j + 4, stride, i)
                for j in range(2):
                    n = i * (stride // 3) + 2 * k + j + 1
                    dve.wait_ge(swi_hi, n)
                    TT(hid2_l[:, j, :], hid2[:, j, :], hid2_h[:, j, :].bitcast(F32), ALU.subtract).then_inc(swi_lo, 1)

            gate_units(F2)
            hid2_mul(F2 + 2)
            for i in rounds(dve, 4):
                for n in range(2):
                    gate_units(F2 + 4 + 6 * n, 12, i)
                    acc_units(F2 + 6 + 6 * n, 12, i)
                    hid2_mul(F2 + 8 + 6 * n, 12, i, n + 1)
            for n in range(2):
                gate_units(F2 + 52 + 6 * n)
                acc_units(F2 + 54 + 6 * n)
                hid2_mul(F2 + 56 + 6 * n, 0, 0, n + 9)
            acc_units(F2 + 64)
            residual(8, 7)
            dve.wait_ge(ut_hi, 10)
            TT(xTl[:, 0:2, 0:S].rearrange("p k (t n) -> p t k n", t=2), ma[:, :].rearrange("p (t k n) -> p t k n", t=2, k=2),
               xTh[:, 0:2, 0:S].rearrange("p k (t n) -> p t k n", t=2).bitcast(F32), ALU.subtract).then_inc(ut_lo, 1)
            for n in range(2):
                lo(2 * P_PLE + n + 4)
            dve.wait_ge(stat, 9)
            link(dve.reciprocal(st[:, 4:6], st[:, 4:6]))
            dve.wait_ge(gain_loaded[0], 16 * 5)
            for t in range(NT):
                STT(e_row[:, t, :], acc[:, 2 * t:2 * t + 2, :].rearrange("p b n -> p (b n)"), st[:, 4 + t:5 + t], gain[:, 0, :],
                    ALU.mult, ALU.mult).then_inc(e_out, 1)
            norm_lo(10, 0)
            for n in range(8):
                lo(2 * P_PGATE + n + 4)
            for t in range(NT):
                dve.wait_ge(fin_sig, t + 1)
                dve.wait_ge(e_out, t + 1)
                link(TT(u[:, t, :], u[:, t, :], e_row[:, t, :], ALU.mult))
                TT(u[:, t, :], u[:, t, :], h[:, t, :], ALU.add).then_inc(fin_out, 1)

        @block.tensor
        def _(pe):
            mm = pe.matmul

            def unit_ready(pu, stride=0, i=0):
                pe.wait_ge(w_lo, i * stride + (pu + 1))

            def bank_ready(j, pu, stride=0, i=0):
                n = along((EMPTIED0, EMPTIED1)[j], pu, stride, i)
                if not isinstance(n, int) or n > 0:
                    pe.wait_ge(emptied[j], n)

            def three(out, wh_, wl_, xh, xl, first, last):
                mm(out, wh_, xh, start=first, stop=False)
                mm(out, wh_, xl, start=False, stop=False)
                return mm(out, wl_, xh, start=False, stop=last)

            def three_tok(out, xh, xl, wh_, wl_, first, last, group=True):
                mm(out, xh, wh_, start=first, stop=False, skip_group_check=not group)
                mm(out, xh, wl_, start=False, stop=False, skip_group_check=not group)
                return mm(out, xl, wh_, start=False, stop=last, skip_group_check=not group)

            def fm_steps(pu, xh, xl, off, n, col=0, stride=0, i=0):
                unit_ready(pu, stride, i)
                bank_ready(pu % 2, pu, stride, i)
                a, b = (split_view(w, pu % UNITS, "cols") for w in (wh, wl))
                for k in range(KC):
                    last = three(fm[:, pu % 2, col:col + n], a[:, k, :], b[:, k, :], xh[:, k, off:off + n], xl[:, k, off:off + n],
                                 k == 0, k == KC - 1)
                    if k == KC - 1:
                        last.then_inc(unit_done, 1)
                    yield

            def tok_steps(pu, off, stride=0, i=0):
                unit_ready(pu, stride, i)
                j = pu % 2
                if j == 0:
                    bank_ready(0, pu, stride, i)
                    bank_ready(1, pu, stride, i)
                a, b = (w[:, pu % UNITS, :].rearrange("p (k n) -> p k n", k=4) for w in (wh, wl))
                for kk in range(4):
                    for t in range(NT):
                        k = 4 * j + kk
                        last = three_tok(fm[:, t, 0:S], xTh[:, k, off + t * P:off + (t + 1) * P], xTl[:, k, off + t * P:off + (t + 1) * P],
                                         a[:, kk, :], b[:, kk, :], k == 0, k == KC - 1)
                        if kk == 3 and t == NT - 1:
                            last.then_inc(unit_done, 1)
                        yield

            def run(steps):
                for _ in steps:
                    pass

            def acc_unit(pu, xh, xl, first, last_, stride=0, i=0):
                unit_ready(pu, stride, i)
                a, b = wh[:, pu % UNITS, :], wl[:, pu % UNITS, :]
                for t in range(NT):
                    for half in range(2):
                        last = three_tok(acc[:, 2 * t + half, :], xh[:, t * P:(t + 1) * P], xl[:, t * P:(t + 1) * P],
                                         a[:, half * 512:(half + 1) * 512], b[:, half * 512:(half + 1) * 512], first, last_, group=False)
                last.then_inc(unit_done, 1)

            def transposes(base, u_base, rows_):
                for t in range(NT):
                    pe.wait_ge(u_ready, u_base + t + 1)
                    for k in range(KC):
                        last = pe.transpose(acc[:, 2 * t + k // 4, (k % 4) * P:(k % 4 + 1) * P], rows_[:, t, k * P:(k + 1) * P], ident)
                    last.then_inc(ut_ps, 1)

            pe.wait_ge(cst_loaded, 16)
            pe.wait_ge(u_ready, 1)
            for k in range(KC):
                last = pe.transpose(ma[:, k * META:(k + 1) * META], meta[0:META, k * P:(k + 1) * P], ident[0:META, 0:META])
            last.then_inc(ut_ps, 1)
            transposes(1, 1, u)
            pe.wait_ge(ut_lo, 3)
            run(fm_steps(0, xTh, xTl, 0, T1))
            unit_ready(1)
            a, b = (split_view(w, 1, "cols") for w in (wh, wl))
            for t, (off, n) in enumerate(((META, P), (META + P, P), (0, META))):
                for k in range(KC):
                    last = three_tok(ma[0:n, t * P:(t + 1) * P], xTh[:, k, off:off + n], xTl[:, k, off:off + n], a[:, k, :], b[:, k, :],
                                     k == 0, k == KC - 1)
            last.then_inc(unit_done, 1)
            for m in range(LT):
                run(fm_steps(2 + m, xTh, xTl, 0, T1))
            for m in range(2):
                run(fm_steps(6 + m, xTh, xTl, META, S))
            pe.wait_ge(small3, 64)
            pe.wait_ge(v1_out, 1)
            for m in range(LT):
                pe.wait_ge(xc_ready, m // 2 + 1)
                if m >= 2:
                    pe.wait_ge(r_act, m - 1)
                mm(acc[:, m, 0:T1], wa_bd[:, m, :], xc[:, m, :], start=True, stop=True)
                mm((ma, mb)[m % 2][:, 0:T1], wx_bd[:, m, :], xc[:, m, :], start=True, stop=True).then_inc(r_ps, 1)
            for m in range(4):
                run(fm_steps(8 + m, xTh, xTl, META, S))
            for m in range(2):
                run(fm_steps(12 + m, xTh, xTl, META, S))
            pe.wait_ge(r_act, LT)
            pe.wait_ge(emptied[0], EMPTIED0[12])
            pe.wait_ge(emptied[1], EMPTIED1[12])
            for b in range(2):
                nk, k0 = ((P + META, 0), (2 * P, META))[b]
                if b:
                    pe.wait_ge(p1T_out, 2 * b)
                for hh in range(QH):
                    at_ = (hh % 2) * 4 + hh // 2
                    part = slice(64 * (hh % 2), 64 * (hh % 2) + 64)
                    last = mm(acc[:, at_ // 2, (at_ % 2) * 256:(at_ % 2) * 256 + nk], qT1[part, hh // 2, b * P:(b + 1) * P],
                              kT1[part, hh // 4, k0:k0 + nk], start=True, stop=True)
                last.then_inc(s1_ps, 1)
                chunks = (((0, META, 2), (META, P, 0)), ((0, P, 0), (P, P, 1)))[b]
                pe.wait_ge(s1_exp, QH * (b + 1))
                for hh in range(QH):
                    for c, (at, n, _) in enumerate(chunks):
                        last = pe.transpose(acc[0:n, hh // 2, (hh % 2) * 256 + c * P:(hh % 2) * 256 + c * P + P], p1[:, hh, at:at + n], ident)
                    if hh % 4 == 3:
                        last.then_inc(p1T_ps, 1)
                pe.wait_ge(p1T_out, 2 * b + 2)
                if b:
                    pe.wait_ge(o1_out, b)
                for hh in range(QH):
                    at_ = (hh % 2) * 4 + hh // 2
                    kv = slice(64 * (hh // 4), 64 * (hh // 4) + 64)
                    for c, (at, n, vt) in enumerate(chunks):
                        last = mm(ma[:, hh * HD1:(hh + 1) * HD1], pT1[0:n, at_, c, :], v1[0:n, vt, kv], start=c == 0, stop=c == 1)
                last.then_inc(o1_ps, 1)
                pe.wait_ge(o1_out, b + 1)
                if b:
                    pe.wait_ge(o1T_lo, b)
                for k in range(4):
                    last = pe.transpose(mb[:, k * P:(k + 1) * P], o1[:, k * P:(k + 1) * P], ident)
                last.then_inc(o1T_ps, 1)
            pe.wait_ge(rec_lo, 1)
            pe.wait_ge(o1T_lo, 2)
            for n in range(8):
                k = (4 + n) % 8
                acc_unit(2 * P_OUT1 + n, yTh[:, k, :], yTl[:, k, :], n == 0, n == 7)
            transposes(3, 3, u)
            pe.wait_ge(ut_lo, 5)

            F = 2 * P_FF1

            def ffn1_up(fu, stride=0, i=0):
                for j in range(2):
                    run(fm_steps(fu + j, xTh, xTl, 0, S, stride=stride, i=i))

            def ffn1_down(fu, par, n0, stride=0, i=0, last_=False):
                pe.wait_ge(hid_lo, i * (stride // 2) + 2 * n0 + 2)
                for j in range(2):
                    acc_unit(fu + j, hid_h[:, par, j, :], hid_l[:, par, j, :], False, last_ and j == 1, stride, i)

            def open_acc():
                for q in range(4):
                    mm(acc[:, q, :], zero_r[:, :], junk0, start=True, stop=False, skip_group_check=True)

            junk0 = cst[:, 0:512]
            open_acc()
            ffn1_up(F)
            for i in rounds(pe, 7):
                ffn1_up(F + 2, 8, i)
                ffn1_down(F + 4, 0, 0, 8, i)
                ffn1_up(F + 6, 8, i)
                ffn1_down(F + 8, 1, 1, 8, i)
            ffn1_up(F + 58)
            ffn1_down(F + 60, 0, 14)
            ffn1_down(F + 62, 1, 15, last_=True)
            transposes(5, 5, u)
            pe.wait_ge(ut_lo, 7)
            pe.wait_ge(ab_lo, 1)
            for t in range(NT):
                for k in range(KC):
                    last = three_tok(ma[:, t * 16:(t + 1) * 16], xTh[:, k, t * P:(t + 1) * P], xTl[:, k, t * P:(t + 1) * P],
                                     ab_h[:, k, :], ab_l[:, k, :], k == 0, k == KC - 1)
            last.then_inc(ab_ps, 1)
            M, G = 2 * P_MOBA, 2 * P_GDN

            def pair_steps(kinds, fu, stride, i):
                for c in range(8):
                    if kinds[c] == "t":
                        yield from tok_steps(fu + c, 0, stride, i)
                    else:
                        yield from fm_steps(fu + c, xTh, xTl, 0, S, stride=stride, i=i)

            run(pair_steps("ffffff" + "tt", M, 0, 0))
            pe.wait_ge(g_ready, 1)
            for c in range(2):
                mm(mb[:, c * 8:(c + 1) * 8], tri, g_all[:, 5, c, :], start=True, stop=True)
            for c in range(2):
                last = mm(mb[:, 16 + c * 8:16 + (c + 1) * 8], ones[:, :], g_all[:, 5, c, :], start=True, stop=True)
            last.then_inc(gc_ps, 1)

            def moba_stage(s, a):
                if s == 1:
                    pe.wait_ge(rope_out, a + 1)
                    for j in range(2):
                        mm(acc[:, j, 0:256], qr[:, j, P:2 * P], qr[:, 2 + j, :], start=True, stop=True)
                        last = mm(acc[:, j, 256:384], qr[:, j, 0:P], qr[:, 2 + j, 0:P], start=True, stop=True)
                    last.then_inc(s2_ps, 1)
                if s == 3:
                    pe.wait_ge(s2_p, a + 1)
                    for j in range(2):
                        for c in range(3):
                            last = pe.transpose(acc[:, 2 + j, c * P:(c + 1) * P], p2[:, j, c * P:(c + 1) * P], ident)
                    last.then_inc(p2T_ps, 1)
                if s == 4:
                    pe.wait_ge(p2T_a, a + 1)
                    pe.wait_ge(p2T_v, a + 1)
                    for j in range(2):
                        hd = slice(j * P, (j + 1) * P)
                        mm(ma[:, j * 256:j * 256 + P], va[:, 0, hd], pT2[:, j, 256:384], start=True, stop=True)
                        mm(ma[:, j * 256 + P:(j + 1) * 256], va[:, 0, hd], pT2[:, j, 0:P], start=True, stop=False)
                        last = mm(ma[:, j * 256 + P:(j + 1) * 256], va[:, 1, hd], pT2[:, j, P:2 * P], start=False, stop=True)
                    last.then_inc(o2_ps, 1)

            def gdn_stage(s, a):
                if s == 1:
                    pe.wait_ge(sq_out, a + 1)
                    for q in range(2):
                        last = mm(acc[:, q, :], ones[:, :], sq[:, q * 512:(q + 1) * 512], start=True, stop=True)
                    last.then_inc(ssq_ps, 1)
                if s == 2:
                    pe.wait_ge(gb_out, a + 1)
                    for pr in range(4):
                        last = mm(acc[:, 2, pr * P:(pr + 1) * P], gb[:, pr, :], tri, start=True, stop=True)
                    last.then_inc(gcb_ps, 1)
                    for pr in range(4):
                        c, j = pr // 2, pr % 2
                        last = pe.transpose(acc[:, 3, pr * P:(pr + 1) * P], cv[:, 4 + j, c * P:(c + 1) * P], ident)
                    last.then_inc(vT_ps, 1)
                if s == 3:
                    pe.wait_ge(qkn_out, a + 1)
                    for pr in range(4):
                        c, j = pr // 2, pr % 2
                        last = pe.transpose(acc[:, 0, pr * P:(pr + 1) * P], cv[:, 2 + j, c * P:(c + 1) * P], ident)
                    last.then_inc(kT_ps, 1)
                    pe.wait_ge(dt_out, a + 1)
                    for pr in range(4):
                        c, j = pr // 2, pr % 2
                        last = mm(acc[:, 1 + pr // 2, (pr % 2) * 256:(pr % 2) * 256 + 256], cv[:, 2 + j, c * P:(c + 1) * P],
                                  cv[:, j:j + 3:2, c * P:(c + 1) * P], start=True, stop=True)
                    last.then_inc(qkg_ps, 1)
                if s == 4:
                    pe.wait_ge(c0_out, a + 1)
                    pe.wait_ge(vb_out, a + 1)
                    for pr in range(4):
                        last = pe.transpose(acc[:, 3, pr * P:(pr + 1) * P], C_[:, 0, pr * P:(pr + 1) * P], ident)
                    last.then_inc(c0_ps, 1)
                if 5 <= s < 17 and s % 2 == 1:
                    lv = (s - 5) // 2 + 1
                    pe.wait_ge(lv_x, a * 7 + lv)
                    if lv == 1:
                        pe.wait_ge(kv_out, a + 1)
                    else:
                        pe.wait_ge(lv_c, a * 5 + (lv - 1))
                    for pr in range(4):
                        last = mm(acc[:, 0, pr * P:(pr + 1) * P], C_[:, lv % 2, pr * P:(pr + 1) * P], XT_[:, pr, :], start=True, stop=True)
                    last.then_inc(lv_p, 1)
                if 5 <= s < 17 and s % 2 == 0:
                    lv = (s - 5) // 2 + 1
                    pe.wait_ge(lv_pe, a * 6 + lv)
                    if lv < 6:
                        for pr in range(4):
                            mm(acc[:, 2, pr * P:(pr + 1) * P], P_[:, pr, :], X_[:, pr, :], start=True, stop=True)
                    for pr in range(4):
                        last = mm(acc[:, 1, pr * P:(pr + 1) * P], X_[:, pr, :], P_[:, pr, :], start=True, stop=True)
                    last.then_inc(lv_z, 1)
                if s == 17:
                    pe.wait_ge(lv_x, a * 7 + 7)
                    for j in range(2):
                        mm(acc[:, 3, j * P:(j + 1) * P], XT_[:, j, :], vb[:, j, :], start=True, stop=True)
                    for j in range(2):
                        last = mm(acc[:, 0, j * P:(j + 1) * P], kbe[:, j, :], XT_[:, 2 + j, :], start=True, stop=True)
                    last.then_inc(uw_ps, 1)
                if s == 18:
                    pe.wait_ge(u0_out, a + 1)
                    for j in range(2):
                        last = mm(acc[:, 1, j * P:(j + 1) * P], kdec[:, j, :], u0[:, j, :], start=True, stop=True)
                    last.then_inc(so_ps, 1)
                    for j in range(2):
                        mm(acc[:, 2, j * P:(j + 1) * P], attnT[:, j, :], u0[:, j, :], start=True, stop=True)
                if s == 19:
                    pe.wait_ge(S1_out, a + 1)
                    pe.wait_ge(nw_out, a + 1)
                    for j in range(2):
                        out = acc[:, 3, (2 + j) * P:(3 + j) * P]
                        mm(out, XT_[:, 2 + j, :], vb[:, 2 + j, :], start=True, stop=False)
                        last = mm(out, nwT[:, j, :], S1[:, j, :], start=False, stop=True)
                    last.then_inc(vn_ps, 1)
                if s == 20:
                    pe.wait_ge(vn_out, a + 1)
                    for j in range(2):
                        out = acc[:, 2, (2 + j) * P:(3 + j) * P]
                        mm(out, qeg[:, j, :], S1[:, j, :], start=True, stop=False)
                        last = mm(out, attnT[:, 2 + j, :], vn[:, j, :], start=False, stop=True)
                    last.then_inc(o_ps, 1)
                if s == 21:
                    pe.wait_ge(y_out, a + 1)
                    for pr in range(4):
                        last = pe.transpose(acc[:, 0, pr * P:(pr + 1) * P], y_[:, pr, :], ident)
                    last.then_inc(yT_ps, 1)

            def pair_round(weave, stage, kinds, fu, a):
                steps = pair_steps(kinds, fu, 8, a)
                for s, n in enumerate(weave):
                    stage(s, a)
                    for _ in range(n):
                        next(steps)

            for i in rounds(pe, 3):
                pair_round(MOBA_WEAVE, moba_stage, "fffffftt", M + 8, i)
            pair_round(MOBA_WEAVE, moba_stage, "fffffftt", M + 8, 3)
            for i in rounds(pe, 3):
                pair_round(GDN_WEAVE, gdn_stage, "fffffftt", G + 8, i)
            pair_round(GDN_WEAVE, gdn_stage, "ffffffff", G + 8, 3)
            pe.wait_ge(o2_lo, PAIRS)
            for m in range(KC):
                run(fm_steps(2 * P_PROJA + m, yTh, yTl, 0, S))
            pe.wait_ge(yb_lo, PAIRS)
            for m in range(KC):
                run(fm_steps(2 * P_PROJB + m, ybh, ybl, 0, S))
            for k in range(KC):
                pe.wait_ge(mg_lo, k // 4 + 1)
                acc_unit(2 * P_OUT2 + k, yTh[:, k, :], yTl[:, k, :], k == 0, k == KC - 1)
            transposes(7, 7, u)
            pe.wait_ge(ut_lo, 9)
            F2 = 2 * P_FF2

            def slice_up(fu, banks, read, need, stride=0, i=0):
                for j in range(2):
                    unit_ready(fu + j, stride, i)
                    if need is not None:
                        pe.wait_ge(read, i * (stride // 3) + need + j)
                    a, b = (split_view(w, (fu + j) % UNITS, "cols") for w in (wh, wl))
                    for k in range(KC):
                        last = three(banks[j], a[:, k, :], b[:, k, :], xTh[:, k, 0:S], xTl[:, k, 0:S], k == 0, k == KC - 1)
                    last.then_inc(unit_done, 1)

            def ffn2_down(fu, k, stride=0, i=0, last_=False):
                pe.wait_ge(swi_lo, i * (stride // 3) + 2 * k + 2)
                for j in range(2):
                    acc_unit(fu + j, hid2_h[:, j, :], hid2_l[:, j, :], False, last_ and j == 1, stride, i)

            pe.wait_ge(emptied[0], EMPTIED0[F2])
            pe.wait_ge(emptied[1], EMPTIED1[F2])
            open_acc()
            gates, ups = (fm[:, 0, 0:S], fm[:, 1, 0:S]), (ma[:, 0:S], mb[:, 0:S])
            slice_up(F2, gates, swi_a, None)
            slice_up(F2 + 2, ups, swi_m, None)
            for i in rounds(pe, 5):
                for n in range(2):
                    slice_up(F2 + 4 + 6 * n, gates, swi_a, 2 * n + 1, 12, i)
                    ffn2_down(F2 + 6 + 6 * n, n, 12, i)
                    slice_up(F2 + 8 + 6 * n, ups, swi_m, 2 * n + 1, 12, i)
            ffn2_down(F2 + 64, 10, last_=True)
            pe.wait_ge(p_loaded, 16)
            for t in range(NT):
                for k in range(2):
                    last = pe.transpose(ma[:, (2 * t + k) * P:(2 * t + k + 1) * P], p_in[:, t, k * P:(k + 1) * P], ident)
            last.then_inc(ut_ps, 1)
            pe.wait_ge(ut_lo, 10)
            pe.wait_ge(h_ready, 8)
            for k in range(2):
                acc_unit(2 * P_PLE + k, xTh[:, k, 0:S], xTl[:, k, 0:S], k == 0, k == 1)
            pe.wait_ge(e_out, NT)
            for t in range(NT):
                for k in range(KC):
                    last = pe.transpose(acc[:, 2 * t + k // 4, (k % 4) * P:(k % 4 + 1) * P], h[:, t, k * P:(k + 1) * P], ident)
                last.then_inc(ut_ps, 1)
            pe.wait_ge(ut_lo, 12)
            for k in range(KC):
                acc_unit(2 * P_PGATE + k, xTh[:, k, 0:S], xTl[:, k, 0:S], k == 0, k == KC - 1)


_INS = ["x", "meta_tokens", "g_pre_mix", "w_in", "conv_w", "conv_b", "w_a", "b_a", "w_x", "b_x", "lru_lambda",
        "attn_sinks", "w_out", "g_post_mix", "g_pre_ffn", "w_ff1", "w_ff2", "g_post_ffn", "p_2", "ln_pre_mix_2",
        "w_in_2", "conv_w_2", "a_log_2", "dt_bias_2", "gdn_norm_2", "w_proj_a_2", "w_proj_b_2", "w_out_2",
        "ln_post_mix_2", "ln_pre_ffn_2", "w_ffn_gate_2", "w_ffn_up_2", "w_ffn_down_2", "ln_post_ffn_2", "w_ple_2",
        "ln_ple_2", "w_ple_gate_2"]


def kernel(**inputs):
    import concourse.bacc as _bacc
    from concourse.bass_utils import run_bass_kernel_spmd as _run

    nc = _bacc.Bacc("TRN2", target_bir_lowering=False, num_devices=1)
    arrays, aps = {}, {}
    for name in _INS:
        a = np.ascontiguousarray(inputs[name])
        arrays[f"in_{name}_dram"] = a
        aps[name] = nc.dram_tensor(f"in_{name}_dram", a.shape, mybir.dt.from_np(a.dtype), kind="ExternalInput").ap()
    table = constant_table()
    arrays["constants_dram"] = table
    aps["cst"] = nc.dram_tensor("constants_dram", table.shape, F32, kind="ExternalInput").ap()
    aps["out"] = nc.dram_tensor("out_0_dram", (1, S, D), F32, kind="ExternalOutput").ap()
    build(nc, aps)
    r = _run(nc, [arrays], core_ids=[0])
    return r.results[0]["out_0_dram"]
```

```python
from contextlib import ExitStack

import numpy as np

import concourse.bass as bass
from concourse import mybir

F32 = mybir.dt.float32
F32R = mybir.dt.float32r
ALU = mybir.AluOpType
ACT = mybir.ActivationFunctionType
AX = mybir.AxisListType.X

P = 128
D = 1024
KC = D // P
S = 256
META = 16
T1 = S + META
NT = S // P
EPS = 1e-6
NEG = -1e30
QH, KVH, HD1 = 8, 2, 64
WINDOW = 128
LRU = 512
LT = LRU // P
FF1_TILES = 16
HEADS2 = 8
PAIRS = HEADS2 // 2
LEVELS = 7
FF2_TILES = 11
PLE = 256
REGION = 16128
SC1 = HD1 ** -0.5
SC2 = P ** -0.5
IN2_Q, IN2_K, IN2_V, IN2_CONV, IN2_Z, IN2_B, IN2_GA, IN2_GB = (
    0, 1024, 2048, 3072, 6144, 7168, 7184, 8208)

C_IDENT, C_TRI, C_MUP, C_MLOW, C_LEV, C_MOBA, C_WIN0, C_WIN1, C_COS, C_SIN, C_END = (
    0, 128, 256, 384, 512, 1408, 1792, 1936, 2192, 2448, 2704)


def constant_table():
    c = np.zeros((P, C_END), np.float32)
    r, k = np.arange(P)[:, None], np.arange(P)[None, :]
    c[:, C_IDENT:C_TRI] = r == k
    c[:, C_TRI:C_MUP] = r <= k
    c[:, C_MUP:C_MLOW] = np.where(r <= k, 0.0, NEG)
    c[:, C_MLOW:C_LEV] = np.where(k < r, 0.0, NEG)
    for n in range(LEVELS):
        b = 1 << n
        low = (r // (2 * b) == k // (2 * b)) & (r % (2 * b) >= b) & (k % (2 * b) < b)
        at = C_LEV + n * P
        if n:
            c[:, at:at + P] = low.T
        else:
            c[:, at:at + P // 2] = low[:, 0::2]
    diag = np.where(k <= r, 0.0, NEG)
    c[:, C_MOBA + P:C_MOBA + 2 * P] = diag
    c[:, C_MOBA + 2 * P:C_MOBA + 3 * P] = diag
    k0 = np.arange(P + META)[None, :]
    gap = META + r - k0
    c[:, C_WIN0:C_WIN1] = np.where((gap >= 0) & (gap < WINDOW), 0.0, NEG)
    gap = P + r - np.arange(2 * P)[None, :]
    c[:, C_WIN1:C_COS] = np.where((gap >= 0) & (gap < WINDOW), 0.0, NEG)
    half = P // 2
    inv = (1.0 / (np.float32(10000.0) ** (np.arange(0, P, 2, dtype=np.float32) / np.float32(P)))).astype(np.float32)
    ang = (np.arange(S, dtype=np.float32)[None, :] * inv[:, None]).astype(np.float32)
    c[:half, C_COS:C_SIN] = c[half:, C_COS:C_SIN] = np.cos(ang)
    c[:half, C_SIN:C_END] = -np.sin(ang)
    c[half:, C_SIN:C_END] = np.sin(ang)
    return c


RING = 4
UNITS = 4
(P_KV, P_XR, P_YR0, P_Q, P_YR1, P_OUT1, P_FF1, P_MOBA, P_GDN, P_GATEB, P_PROJA, P_PROJB, P_OUT2, P_FF2, P_PLE,
 P_PGATE, P_ALL) = (0, 1, 3, 4, 6, 7, 11, 43, 59, 75, 79, 83, 87, 91, 124, 125, 129)


def panel_plan():
    plan = [("cols", "kv")] + [("cols", "fm")] * 6 + [("rows", "acc")] * 4
    plan += [("cols", "fm")] + [("cols", "fm"), ("rows", "acc")] * 15 + [("rows", "acc")]
    plan += ([("cols", "fm")] * 3 + [("rows", "tok")]) * PAIRS
    plan += ([("cols", "fm")] * 3 + [("rows", "tok")]) * PAIRS
    plan += [("cols", "fm")] * 12 + [("rows", "acc")] * 4
    plan += [("cols", "fm")] * 2 + [("cols", "fm"), ("rows", "acc"), ("cols", "fm")] * 10 + [("rows", "acc")]
    plan += [("rows", "acc")] * 5
    assert len(plan) == P_ALL
    return plan


PLAN = panel_plan()
SLOT = [p % RING if p < P_FF2 else (p - P_FF2) % 3 if p < P_PLE else (p - P_PLE) % RING for p in range(P_ALL)]
LOADS = [16 * sum(SLOT[q] == SLOT[p] for q in range(p + 1)) for p in range(P_ALL)]
REUSE = [max((q for q in range(p) if SLOT[q] == SLOT[p]), default=-1) for p in range(P_ALL)]


def bank_counts():
    n, before = [0, 0], []
    for layout, to in PLAN:
        for j in range(2):
            before.append(tuple(n))
            if to == "fm":
                n[j] += 1
            elif to == "kv" and j == 0:
                n[0] += 1
            elif to == "tok" and j == 1:
                n[0] += 1
                n[1] += 1
    return before


EMPTIED = bank_counts()
AFTER = [[EMPTIED[min(n + 1, 2 * P_ALL - 1)][b] for n in range(2 * P_ALL)] for b in range(2)]
EMPTIED0 = [e[0] for e in EMPTIED] + [0] * 64
EMPTIED1 = [e[1] for e in EMPTIED] + [0] * 64


def along(table, at, stride, i):
    if isinstance(i, int):
        return table[at + stride * i]
    step = table[at + stride] - table[at]
    return i * step + table[at]


class Chain:

    def __init__(self, eng, sem):
        self.eng, self.sem, self.n, self.links = eng, sem, 0, 0

    def mark(self, ins):
        ins.then_inc(self.sem, 1)
        self.n, self.links = self.n + 1, self.links + 1

    def wait(self):
        self.eng.wait_ge(self.sem, self.n)

    def link(self, ins):
        self.mark(ins)
        self.wait()


def rounds(eng, n, chain=None, per=0):
    base, links = (chain.n, chain.links) if chain else (0, 0)
    with eng.Fori(0, n) as i:
        if chain:
            chain.n = i * per + base
        yield i
    if chain:
        assert chain.links - links == per, chain.links - links
        chain.n = base + n * per


MOBA_WEAVE = [16, 8, 16, 8, 16]
GDN_WEAVE = [8, 6, 4, 6, 4] + [1] * 12 + [4, 3, 3, 14]
assert sum(MOBA_WEAVE) == 64 and sum(GDN_WEAVE) == 64


def finished(weave):
    done, out = 0, []
    for n in weave:
        out.append(range(done // 8, (done + n) // 8))
        done += n
    return out


def build(nc, A):
    ctx = ExitStack()
    with ctx:
        def sb(name, shape, dt=F32):
            return ctx.enter_context(nc.sbuf_tensor(name, shape, dt))

        def sem(name):
            return ctx.enter_context(nc.semaphore(name))

        acc = ctx.enter_context(nc.psum_tensor("acc", [P, 4, 512], F32))
        fm = ctx.enter_context(nc.psum_tensor("fm", [P, 2, 512], F32))
        ma = ctx.enter_context(nc.psum_tensor("ma", [P, 512], F32))
        mb = ctx.enter_context(nc.psum_tensor("mb", [P, 512], F32))

        w_raw = sb("w_raw", [P, RING, 2048])
        wh = sb("wh", [P, UNITS, 1024], F32R)
        wl = sb("wl", [P, UNITS, 1024], F32R)
        h = sb("h", [P, NT, D])
        xTh = sb("xTh", [P, KC, T1], F32R)
        xTl = sb("xTl", [P, KC, T1], F32R)
        yTh = sb("yTh", [P, KC, S], F32R)
        yTl = sb("yTl", [P, KC, S], F32R)
        y2 = sb("y2", [P, 2 * KC * S], F32R)
        gain = sb("gain", [P, 2, D])
        cst = sb("cst", [P, C_END])
        ones = sb("ones", [P, P])
        zero_r = sb("zero_r", [P, P])
        eps = sb("eps", [P, 1])
        st = sb("st", [P, 32])
        R = sb("R", [P, REGION])

        def carve(state, *shape):
            n = int(np.prod(shape))
            a = R[:, state[0]:state[0] + n]
            state[0] += n
            assert state[0] <= REGION, state
            if len(shape) == 2:
                return a.rearrange("p (a b) -> p a b", a=shape[0])
            if len(shape) == 3:
                return a.rearrange("p (a b c) -> p a b c", a=shape[0], b=shape[1])
            return a

        c1 = [0]
        u = carve(c1, NT, D)
        meta = carve(c1, D)
        xr_pad = carve(c1, LT, T1 + 3)
        xc = carve(c1, LT, T1)
        r_g = carve(c1, LT, T1)
        i_g = carve(c1, LT, T1)
        th_ = carve(c1, LT, T1)
        a_ = carve(c1, LT, T1)
        a2 = carve(c1, LT, T1)
        gy = carve(c1, LT, S)
        qT1 = carve(c1, 4, S)
        kT1 = carve(c1, KVH, T1)
        v1 = carve(c1, 3, P)
        o1 = carve(c1, QH * HD1)
        wa_bd = carve(c1, LT, P)
        wx_bd = carve(c1, LT, P)
        cwb = carve(c1, LT, 8)
        lam_t = carve(c1, 8, LT)
        sink = carve(c1, QH)
        cp = [NT * D + D]
        p1 = carve(cp, QH, S)
        pT1 = carve(cp, QH, 2, P)
        sm1 = carve(cp, QH, S)
        cf = [NT * D + D]
        hid_t = carve(cf, 2, S)
        hid_q = carve(cf, 2, S)
        hid_h = y2[:, 0:4 * S].rearrange("p (a b c) -> p a b c", a=2, b=2)
        hid_l = y2[:, 4 * S:8 * S].rearrange("p (a b c) -> p a b c", a=2, b=2)
        c2 = [NT * D]
        ybh = y2[:, 0:KC * S].rearrange("p (k n) -> p k n", k=KC)
        ybl = y2[:, KC * S:2 * KC * S].rearrange("p (k n) -> p k n", k=KC)
        ga = carve(c2, KC, S)
        g_all = carve(c2, 7, 2, HEADS2)
        cw_all = carve(c2, 4, 24)
        ab_w = carve(c2, KC, 16)
        ab_h = y2[:, 0:KC * 16].rearrange("p (k n) -> p k n", k=KC)
        ab_l = y2[:, KC * 16:2 * KC * 16].rearrange("p (k n) -> p k n", k=KC)
        ab = carve(c2, 2, 16)
        dt_row = carve(c2, 2, HEADS2)
        tmp16 = carve(c2, 8, 16)
        gnorm = carve(c2, P)
        sc = carve(c2, 6, 2, 2)
        cw = carve(c2, 4, 6)
        raw = carve(c2, 6, S + 3)
        zr = carve(c2, NT, S)
        cvn = carve(c2, 6, S)
        cvt = gain[:, 0, 0:2 * S].rearrange("p (m n) -> p m n", m=2)
        c3 = [c2[0]]
        qk = carve(c3, 4, S)
        qr = carve(c3, 4, S)
        rot = carve(c3, 4, S)
        va = carve(c3, NT, S)
        sm2 = carve(c3, 2, 384)
        p2 = carve(c3, 2, 384)
        pT2 = carve(c3, 2, 384)
        c4 = [c2[0]]
        cv = carve(c4, 6, S)
        c5 = [0]
        rk = carve(c5, 4 * S)
        sq = rk
        kbe = carve(c5, 2, P)
        kdec = carve(c5, 2, P)
        vb = carve(c5, 4, P)
        dt_ = carve(c4, 4, P)
        dl_ = carve(c4, 4, P)
        eg = carve(c4, 2, P)
        attnT = carve(c4, 4, P)
        A_ = carve(c4, 4, P)
        gb = carve(c4, 4, P)
        X_ = carve(c4, 4, P)
        XT_ = carve(c4, 4, P)
        PM_ = carve(c4, 4, P)
        u0 = carve(c4, 2, P)
        nwT = carve(c4, 2, P)
        S1 = carve(c4, 2, P)
        vn = carve(c4, 2, P)
        qeg = carve(c4, 2, P)
        y_ = gb
        sz = carve(c4, NT, S)
        c6 = [c2[0]]
        gate_s = carve(c6, 2, S)
        hid2 = carve(c6, 2, S)
        hid2_h = y2[:, 0:2 * S].rearrange("p (j n) -> p j n", j=2)
        hid2_l = y2[:, 2 * S:4 * S].rearrange("p (j n) -> p j n", j=2)
        gb_s = gain[:, :, :].rearrange("p a (m n) -> p (a m) n", n=S)
        p_in = carve(c6, NT, PLE)
        e_row = ga.rearrange("p a b -> p (a b)").rearrange("p (t n) -> p t n", t=NT)
        junk = sb("junk", [P, D])
        o_s = junk[:, 0:512].rearrange("p (r n) -> p r n", r=4)

        ident = cst[:, C_IDENT:C_TRI]
        tri = cst[:, C_TRI:C_MUP]

        w_loaded = [sem(f"w_loaded{n}") for n in range(RING)]
        w_hi, w_lo, unit_done = sem("w_hi"), sem("w_lo"), sem("unit_done")
        emptied = [sem("fm0_emptied"), sem("fm1_emptied")]
        x_loaded, cst_loaded, small1, small2 = (sem(n) for n in ("x_loaded", "cst_loaded", "small1_loaded", "small2_loaded"))
        small3 = sem("block_diag_loaded")
        gain_loaded = [sem("gain0_loaded"), sem("gain1_loaded")]
        gain_used = sem("gain_used")
        filled = sem("pool_filled")
        act_chain, dve_chain, pool_chain = sem("act_chain"), sem("dve_chain"), sem("pool_chain")
        stat = sem("norm_root_ready")
        u_ready = sem("u_ready")
        ut_ps = sem("uT_in_psum")
        ut_hi, ut_lo = sem("uT_hi_ready"), sem("uT_lo_ready")
        h_ready = sem("h_ready")
        v1_out = sem("v1_ready")
        lam_e, sp_ready, xc_ready = sem("lam_exp_ready"), sem("softplus_ready"), sem("conv_ready")
        r_ps, r_act, tanh_out, a_out, m2_out, mult_out = (
            sem(n) for n in ("lru_gates_in_psum", "lru_gates_ready", "lru_tanh_ready", "lru_a_ready",
                             "lru_mult2_ready", "lru_mult_ready"))
        rec_out, rec_hi, rec_lo = sem("rec_ready"), sem("rec_hi_ready"), sem("rec_lo_ready")
        s1_ps, s1_max, s1_exp, p1T_ps, p1T_out, o1_ps, o1_out, o1T_ps, o1T_hi, o1T_lo = (
            sem(n) for n in ("attn1_scores", "attn1_max", "attn1_exp", "attn1_pT", "attn1_pT_ready", "attn1_o",
                             "attn1_o_ready", "attn1_oT", "attn1_oT_hi", "attn1_oT_lo"))
        s1_sink = sem("attn1_sink_exp")
        hid_a, hid_s, hid_hi, hid_lo = (sem(n) for n in ("hid_relu", "hid_square", "hid_hi", "hid_lo"))
        ab_hi, ab_ps, ab_out, ab_act, g_ready, gc_ps, gc_act, gc_ready = (
            sem(n) for n in ("ab_w_hi", "ab_in_psum", "ab_ready", "ab_act", "g_ready", "gc_in_psum", "gc_exp", "gc_ready"))
        ab_lo = sem("ab_w_lo")
        rot_out, rope_out, s2_ps, s2_max, s2_exp, s2_p, p2T_ps, p2T_a, p2T_v, o2_ps, o2_hi, o2_lo = (
            sem(n) for n in ("rope_halves", "rope_ready", "moba_scores", "moba_max", "moba_exp", "moba_p", "moba_pT",
                             "moba_pT0_ready", "moba_pT1_ready", "moba_o", "moba_o_hi", "moba_o_lo"))
        cv_out, silu_out, sq_out, ssq_ps, rk_out, qkn_out, gb_out, gcb_ps, t12_out, dt_out, dl_out = (
            sem(n) for n in ("gdn_conv", "gdn_silu", "gdn_squares", "gdn_square_sums", "gdn_inv_norms", "gdn_qk_ready",
                             "gdn_g_rows", "gdn_gc_rows", "gdn_exponents", "gdn_decay_up", "gdn_decay_low"))
        vT_ps, kT_ps, kk_ps, kq_ps, attn_out, qeg_out, kv_out, A_out, inv_start, x0_out, xt0_ps, xt0_out = (
            sem(n) for n in ("gdn_v_rows", "gdn_k_rows", "gdn_kk_products", "gdn_kq_products", "gdn_attn_ready", "gdn_q_scaled", "gdn_kv_scaled", "gdn_A_ready", "inv_identity_ready",
                             "inv_x0_ready", "inv_xt0_in_psum", "inv_xt0_ready"))
        lv_p, lv_pm, lv_z, lv_x, lv_xt = ([sem(f"{n}{g}") for g in range(2)] for n in (
            "inv_p_in_psum", "inv_p_ready", "inv_z_in_psum", "inv_x_ready", "inv_xt_ready"))
        vb_out, sz_out, os_out = sem("gdn_vb_ready"), sem("gdn_gate_ready"), sem("gdn_o_copied")
        uw_ps, u0_out, nw_out, so_ps, S1_out, vn_ps, vn_out, o_ps, og_out, y_out, yT_ps, yb_hi, yb_lo = (
            sem(n) for n in ("gdn_u_w", "gdn_u0", "gdn_nwT", "gdn_state_ps", "gdn_state", "gdn_vnew_ps", "gdn_vnew",
                             "gdn_o_ps", "gdn_o_root", "gdn_y", "gdn_yT_ps", "gdn_yT_hi", "gdn_yT_lo"))
        sig_a, sig_b, mg_out, mg_hi, mg_lo = (sem(n) for n in ("gate_a_sig", "gate_b_sig", "merged", "merged_hi", "merged_lo"))
        swi_a, swi_m, swi_hi, swi_lo = (sem(n) for n in ("ffn2_silu", "ffn2_hidden", "ffn2_hid_hi", "ffn2_hid_lo"))
        p_loaded, e_out = sem("ple_loaded"), sem("ple_rows_ready")
        fin_sig, fin_out, stored = sem("final_sigmoid"), sem("out_ready"), sem("out_stored")

        def raw_unit(slot, j, layout):
            if layout == "cols":
                return w_raw[:, slot, :].rearrange("p (k n) -> p k n", k=KC)[:, :, j * P:(j + 1) * P]
            return w_raw[:, slot, j * 1024:(j + 1) * 1024]

        def split_view(buf, ring, layout):
            if layout == "cols":
                return buf[:, ring, :].rearrange("p (k n) -> p k n", k=KC)
            return buf[:, ring, :]

        block = ctx.enter_context(nc.Block())

        @block.sync
        def _(sp):
            w_in, w_in2 = A["w_in"][0], A["w_in_2"][0]

            def cols(w, off, n, m):
                src = w[:, off:off + 256 * n].rearrange("(k p) (m n) -> m p k n", p=P, n=256)
                return src[bass.ds(m, 1)].rearrange("a p k n -> p (a k) n")

            def rows(w, m):
                src = w.rearrange("(m k p) n -> m p k n", k=2, p=P)
                return src[bass.ds(m, 1)].rearrange("a p k n -> p (a k) n")

            def tokcols(w, off, n, m):
                return cols(w, off, n, m)

            def load(p, src, stride=0, i=0):
                if isinstance(i, int):
                    last = REUSE[p + stride * i]
                    if last >= 0:
                        sp.wait_ge(w_lo, 2 * last + 2)
                else:
                    sp.wait_ge(w_lo, along([2 * q + 2 for q in REUSE], p, stride, i))
                k = 8 if src.shape[-1] == 256 else 2
                dst = w_raw[:, SLOT[p], :].rearrange("p (k n) -> p k n", k=k)
                sp.dma_start(dst, src).then_inc(w_loaded[SLOT[p]], 16)

            sp.dma_start(u[:, :, :], A["x"][0].rearrange("(t p) d -> p t d", p=P)).then_inc(x_loaded, 16)
            sp.dma_start(meta[0:META, :], A["meta_tokens"]).then_inc(x_loaded, 16)
            load(P_KV, cols(w_in, 512, 1, 0))
            for m in range(2):
                load(P_XR + m, cols(w_in, 768, 2, m))
            load(P_YR0, cols(w_in, 1280, 2, 0))
            for m in range(2):
                load(P_Q + m, cols(w_in, 0, 2, m))
            load(P_YR1, cols(w_in, 1280, 2, 1))
            for n, m in enumerate((2, 3, 0, 1)):
                load(P_OUT1 + n, rows(A["w_out"][0], m))
            w1, w2 = A["w_ff1"][0], A["w_ff2"][0]
            load(P_FF1, cols(w1, 0, 16, 0))
            for i in rounds(sp, 7):
                load(P_FF1 + 1, cols(w1, 0, 16, i * 2 + 1), 4, i)
                load(P_FF1 + 2, rows(w2, i * 2), 4, i)
                load(P_FF1 + 3, cols(w1, 0, 16, i * 2 + 2), 4, i)
                load(P_FF1 + 4, rows(w2, i * 2 + 1), 4, i)
            load(P_FF1 + 29, cols(w1, 0, 16, 15))
            load(P_FF1 + 30, rows(w2, 14))
            load(P_FF1 + 31, rows(w2, 15))
            for i in rounds(sp, PAIRS):
                for n, off in enumerate((IN2_Q, IN2_K, IN2_GA, IN2_V)):
                    load(P_MOBA + n, cols(w_in2, off, 4, i), 4, i)
            for i in rounds(sp, PAIRS):
                for n, off in enumerate((IN2_CONV, IN2_CONV + D, IN2_CONV + 2 * D, IN2_Z)):
                    load(P_GDN + n, cols(w_in2, off, 4, i), 4, i)
            for m in range(4):
                load(P_GATEB + m, cols(w_in2, IN2_GB, 4, m))
            for n, w in enumerate((A["w_proj_a_2"][0], A["w_proj_b_2"][0])):
                for m in range(4):
                    load(P_PROJA + 4 * n + m, cols(w, 0, 4, m))
            for m in range(4):
                load(P_OUT2 + m, rows(A["w_out_2"][0], m))
            wg, wu, wd = A["w_ffn_gate_2"][0], A["w_ffn_up_2"][0], A["w_ffn_down_2"][0]
            load(P_FF2, cols(wg, 0, 11, 0))
            load(P_FF2 + 1, cols(wu, 0, 11, 0))
            for i in rounds(sp, 5):
                for n in range(2):
                    load(P_FF2 + 2 + 3 * n, cols(wg, 0, 11, i * 2 + (n + 1)), 6, i)
                    load(P_FF2 + 3 + 3 * n, rows(wd, i * 2 + n), 6, i)
                    load(P_FF2 + 4 + 3 * n, cols(wu, 0, 11, i * 2 + (n + 1)), 6, i)
            load(P_FF2 + 32, rows(wd, 10))
            load(P_PLE, rows(A["w_ple_2"][0], 0))
            for m in range(4):
                load(P_PGATE + m, rows(A["w_ple_gate_2"][0], m))
            for t in range(NT):
                sp.wait_ge(fin_out, t + 1)
                sp.dma_start(A["out"][0].rearrange("(t p) d -> t p d", p=P)[t], u[:, t, :]).then_inc(stored, 16)
            sp.wait_ge(stored, 16 * NT)

        GAINS = ["g_pre_mix", "g_post_mix", "g_pre_ffn", "g_post_ffn", "ln_pre_mix_2", "ln_post_mix_2",
                 "ln_pre_ffn_2", "ln_post_ffn_2", "ln_ple_2"]

        @block.gpsimd
        def _(pool):
            pool.memset(eps[:, :], EPS).then_inc(filled, 1)
            pool.memset(ones[:, :], 1.0).then_inc(filled, 1)
            pool.memset(zero_r[:, :], 0.0).then_inc(filled, 1)
            pool.memset(xr_pad[:, :, 0:3], 0.0).then_inc(filled, 1)
            pool.memset(wa_bd[:, :, :], 0.0).then_inc(filled, 1)
            pool.memset(wx_bd[:, :, :], 0.0).then_inc(filled, 1)
            pool.dma_start(gain[:, 0, :], A[GAINS[0]][0].partition_broadcast(P)).then_inc(gain_loaded[0], 16)
            pool.dma_start(cst[:, :], A["cst"]).then_inc(cst_loaded, 16)
            pool.dma_start(gain[:, 1, :], A[GAINS[1]][0].partition_broadcast(P)).then_inc(gain_loaded[1], 16)
            with nc.allow_non_contiguous_dma(reason="per-channel vectors"):
                for tap in range(4):
                    pool.dma_start(cwb[:, :, tap], A["conv_w"][0, tap].rearrange("(m p) -> p m", p=P)).then_inc(small1, 16)
                for n, name in enumerate(("conv_b", "b_a", "b_x", "lru_lambda")):
                    pool.dma_start(cwb[:, :, 4 + n], A[name][0].rearrange("(m p) -> p m", p=P)).then_inc(small1, 16)
                for b in range(2):
                    sinks = A["attn_sinks"][0].rearrange("(m b) -> b m", b=2)[b].partition_broadcast(P)
                    pool.dma_start(sink[:, 4 * b:4 * b + 4], sinks).then_inc(small1, 16)
            pool.wait_ge(filled, 6)
            for dst, name in ((wa_bd, "w_a"), (wx_bd, "w_x")):
                src = A[name][0].rearrange("(m b) c d -> b c m d", b=2)
                for b in range(2):
                    pool.dma_start(dst[64 * b:64 * b + 64, :, 64 * b:64 * b + 64], src[b]).then_inc(small3, 16)
            def gain_free(n):
                if n % 2 == 0:
                    pool.wait_ge(u_ready, n + 1)
                else:
                    pool.wait_ge(gain_used, n // 2)

            for n in range(2, 5):
                gain_free(n)
                pool.dma_start(gain[:, n % 2, :], A[GAINS[n]][0].partition_broadcast(P)).then_inc(gain_loaded[n % 2], 16)
            pool.wait_ge(h_ready, 4)
            with nc.allow_non_contiguous_dma(reason="per-channel vectors"):
                for tap in range(4):
                    pool.dma_start(cw_all[:, tap, :], A["conv_w_2"][0, tap].rearrange("(m p) -> p m", p=P)).then_inc(small2, 16)
                pool.dma_start(ab_w, A["w_in_2"][0][:, IN2_B:IN2_B + 16].rearrange("(k p) n -> p k n", p=P)).then_inc(small2, 16)
            pool.dma_start(dt_row[:, 0, :], A["dt_bias_2"][0].partition_broadcast(P)).then_inc(small2, 16)
            pool.dma_start(dt_row[:, 1, :], A["a_log_2"][0].partition_broadcast(P)).then_inc(small2, 16)
            pool.dma_start(gnorm, A["gdn_norm_2"][0].partition_broadcast(P)).then_inc(small2, 16)
            pool.memset(raw[:, :, 0:3], 0.0).then_inc(filled, 1)
            chp = Chain(pool, pool_chain)
            pool.wait_ge(small2, 16 * 8)
            pool.wait_ge(filled, 7)

            def convolve(fu, stride, a, pair):
                if not (isinstance(pair, int) and pair == 0):
                    pool.wait_ge(cv_out, pair * 3)
                chp.link(pool.tensor_copy(cw.rearrange("p t (k j) -> p t k j", k=3),
                                          cw_all.rearrange("p t (k h) -> p t k h", k=3)[:, :, :, bass.ds(pair * 2, 2)]))
                for c in (1, 3, 5):
                    for b in range(2):
                        pool.wait_ge(emptied[b], along(AFTER[b], fu + c, stride, a))
                    if not (isinstance(pair, int) and pair == 0):
                        pool.wait_ge(silu_out, pair)
                    y = cvn[:, c - 1:c + 1, :]
                    for tap in range(4):
                        x = raw[:, c - 1:c + 1, tap:tap + S]
                        w = cw[:, tap, c - 1:c + 1].unsqueeze(2).to_broadcast([P, 2, S])
                        ins = pool.tensor_tensor(cvt if tap else y, x, w, ALU.mult)
                        if tap:
                            chp.link(ins)
                            ins = pool.tensor_tensor(y, y, cvt, ALU.add)
                        if tap < 3:
                            chp.link(ins)
                    ins.then_inc(cv_out, 1)

            convolve(2 * P_MOBA + 32, 8, 0, 0)
            for i in rounds(pool, 3, chp, 19):
                convolve(2 * P_GDN + 8, 8, i, i + 1)
            pool.wait_ge(mg_lo, 2)
            for n in range(5, 9):
                gain_free(n)
                pool.dma_start(gain[:, n % 2, :], A[GAINS[n]][0].partition_broadcast(P)).then_inc(gain_loaded[n % 2], 16)
                if n == 6:
                    pool.wait_ge(ut_lo, 9)
                    pool.dma_start(p_in, A["p_2"][0, 0].rearrange("(t p) n -> p t n", p=P)).then_inc(p_loaded, 16)

        @block.scalar
        def _(act):
            ch = Chain(act, act_chain)

            def hi(pu, stride=0, i=0):
                p, j = pu // 2, pu % 2
                if p >= P_ALL:
                    return
                layout = PLAN[p][0]
                if not isinstance(i, int):
                    assert stride % (2 * UNITS) == 0 or stride == 12
                    assert PLAN[(pu + stride) // 2] == PLAN[p]
                if isinstance(i, int):
                    pu, i, stride = pu + stride * i, 0, 0
                    p, layout = pu // 2, PLAN[pu // 2][0]
                if j == 0:
                    act.wait_ge(w_loaded[SLOT[p]], along(LOADS, p, stride // 2, i))
                if pu >= UNITS or not isinstance(i, int):
                    act.wait_ge(unit_done, i * stride + (pu - UNITS + 1))
                act.activation(split_view(wh, pu % UNITS, layout), raw_unit(SLOT[p], j, layout), ACT.Copy).then_inc(w_hi, 1)

            def unit_wait(pu, stride=0, i=0):
                act.wait_ge(unit_done, i * stride + (pu + 1))

            def root(n, cols, width=D):
                act.activation(st[:, 4:4 + cols], st[:, 0:cols], ACT.Sqrt, bias=eps[:, 0:1], scale=1.0 / width).then_inc(stat, 1)

            def norm(n, src, off):
                for t in range(NT):
                    act.wait_ge(h_ready, 2 * n + t + 1)
                    ch.link(act.activation(junk[:, :], src[:, t, :], ACT.Square, accum_out=st[:, t:t + 1]))
                root(n, NT)

            def acc_stat(last_unit):
                act.wait_ge(unit_done, last_unit + 1)
                for t in range(NT):
                    ch.link(act.activation(junk[:, :], acc[:, 2 * t:2 * t + 2, :].rearrange("p b n -> p (b n)"), ACT.Square,
                                           accum_out=st[:, t:t + 1]))
                root(0, NT)

            act.wait_ge(x_loaded, 32)
            act.wait_ge(filled, 4)
            for t in range(NT):
                ch.link(act.activation(junk[:, :], u[:, t, :], ACT.Square, accum_out=st[:, t:t + 1]))
            ch.link(act.activation(junk[0:META, :], meta[0:META, :], ACT.Square, accum_out=st[0:META, 2:3]))
            act.activation(st[:, 4:6], st[:, 0:2], ACT.Sqrt, bias=eps[:, 0:1], scale=1.0 / D)
            act.activation(st[0:META, 6:7], st[0:META, 2:3], ACT.Sqrt, bias=eps[0:META, 0:1], scale=1.0 / D).then_inc(stat, 1)
            act.wait_ge(small1, 16 * 10)
            ch.link(act.activation(lam_t[:, 0, :], cwb[:, :, 7], ACT.Abs))
            act.activation(lam_t[:, 1, :], lam_t[:, 0, :], ACT.Exp, scale=-1.0).then_inc(lam_e, 1)
            for n in range(4):
                hi(n)
            act.wait_ge(ut_ps, 1)
            act.activation(xTh[:, :, 0:META], ma[:, 0:KC * META].rearrange("p (k n) -> p k n", k=KC), ACT.Copy).then_inc(ut_hi, 1)
            for t in range(NT):
                act.wait_ge(ut_ps, t + 2)
                act.activation(xTh[:, :, META + t * P:META + (t + 1) * P],
                               acc[:, 2 * t:2 * t + 2, :].rearrange("p b (k n) -> p (b k) n", n=P), ACT.Copy).then_inc(ut_hi, 1)
            unit_wait(0)
            for v in range(KVH):
                for half in range(2):
                    ins = act.activation(kT1[64 * half:64 * half + 64, v, :], fm[64 * v:64 * v + 64, 0, 0:T1], ACT.Copy)
            ins.then_inc(emptied[0], 1)
            hi(4)
            unit_wait(1)
            act.activation(v1[:, 0:2, :], ma[:, 0:256].rearrange("p (a b) -> p a b", a=2), ACT.Copy)
            act.activation(v1[0:META, 2, :], ma[0:META, 256:384], ACT.Copy).then_inc(v1_out, 1)
            hi(5)
            act.wait_ge(filled, 4)
            for m in range(LT):
                unit_wait(2 + m)
                act.activation(xr_pad[:, m, 3:3 + T1], fm[:, m % 2, 0:T1], ACT.Copy).then_inc(emptied[m % 2], 1)
                hi(6 + m)
            for m in range(2):
                unit_wait(6 + m)
                act.activation(gy[:, m, :], fm[:, m % 2, 0:S], ACT.Gelu_apprx_tanh).then_inc(emptied[m % 2], 1)
                hi(10 + m)
            for m in range(LT):
                act.wait_ge(r_ps, m + 1)
                act.activation(r_g[:, m, :], acc[:, m, 0:T1], ACT.Sigmoid, bias=cwb[:, m, 5:6])
                act.activation(i_g[:, m, :], (ma, mb)[m % 2][:, 0:T1], ACT.Sigmoid, bias=cwb[:, m, 6:7]).then_inc(r_act, 1)
            act.wait_ge(sp_ready, 1)
            act.wait_ge(r_act, LT)
            for m in range(LT):
                act.activation(th_[:, m, :], r_g[:, m, :], ACT.Tanh, scale=lam_t[:, 6, m:m + 1]).then_inc(tanh_out, 1)
            for m in range(LT):
                act.activation(a_[:, m, :], r_g[:, m, :], ACT.Exp, scale=lam_t[:, 7, m:m + 1]).then_inc(a_out, 1)
            act.wait_ge(a_out, LT)
            act.activation(a2, a_, ACT.Square).then_inc(a_out, 1)
            for m in range(4):
                unit_wait(8 + m)
                act.activation(qT1[:, m, :], fm[:, m % 2, 0:S], ACT.Copy).then_inc(emptied[m % 2], 1)
                hi(12 + m)
            act.wait_ge(m2_out, 1)
            act.activation(a2, th_, ACT.Sqrt).then_inc(mult_out, 1)
            for m in range(2):
                unit_wait(12 + m)
                act.activation(gy[:, 2 + m, :], fm[:, m % 2, 0:S], ACT.Gelu_apprx_tanh).then_inc(emptied[m % 2], 1)
                hi(16 + m)
            act.wait_ge(rec_out, 1)
            act.activation(yTh[:, 4:8, :], gy, ACT.Copy).then_inc(rec_hi, 1)
            for b in range(2):
                nk = (P + META, 2 * P)[b]
                act.wait_ge(s1_max, b + 1)
                for hh in range(QH):
                    act.activation(p1[:, hh, 0:nk], sm1[:, hh, 0:nk], ACT.Exp, bias=st[:, 16 + hh:17 + hh],
                                   accum_out=st[:, 8 + hh:9 + hh]).then_inc(s1_exp, 1)
                act.activation(st[:, 24:32], st[:, 24:32], ACT.Exp).then_inc(s1_sink, 1)
                act.wait_ge(p1T_ps, 2 * b + 1)
                act.activation(pT1[:, 0:4, :, :], acc[:, 0:2, :].rearrange("p b (h c n) -> p (b h) c n", h=2, c=2), ACT.Copy).then_inc(p1T_out, 1)
                act.wait_ge(o1T_ps, b + 1)
                act.activation(yTh[:, 0:4, b * P:(b + 1) * P], mb[:, :].rearrange("p (k n) -> p k n", k=4), ACT.Copy).then_inc(o1T_hi, 1)
            for n in range(14, 22):
                hi(n + 4)
            acc_stat(21)
            norm(0, h, META)

            def norm_hi(base, off):
                for t in range(NT):
                    act.wait_ge(ut_ps, base + t + 1)
                    act.activation(xTh[:, :, off + t * P:off + (t + 1) * P],
                                   acc[:, 2 * t:2 * t + 2, :].rearrange("p b (k n) -> p (b k) n", n=P), ACT.Copy).then_inc(ut_hi, 1)

            norm_hi(3, 0)

            def ffn1_hidden(fu, par, n0, stride=0, i=0):
                for j in range(2):
                    unit_wait(fu + j, stride, i)
                    act.activation(hid_t[:, j, :], fm[:, j, 0:S], ACT.Relu).then_inc(emptied[j], 1)
                    hi(fu + j + 4, stride, i)
                for j in range(2):
                    act.wait_ge(hid_s, i * (stride // 2) + (2 * n0 + j + 1))
                    act.activation(hid_h[:, par, j, :], hid_q[:, j, :], ACT.Copy).then_inc(hid_hi, 1)

            def acc_units(fu, stride=0, i=0):
                for j in range(2):
                    hi(fu + j + 4, stride, i)

            F = 2 * P_FF1
            ffn1_hidden(F, 0, 0)
            for i in rounds(act, 7):
                ffn1_hidden(F + 2, 1, 1, 8, i)
                acc_units(F + 4, 8, i)
                ffn1_hidden(F + 6, 0, 2, 8, i)
                acc_units(F + 8, 8, i)
            ffn1_hidden(F + 58, 1, 15)
            acc_units(F + 60)
            acc_units(F + 62)
            acc_stat(F + 63)
            norm(1, h, 0)
            norm_hi(5, 0)
            act.wait_ge(small2, 16 * 8)
            act.activation(ab_h, ab_w, ACT.Copy).then_inc(ab_hi, 1)
            act.activation(dt_row[:, 1, :], dt_row[:, 1, :], ACT.Exp).then_inc(ab_act, 1)
            act.wait_ge(ab_out, 1)
            act.activation(g_all[:, 0, :, :], ma[:, 0:32].rearrange("p (t n) -> p t n", t=2)[:, :, 0:8], ACT.Sigmoid).then_inc(ab_act, 1)
            ch.link(act.activation(tmp16[:, 1, :], tmp16[:, 0, :], ACT.Abs))
            act.activation(tmp16[:, 2, :], tmp16[:, 1, :], ACT.Exp, scale=-1.0).then_inc(ab_act, 1)

            def moba_unit(c, fu, stride, a, pair):
                unit_wait(fu, stride, a)
                if c < 4:
                    act.wait_ge(rope_out, pair) if not (isinstance(pair, int) and pair == 0) else None
                    act.activation(qk[:, c, :], fm[:, c % 2, 0:S], ACT.Copy).then_inc(emptied[c % 2], 1)
                elif c < 6:
                    act.activation(ga[:, bass.ds(pair * 2 + (c - 4), 1), :].rearrange("p a n -> p (a n)"),
                                   fm[:, c % 2, 0:S], ACT.Copy).then_inc(emptied[c % 2], 1)
                elif c == 7:
                    for t in range(NT):
                        act.activation(va[:, t, :], fm[:, t, 0:S], ACT.Copy).then_inc(emptied[t], 1)
                hi(fu + 4, stride, a)

            def gdn_unit(c, fu, stride, a, pair):
                unit_wait(fu, stride, a)
                later = not (isinstance(pair, int) and pair == 0)
                if c < 6:
                    if later:
                        act.wait_ge(cv_out, (pair - 1) * 3 + (c // 2 + 1))
                    act.activation(raw[:, c, 3:3 + S], fm[:, c % 2, 0:S], ACT.Copy).then_inc(emptied[c % 2], 1)
                elif c == 7:
                    if later:
                        act.wait_ge(sz_out, pair)
                    for t in range(NT):
                        act.activation(zr[:, t, :], fm[:, t, 0:S], ACT.Copy).then_inc(emptied[t], 1)
                hi(fu + 4, stride, a)

            def gateb_unit(c, fu, stride, a, pair):
                unit_wait(fu, stride, a)
                act.activation(gb_s[:, c, :], fm[:, c % 2, 0:S], ACT.Copy).then_inc(emptied[c % 2], 1)
                hi(fu + 4, stride, a)

            def moba_stage(s, a):
                if s == 0:
                    act.wait_ge(emptied[0], along(EMPTIED0, 2 * P_MOBA + 4, 8, a))
                    act.wait_ge(emptied[1], along(EMPTIED1, 2 * P_MOBA + 4, 8, a))
                    act.activation(rot[0:64, :, :], qk[64:128, :, :], ACT.Copy)
                    act.activation(rot[64:128, :, :], qk[0:64, :, :], ACT.Copy).then_inc(rot_out, 1)
                if s == 2:
                    act.wait_ge(s2_max, a + 1)
                    for n, (lo_, hi_) in enumerate(((0, 256), (256, 384))):
                        for j in range(2):
                            ins = act.activation(p2[:, j, lo_:hi_], sm2[:, j, lo_:hi_], ACT.Exp,
                                                 bias=st[:, 16 + 2 * n + j:17 + 2 * n + j], accum_out=st[:, 8 + 2 * n + j:9 + 2 * n + j])
                    ins.then_inc(s2_exp, 1)
                if s == 3:
                    act.wait_ge(p2T_ps, a + 1)
                    act.activation(pT2[:, 0, :], acc[:, 2, 0:384], ACT.Copy).then_inc(p2T_a, 1)
                if s == 4:
                    act.wait_ge(o2_ps, a + 1)
                    act.activation(yTh[:, bass.ds(a * 2, 2), :], ma[:, :].rearrange("p (j n) -> p j n", j=2), ACT.Copy).then_inc(o2_hi, 1)

            def start_inverse():
                act.activation(X_, ident.unsqueeze(1).to_broadcast([P, 4, P]), ACT.Copy).then_inc(inv_start, 1)

            def gdn_stage(s, a):
                if s == 0:
                    act.wait_ge(cv_out, a * 3 + 3)
                    act.activation(cv, cvn, ACT.Silu).then_inc(silu_out, 1)
                    act.wait_ge(silu_out, a + 1)
                    for q in (1, 0):
                        act.activation(sq[:, q * 512:(q + 1) * 512], cv[:, 2 * q:2 * q + 2, :].rearrange("p a b -> p (a b)"),
                                       ACT.Square).then_inc(sq_out, 1)
                if s == 1:
                    act.preload_act_table_set("natural_log_exp_and_others")
                    for n, q in enumerate((1, 0)):
                        act.wait_ge(ssq_ps, a * 2 + (n + 1))
                        rq = rk[:, q * 512:(q + 1) * 512]
                        ch.link(act.activation(rq, acc[:, q, :], ACT.Ln, bias=eps[:, 0:1]))
                        act.activation(rq, rq, ACT.Exp, scale=-0.5).then_inc(rk_out, 1)
                if s == 2:
                    act.wait_ge(vT_ps, a + 1)
                    for pr in range(4):
                        c, j = pr // 2, pr % 2
                        ins = act.activation(vb[:, pr, :], acc[:, 3, pr * P:(pr + 1) * P], ACT.Copy, scale=sc[:, 0, c, j:j + 1])
                    ins.then_inc(vb_out, 1)
                if s == 3:
                    act.wait_ge(kT_ps, a + 1)
                    for j in range(2):
                        act.activation(kdec[:, j, :], acc[:, 0, j * P:(j + 1) * P], ACT.Copy, scale=sc[:, 4, 0, j:j + 1])
                        ins = act.activation(kbe[:, j, :], acc[:, 0, (2 + j) * P:(3 + j) * P], ACT.Copy, scale=sc[:, 3, 1, j:j + 1])
                    ins.then_inc(kv_out, 1)
                if s == 4:
                    act.wait_ge(xt0_ps, a + 1)
                    act.activation(XT_, acc[:, 3, :].rearrange("p (r n) -> p r n", r=4), ACT.Copy).then_inc(xt0_out, 1)
                if s == 17:
                    act.wait_ge(uw_ps, a + 1)
                    act.activation(u0, acc[:, 3, 0:256].rearrange("p (j n) -> p j n", j=2), ACT.Copy).then_inc(u0_out, 1)
                if s == 18:
                    act.wait_ge(so_ps, a + 1)
                    act.activation(S1, acc[:, 1, 0:256].rearrange("p (j n) -> p j n", j=2), ACT.Copy).then_inc(S1_out, 1)
                if s == 19:
                    act.wait_ge(vn_ps, a + 1)
                    act.activation(vn, acc[:, 3, 256:512].rearrange("p (j n) -> p j n", j=2), ACT.Copy).then_inc(vn_out, 1)
                if s == 7 and not (isinstance(a, int) and a == 0):
                    out_root(a - 1)
                if s == 14 and not (isinstance(a, int) and a == 0):
                    out_hi(a - 1)
                if s == 13 and not (isinstance(a, int) and a == PAIRS - 1):
                    decays(a + 1)
                if s == 15:
                    act.wait_ge(emptied[0], along(EMPTIED0, 2 * P_GDN + 8, 8, a))
                    act.wait_ge(emptied[1], along(EMPTIED1, 2 * P_GDN + 8, 8, a))
                    if not (isinstance(a, int) and a == 0):
                        act.wait_ge(y_out, a)
                    act.activation(sz, zr, ACT.Silu).then_inc(sz_out, 1)
                if s == 20:
                    act.wait_ge(o_ps, a + 1)
                    act.activation(o_s, acc[:, 2, :].rearrange("p (r n) -> p r n", r=4), ACT.Copy).then_inc(os_out, 1)
                    if not (isinstance(a, int) and a == PAIRS - 1):
                        start_inverse()

            def decays(b):
                act.wait_ge(t12_out, b + 1)
                act.activation(eg, mb[:, 256:512].rearrange("p (j n) -> p j n", j=2), ACT.Exp)
                for pr in range(4):
                    c, j = pr // 2, pr % 2
                    act.activation(dt_[:, pr, :], dt_[:, pr, :], ACT.Exp, bias=sc[:, 2, c, j:j + 1])
                    ins = act.activation(dl_[:, pr, :], dl_[:, pr, :], ACT.Exp, bias=sc[:, 1, c, j:j + 1])
                ins.then_inc(dt_out, 1)

            def out_root(b):
                act.wait_ge(os_out, b + 1)
                for pr in range(4):
                    ins = act.activation(junk[:, 512 + pr * P:640 + pr * P], o_s[:, pr, :], ACT.Square, accum_out=st[:, pr:pr + 1])
                ch.link(ins)
                ch.link(act.activation(st[:, 4:8], st[:, 0:4], ACT.Ln, bias=eps[:, 0:1], scale=1.0 / P))
                act.activation(st[:, 4:8], st[:, 4:8], ACT.Exp, scale=-0.5).then_inc(og_out, 1)

            def out_hi(b):
                act.wait_ge(yT_ps, b + 1)
                dst = ybh[:, bass.ds(b * 2, 2), :].rearrange("p j (c n) -> p j c n", c=2)
                act.activation(dst, ma[:, :].rearrange("p (c j n) -> p j c n", c=2, j=2), ACT.Copy).then_inc(yb_hi, 1)

            def pair_round(weave, stage, unit, fu, a, pair, mine=0):
                before = ch.n
                for s, done in enumerate(finished(weave)):
                    stage(s, a)
                    for c in done:
                        unit(c, fu + c, 8, a, pair)
                return ch.n - before if isinstance(ch.n, int) else None

            M, G = 2 * P_MOBA, 2 * P_GDN
            for c in range(8):
                moba_unit(c, M + c, 8, 0, 0)
            act.wait_ge(gc_ps, 1)
            gcs = mb[:, 0:32].rearrange("p (v c h) -> p v c h", v=2, c=2)
            act.activation(g_all[:, 1, :, :], gcs[:, 0], ACT.Copy)
            act.activation(g_all[:, 2, :, :], gcs[:, 0], ACT.Copy, scale=-1.0)
            act.activation(g_all[:, 3, :, :], gcs[:, 0], ACT.Exp).then_inc(gc_act, 1)
            act.wait_ge(gc_ready, 1)
            act.activation(g_all[:, 4, :, :], g_all[:, 6, :, :], ACT.Exp).then_inc(gc_act, 1)
            for i in rounds(act, 3, ch, 0):
                pair_round(MOBA_WEAVE, moba_stage, moba_unit, M + 8, i, i + 1)
            pair_round(MOBA_WEAVE, moba_stage, gdn_unit, M + 8, 3, 0)
            start_inverse()
            decays(0)
            pair_round(GDN_WEAVE, gdn_stage, gdn_unit, G + 8, 0, 1)
            for i in rounds(act, 2, ch, 4):
                pair_round(GDN_WEAVE, gdn_stage, gdn_unit, G + 8, i + 1, i + 2)
            pair_round(GDN_WEAVE, gdn_stage, gateb_unit, G + 8, 3, 0)
            out_root(3)
            act.activation(ga, ga, ACT.Sigmoid).then_inc(sig_a, 1)
            act.wait_ge(emptied[0], EMPTIED0[2 * P_PROJA])
            act.wait_ge(emptied[1], EMPTIED1[2 * P_PROJA])
            act.activation(gb_s, gb_s, ACT.Sigmoid).then_inc(sig_b, 1)
            for n in range(16):
                hi(2 * P_PROJA + n + 4)
                if n == 2:
                    out_hi(3)
            for q in range(2):
                act.wait_ge(mg_out, 4 * q + 4)
                act.activation(yTh[:, 4 * q:4 * q + 4, :], gb_s[:, 4 * q:4 * q + 4, :], ACT.Copy).then_inc(mg_hi, 1)
            for n in range(8):
                hi(2 * P_OUT2 + n + 4)
            acc_stat(2 * P_OUT2 + 7)
            norm(2, h, 0)
            norm_hi(7, 0)
            F2 = 2 * P_FF2

            def silu_gate(fu, stride=0, i=0, k=0):
                for j in range(2):
                    unit_wait(fu + j, stride, i)
                    if k > 0:
                        act.wait_ge(swi_m, i * (stride // 3) + 2 * (k - 1) + j + 1)
                    act.activation(gate_s[:, j, :], fm[:, j, 0:S], ACT.Silu).then_inc(swi_a, 1)
                    hi(fu + j + 4, stride, i)

            def hid2_hi(fu, stride=0, i=0, k=0):
                for j in range(2):
                    act.wait_ge(swi_m, i * (stride // 3) + 2 * k + j + 1)
                    act.activation(hid2_h[:, j, :], hid2[:, j, :], ACT.Copy).then_inc(swi_hi, 1)
                    hi(fu + j + 4, stride, i)

            silu_gate(F2)
            hid2_hi(F2 + 2)
            for i in rounds(act, 4):
                for n in range(2):
                    silu_gate(F2 + 4 + 6 * n, 12, i, n + 1)
                    acc_units(F2 + 6 + 6 * n, 12, i)
                    hid2_hi(F2 + 8 + 6 * n, 12, i, n + 1)
            for n in range(2):
                silu_gate(F2 + 4 + 6 * n + 48, 0, 0, n + 9)
                acc_units(F2 + 6 + 6 * n + 48)
                hid2_hi(F2 + 8 + 6 * n + 48, 0, 0, n + 9)
            acc_units(F2 + 64)
            acc_stat(F2 + 65)
            act.wait_ge(ut_ps, 10)
            act.activation(xTh[:, 0:2, 0:S].rearrange("p k (t n) -> p t k n", t=2), ma[:, :].rearrange("p (t k n) -> p t k n", t=2, k=2), ACT.Copy).then_inc(ut_hi, 1)
            for n in range(2):
                hi(2 * P_PLE + n + 4)
            acc_stat(2 * P_PLE + 1)
            norm_hi(10, 0)
            for n in range(8):
                hi(2 * P_PGATE + n + 4)
            act.wait_ge(unit_done, 2 * P_ALL)
            for t in range(NT):
                act.activation(u[:, t, :], acc[:, 2 * t:2 * t + 2, :].rearrange("p b n -> p (b n)"), ACT.Sigmoid).then_inc(fin_sig, 1)

        @block.vector
        def _(dve):
            ch = Chain(dve, dve_chain)
            link = ch.link
            TT, TS, STT = dve.tensor_tensor, dve.tensor_scalar, dve.scalar_tensor_tensor

            def lo(pu, stride=0, i=0):
                p, j = pu // 2, pu % 2
                if p >= P_ALL:
                    return
                if isinstance(i, int):
                    pu, i, stride = pu + stride * i, 0, 0
                    p = pu // 2
                layout = PLAN[p][0]
                dve.wait_ge(w_hi, i * stride + (pu + 1))
                TT(split_view(wl, pu % UNITS, layout), raw_unit(SLOT[p], j, layout),
                   split_view(wh, pu % UNITS, layout).bitcast(F32), ALU.subtract).then_inc(w_lo, 1)

            def log1p(y, z, t, out):
                link(TS(t, y, 2.0, None, ALU.add))
                link(dve.reciprocal(t, t))
                link(TT(z, y, t, ALU.mult))
                link(TT(t, z, z, ALU.mult))
                link(TS(out, t, 1.0 / 19, None, ALU.mult))
                for c in (17, 15, 13, 11, 9, 7, 5, 3):
                    link(STT(out, out, 1.0 / c, t, ALU.add, ALU.mult))
                link(STT(out, out, 1.0, z, ALU.add, ALU.mult))
                link(TS(out, out, 2.0, None, ALU.mult))

            def norm_rows(n, src, g, off, base):
                dve.wait_ge(stat, n)
                link(dve.reciprocal(st[:, 4:6], st[:, 4:6]))
                dve.wait_ge(gain_loaded[g % 2], 16 * (g // 2 + 1))
                for t in range(NT):
                    STT(u[:, t, :], src[:, t, :], st[:, 4 + t:5 + t], gain[:, g % 2, :], ALU.mult, ALU.mult).then_inc(u_ready, 1)

            def norm_lo(base, off):
                for t in range(NT):
                    dve.wait_ge(ut_hi, base + t + 1)
                    TT(xTl[:, :, off + t * P:off + (t + 1) * P],
                       acc[:, 2 * t:2 * t + 2, :].rearrange("p b (k n) -> p (b k) n", n=P),
                       xTh[:, :, off + t * P:off + (t + 1) * P].bitcast(F32), ALU.subtract).then_inc(ut_lo, 1)

            def residual(n, g):
                dve.wait_ge(stat, n)
                link(dve.reciprocal(st[:, 4:6], st[:, 4:6]))
                dve.wait_ge(gain_loaded[g % 2], 16 * (g // 2 + 1))
                for t in range(NT):
                    ins = STT(u[:, t, :], acc[:, 2 * t:2 * t + 2, :].rearrange("p b n -> p (b n)"), st[:, 4 + t:5 + t],
                              gain[:, g % 2, :], ALU.mult, ALU.mult)
                    if t == 0:
                        link(ins)
                    else:
                        ins.then_inc(gain_used, 1)
                        dve.wait_ge(gain_used, g // 2 + 1)
                    TT(h[:, t, :], h[:, t, :], u[:, t, :], ALU.add).then_inc(h_ready, 1)

            dve.wait_ge(stat, 1)
            dve.wait_ge(filled, 4)
            dve.reciprocal(st[0:META, 6:7], st[0:META, 6:7])
            link(dve.reciprocal(st[:, 4:6], st[:, 4:6]))
            dve.wait_ge(gain_loaded[0], 16)
            dve.wait_ge(x_loaded, 32)
            for t in range(NT):
                link(dve.tensor_copy(h[:, t, :], u[:, t, :]))
            STT(meta[0:META, :], meta[0:META, :], st[0:META, 6:7], gain[0:META, 0, :], ALU.mult, ALU.mult).then_inc(u_ready, 1)
            for t in range(NT):
                STT(u[:, t, :], h[:, t, :], st[:, 4 + t:5 + t], gain[:, 0, :], ALU.mult, ALU.mult).then_inc(u_ready, 1)
            for n in range(4):
                lo(n)
            dve.wait_ge(ut_hi, 1)
            TT(xTl[:, :, 0:META], ma[:, 0:KC * META].rearrange("p (k n) -> p k n", k=KC), xTh[:, :, 0:META].bitcast(F32),
               ALU.subtract).then_inc(ut_lo, 1)
            norm_lo(1, META)
            dve.wait_ge(lam_e, 1)
            log1p(lam_t[:, 1, :], lam_t[:, 2, :], lam_t[:, 3, :], lam_t[:, 4, :])
            link(TS(lam_t[:, 5, :], cwb[:, :, 7], -1.0, 0.0, ALU.mult, ALU.max))
            link(TT(lam_t[:, 4, :], lam_t[:, 4, :], lam_t[:, 5, :], ALU.add))
            TS(lam_t[:, 6, :], lam_t[:, 4, :], 8.0, None, ALU.mult)
            TS(lam_t[:, 7, :], lam_t[:, 4, :], -8.0, None, ALU.mult).then_inc(sp_ready, 1)
            lo(4)
            lo(5)
            for q in range(2):
                lo(6 + 2 * q)
                lo(7 + 2 * q)
                dve.wait_ge(emptied[0], 2 + q)
                dve.wait_ge(emptied[1], 1 + q)
                for m in (2 * q, 2 * q + 1):
                    ins = TS(xc[:, m, :], xr_pad[:, m, 0:T1], cwb[:, m, 0:1], cwb[:, m, 4:5], ALU.mult, ALU.add)
                link(ins)
                for tap in range(1, 4):
                    for m in (2 * q, 2 * q + 1):
                        ins = STT(xc[:, m, :], xr_pad[:, m, tap:tap + T1], cwb[:, m, tap:tap + 1], xc[:, m, :], ALU.mult, ALU.add)
                    if tap < 3:
                        link(ins)
                ins.then_inc(xc_ready, 1)
            lo(10)
            lo(11)
            dve.wait_ge(r_act, LT)
            dve.wait_ge(xc_ready, 2)
            link(TT(xc, i_g, xc, ALU.mult))
            dve.wait_ge(tanh_out, LT)
            dve.wait_ge(a_out, LT + 1)
            STT(th_, a2, 1.0, th_, ALU.add, ALU.mult).then_inc(m2_out, 1)
            for n in range(12, 16):
                lo(n)
            dve.wait_ge(mult_out, 1)
            link(TT(xc, a2, xc, ALU.mult))
            for m in range(LT):
                ins = dve.tensor_tensor_scan(r_g[:, m, :], a_[:, m, :], xc[:, m, :], 0.0, ALU.mult, ALU.add)
            link(ins)
            lo(16)
            lo(17)
            dve.wait_ge(emptied[0], EMPTIED0[14])
            dve.wait_ge(emptied[1], EMPTIED1[14])
            TT(gy, gy, r_g[:, :, META:T1], ALU.mult).then_inc(rec_out, 1)
            dve.wait_ge(rec_hi, 1)
            TT(yTl[:, 4:8, :], gy, yTh[:, 4:8, :].bitcast(F32), ALU.subtract).then_inc(rec_lo, 1)
            dve.wait_ge(small1, 16 * 10)
            for b in range(2):
                nk = (P + META, 2 * P)[b]
                mask = cst[:, (C_WIN0, C_WIN1)[b]:(C_WIN0, C_WIN1)[b] + nk]
                dve.wait_ge(s1_ps, b + 1)
                dve.wait_ge(cst_loaded, 16)
                sc_ps = acc[:, :, :].rearrange("p b (h n) -> p (b h) n", h=2)
                link(STT(sm1[:, :, 0:nk], sc_ps[:, :, 0:nk], SC1, mask.unsqueeze(1).to_broadcast([P, QH, nk]), ALU.mult, ALU.add))
                if b:
                    dve.wait_ge(s1_exp, QH * b)
                link(dve.tensor_reduce(st[:, 16:24], sm1[:, :, 0:nk], AX, ALU.max))
                link(TT(st[:, 16:24], st[:, 16:24], sink, ALU.max))
                link(TT(st[:, 24:32], sink, st[:, 16:24], ALU.subtract))
                TS(st[:, 16:24], st[:, 16:24], -1.0, None, ALU.mult).then_inc(s1_max, 1)
                dve.wait_ge(s1_sink, b + 1)
                dve.wait_ge(s1_exp, QH * (b + 1))
                link(TT(st[:, 8:16], st[:, 8:16], st[:, 24:32], ALU.add))
                link(dve.reciprocal(st[:, 8:16], st[:, 8:16]))
                dve.wait_ge(p1T_ps, 2 * b + 2)
                dve.tensor_copy(pT1[:, 4:8, :, :], acc[:, 2:4, :].rearrange("p b (h c n) -> p (b h) c n", h=2, c=2)).then_inc(p1T_out, 1)
                dve.wait_ge(o1_ps, b + 1)
                TT(o1.rearrange("p (m b n) -> p m b n", m=4, b=2), ma[:, :].rearrange("p (m b n) -> p m b n", m=4, b=2),
                   st[:, 8:16].rearrange("p (b m) -> p m b", b=2).unsqueeze(3).to_broadcast([P, 4, 2, HD1]), ALU.mult).then_inc(o1_out, 1)
                dve.wait_ge(o1T_hi, b + 1)
                TT(yTl[:, 0:4, b * P:(b + 1) * P], mb[:, :].rearrange("p (k n) -> p k n", k=4),
                   yTh[:, 0:4, b * P:(b + 1) * P].bitcast(F32), ALU.subtract).then_inc(o1T_lo, 1)
            for n in range(18, 26):
                lo(n)
            dve.wait_ge(ut_lo, 3)
            residual(2, 1)
            norm_rows(3, h, 2, 0, 3)
            norm_lo(3, 0)

            def ffn1_hidden(fu, par, n0, stride=0, i=0):
                for j in range(2):
                    lo(fu + j + 4, stride, i)
                    dve.wait_ge(emptied[j], along(AFTER[j], fu + j, stride, i))
                    if n0:
                        dve.wait_ge(hid_lo, i * (stride // 2) + 2 * n0 + j - 1)
                    TT(hid_q[:, j, :], hid_t[:, j, :], hid_t[:, j, :], ALU.mult).then_inc(hid_s, 1)
                for j in range(2):
                    k = i * (stride // 2) + 2 * n0 + j + 1
                    dve.wait_ge(hid_hi, k)
                    TT(hid_l[:, par, j, :], hid_q[:, j, :], hid_h[:, par, j, :].bitcast(F32), ALU.subtract).then_inc(hid_lo, 1)

            def acc_units(fu, stride=0, i=0):
                for j in range(2):
                    lo(fu + j + 4, stride, i)

            F = 2 * P_FF1
            ffn1_hidden(F, 0, 0)
            for i in rounds(dve, 7):
                ffn1_hidden(F + 2, 1, 1, 8, i)
                acc_units(F + 4, 8, i)
                ffn1_hidden(F + 6, 0, 2, 8, i)
                acc_units(F + 8, 8, i)
            ffn1_hidden(F + 58, 1, 15)
            acc_units(F + 60)
            acc_units(F + 62)
            residual(4, 3)
            norm_rows(5, h, 4, 0, 5)
            norm_lo(5, 0)
            dve.wait_ge(ab_hi, 1)
            TT(ab_l, ab_w, ab_h.bitcast(F32), ALU.subtract).then_inc(ab_lo, 1)
            dve.wait_ge(ab_ps, 1)
            x_dt = tmp16[:, 0, :].rearrange("p (t n) -> p t n", t=2)
            TT(x_dt, ma[:, 0:32].rearrange("p (t n) -> p t n", t=2)[:, :, 8:16],
               dt_row[:, 0, :].unsqueeze(1).to_broadcast([P, 2, 8]), ALU.add).then_inc(ab_out, 1)
            dve.wait_ge(ab_act, 3)
            log1p(tmp16[:, 2, :], tmp16[:, 3, :], tmp16[:, 4, :], tmp16[:, 5, :])
            link(STT(tmp16[:, 5, :], tmp16[:, 0, :], 0.0, tmp16[:, 5, :], ALU.max, ALU.add))
            STT(g_all[:, 5, :, :], tmp16[:, 5, :].rearrange("p (t n) -> p t n", t=2), -1.0,
                dt_row[:, 1, :].unsqueeze(1).to_broadcast([P, 2, 8]), ALU.mult, ALU.mult).then_inc(g_ready, 1)

            def pair_unit(c, fu, stride, a, pair):
                lo(fu + 4, stride, a)

            def moba_stage(s, a):
                if s == 0:
                    cosb = cst[:, C_COS:C_SIN].unsqueeze(1).to_broadcast([P, 4, S])
                    sinb = cst[:, C_SIN:C_END].unsqueeze(1).to_broadcast([P, 4, S])
                    dve.wait_ge(rot_out, a + 1)
                    TT(qr, qk, cosb, ALU.mult)
                    link(TT(rot, rot, sinb, ALU.mult))
                    TT(qr, qr, rot, ALU.add).then_inc(rope_out, 1)
                if s == 1:
                    dve.wait_ge(s2_ps, a + 1)
                    mask = cst[:, C_MOBA:C_WIN0].unsqueeze(1).to_broadcast([P, 2, 384])
                    link(STT(sm2, acc[:, 0:2, 0:384], SC2, mask, ALU.mult, ALU.add))
                    dve.tensor_reduce(st[:, 16:18], sm2[:, :, 0:256], AX, ALU.max)
                    link(dve.tensor_reduce(st[:, 18:20], sm2[:, :, 256:384], AX, ALU.max))
                    TS(st[:, 16:20], st[:, 16:20], -1.0, None, ALU.mult).then_inc(s2_max, 1)
                if s == 2:
                    dve.wait_ge(s2_exp, a + 1)
                    link(dve.reciprocal(st[:, 8:12], st[:, 8:12]))
                    for n, (lo_, hi_) in enumerate(((0, 256), (256, 384))):
                        for j in range(2):
                            ins = TS(p2[:, j, lo_:hi_], p2[:, j, lo_:hi_], st[:, 8 + 2 * n + j:9 + 2 * n + j], None, ALU.mult)
                    ins.then_inc(s2_p, 1)
                if s == 3:
                    dve.wait_ge(p2T_ps, a + 1)
                    dve.tensor_copy(pT2[:, 1, :], acc[:, 3, 0:384]).then_inc(p2T_v, 1)
                if s == 4:
                    dve.wait_ge(o2_hi, a + 1)
                    TT(yTl[:, bass.ds(a * 2, 2), :], ma[:, :].rearrange("p (j n) -> p j n", j=2),
                       yTh[:, bass.ds(a * 2, 2), :].bitcast(F32), ALU.subtract).then_inc(o2_lo, 1)

            def rows4(x):
                return x.rearrange("p (r n) -> p r n", r=4)

            def spread(x):
                return x.unsqueeze(1).to_broadcast([P, 4, P])

            def half_blocks(x, n, odd):
                return x.rearrange("p r (q two b) -> p (r q) two b", two=2, b=1 << n)[:, :, odd, :]

            def grow(x, n, odd, z):
                v = half_blocks(x, n, odd)
                return TT(v, v, z, ALU.subtract)

            def gdn_stage(s, a):
                if s == 1:
                    for n, q in enumerate((1, 0)):
                        dve.wait_ge(rk_out, a * 2 + (n + 1))
                        x = cv[:, 2 * q:2 * q + 2, :].rearrange("p a b -> p (a b)")
                        TT(x, x, rk[:, q * 512:(q + 1) * 512], ALU.mult).then_inc(qkn_out, 1)
                if s == 3:
                    dve.wait_ge(kk_ps, a + 1)
                    dve.wait_ge(dt_out, a + 1)
                    for pr in range(4):
                        ins = STT(A_[:, pr, :], acc[:, 1, pr * P:(pr + 1) * P], sc[:, 0, pr // 2, pr % 2:pr % 2 + 1], dl_[:, pr, :], ALU.mult, ALU.mult)
                    ins.then_inc(A_out, 1)
                    dve.wait_ge(A_out, a + 1)
                    dve.wait_ge(inv_start, a + 1)
                    low = PM_.rearrange("p r n -> p (r n)")[:, 0:4 * 64]
                    first = cst[:, C_LEV:C_LEV + 64].unsqueeze(1).to_broadcast([P, 4, 64])
                    link(TT(rows4(low), A_.rearrange("p r (q two) -> p r q two", two=2)[:, :, :, 0], first, ALU.mult))
                    grow(X_, 0, 0, low.rearrange("p (m b) -> p m b", b=1)).then_inc(x0_out, 1)
                if s == 4:
                    dve.wait_ge(kq_ps, a + 1)
                    STT(attnT, rows4(acc[:, 2, :]), SC2, dt_, ALU.mult, ALU.mult).then_inc(attn_out, 1)
                    STT(qeg, cv[:, 0:2, P:2 * P], SC2, eg, ALU.mult, ALU.mult).then_inc(qeg_out, 1)
                if s == 8 and not (isinstance(a, int) and a == PAIRS - 1):
                    dve.wait_ge(kv_out, a + 1)
                    dve.wait_ge(qeg_out, a + 1)
                    prepare(a + 1)
                if s == 10 and not (isinstance(a, int) and a == PAIRS - 1):
                    exponents(a + 1)
                if 5 <= s < 17 and s % 2 == 1:
                    lv = (s - 5) // 2 + 1
                    for g in range(2):
                        dve.wait_ge(lv_p[g], a * 6 + lv)
                        mask = cst[:, C_LEV + lv * P:C_LEV + (lv + 1) * P].unsqueeze(1).to_broadcast([P, 2, P])
                        TT(PM_[:, 2 * g:2 * g + 2, :], acc[:, 3 * g, 0:256].rearrange("p (j n) -> p j n", j=2), mask,
                           ALU.mult).then_inc(lv_pm[g], 1)
                if 5 <= s < 17 and s % 2 == 0:
                    lv = (s - 5) // 2 + 1
                    for g in range(2):
                        dve.wait_ge(lv_z[g], a * 6 + lv)
                        z = acc[:, 1 + g, :].rearrange("p (r n) -> p r n", r=4)
                        grow(XT_[:, 2 * g:2 * g + 2, :], lv, 1, half_blocks(z[:, 0:2, :], lv, 1)).then_inc(lv_xt[g], 1)
                        if lv < 6:
                            grow(X_[:, 2 * g:2 * g + 2, :], lv, 0, half_blocks(z[:, 2:4, :], lv, 0)).then_inc(lv_x[g], 1)
                if s == 17:
                    dve.wait_ge(uw_ps, a + 1)
                    TS(nwT, acc[:, 0, 0:256].rearrange("p (j n) -> p j n", j=2), -1.0, None, ALU.mult).then_inc(nw_out, 1)
                if s == 11 and not (isinstance(a, int) and a == 0):
                    out_rows(a - 1)
                if s == 14 and not (isinstance(a, int) and a == 0):
                    out_lo(a - 1)

            def prepare(b):
                link(dve.tensor_copy(sc, g_all[:, 0:6, :, bass.ds(b * 2, 2)]))
                gsrc = sc[:, 5, :, :].rearrange("p c j -> p (c j)").unsqueeze(2).to_broadcast([P, 4, P])
                dve.tensor_copy(gb, gsrc).then_inc(gb_out, 1)

            def exponents(b):
                dve.wait_ge(gcb_ps, b + 1)
                TT(dt_, rows4(mb[:, :]), spread(cst[:, C_MUP:C_MLOW]), ALU.add)
                TT(dl_, spread(cst[:, C_MLOW:C_LEV]), rows4(mb[:, :]), ALU.subtract).then_inc(t12_out, 1)

            def out_rows(b):
                dve.wait_ge(og_out, b + 1)
                dve.wait_ge(sz_out, b + 1)
                for pr in range(4):
                    ins = STT(y_[:, pr, :], o_s[:, pr, :], st[:, 4 + pr:5 + pr], gnorm, ALU.mult, ALU.mult)
                link(ins)
                TT(y_, y_, sz.rearrange("p t (j n) -> p (t j) n", j=2), ALU.mult).then_inc(y_out, 1)

            def out_lo(b):
                dve.wait_ge(yb_hi, b + 1)
                dst = ybl[:, bass.ds(b * 2, 2), :].rearrange("p j (c n) -> p j c n", c=2)
                hi_ = ybh[:, bass.ds(b * 2, 2), :].rearrange("p j (c n) -> p j c n", c=2).bitcast(F32)
                TT(dst, ma[:, :].rearrange("p (c j n) -> p j c n", c=2, j=2), hi_, ALU.subtract).then_inc(yb_lo, 1)

            def pair_round(weave, stage, unit, fu, a, pair):
                for s, done in enumerate(finished(weave)):
                    stage(s, a)
                    for c in done:
                        unit(c, fu + c, 8, a, pair)

            M, G = 2 * P_MOBA, 2 * P_GDN
            for c in range(8):
                pair_unit(c, M + c, 8, 0, 0)
            dve.wait_ge(gc_act, 1)
            gcs = mb[:, 0:32].rearrange("p (v c h) -> p v c h", v=2, c=2)
            TT(g_all[:, 3, :, :], g_all[:, 3, :, :], g_all[:, 0, :, :], ALU.mult)
            TT(g_all[:, 6, :, :], gcs[:, 1], g_all[:, 1, :, :], ALU.subtract).then_inc(gc_ready, 1)
            for i in rounds(dve, 3, ch, 4):
                pair_round(MOBA_WEAVE, moba_stage, pair_unit, M + 8, i, i + 1)
            pair_round(MOBA_WEAVE, moba_stage, pair_unit, M + 8, 3, 0)
            dve.wait_ge(gc_act, 2)
            prepare(0)
            exponents(0)
            pair_round(GDN_WEAVE, gdn_stage, pair_unit, G + 8, 0, 1)
            for i in rounds(dve, 2, ch, 3):
                pair_round(GDN_WEAVE, gdn_stage, pair_unit, G + 8, i + 1, i + 2)
            pair_round(GDN_WEAVE, gdn_stage, pair_unit, G + 8, 3, 0)
            out_rows(3)
            dve.wait_ge(sig_a, 1)
            for m in range(KC):
                pu = 2 * P_PROJA + m
                dve.wait_ge(unit_done, pu + 1)
                TT(ga[:, m, :], ga[:, m, :], fm[:, m % 2, 0:S], ALU.mult).then_inc(emptied[m % 2], 1)
                lo(pu + 4)
                if m == 2:
                    out_lo(3)
            dve.wait_ge(sig_b, 1)
            dve.wait_ge(emptied[0], EMPTIED0[2 * P_PROJB])
            dve.wait_ge(emptied[1], EMPTIED1[2 * P_PROJB])
            for m in range(KC):
                pu = 2 * P_PROJB + m
                dve.wait_ge(unit_done, pu + 1)
                ins = TT(gb_s[:, m, :], gb_s[:, m, :], fm[:, m % 2, 0:S], ALU.mult)
                ins.then_inc(emptied[m % 2], 1)
                dve.wait_ge(emptied[m % 2], AFTER[m % 2][pu])
                TT(gb_s[:, m, :], gb_s[:, m, :], ga[:, m, :], ALU.add).then_inc(mg_out, 1)
                lo(pu + 4)
            for q in range(2):
                dve.wait_ge(mg_hi, q + 1)
                TT(yTl[:, 4 * q:4 * q + 4, :], gb_s[:, 4 * q:4 * q + 4, :], yTh[:, 4 * q:4 * q + 4, :].bitcast(F32), ALU.subtract).then_inc(mg_lo, 1)
            for n in range(8):
                lo(2 * P_OUT2 + n + 4)
            residual(6, 5)
            norm_rows(7, h, 6, 0, 7)
            norm_lo(7, 0)
            F2 = 2 * P_FF2

            def gate_units(fu, stride=0, i=0):
                for j in range(2):
                    lo(fu + j + 4, stride, i)

            def hid2_mul(fu, stride=0, i=0, k=0):
                for j in range(2):
                    n = i * (stride // 3) + 2 * k + j + 1
                    dve.wait_ge(swi_a, n)
                    dve.wait_ge(unit_done, i * stride + (fu + j + 1))
                    if k:
                        dve.wait_ge(swi_lo, n - 2)
                    TT(hid2[:, j, :], gate_s[:, j, :], (ma, mb)[j][:, 0:S], ALU.mult).then_inc(swi_m, 1)
                    lo(fu + j + 4, stride, i)
                for j in range(2):
                    n = i * (stride // 3) + 2 * k + j + 1
                    dve.wait_ge(swi_hi, n)
                    TT(hid2_l[:, j, :], hid2[:, j, :], hid2_h[:, j, :].bitcast(F32), ALU.subtract).then_inc(swi_lo, 1)

            gate_units(F2)
            hid2_mul(F2 + 2)
            for i in rounds(dve, 4):
                for n in range(2):
                    gate_units(F2 + 4 + 6 * n, 12, i)
                    acc_units(F2 + 6 + 6 * n, 12, i)
                    hid2_mul(F2 + 8 + 6 * n, 12, i, n + 1)
            for n in range(2):
                gate_units(F2 + 52 + 6 * n)
                acc_units(F2 + 54 + 6 * n)
                hid2_mul(F2 + 56 + 6 * n, 0, 0, n + 9)
            acc_units(F2 + 64)
            residual(8, 7)
            dve.wait_ge(ut_hi, 10)
            TT(xTl[:, 0:2, 0:S].rearrange("p k (t n) -> p t k n", t=2), ma[:, :].rearrange("p (t k n) -> p t k n", t=2, k=2),
               xTh[:, 0:2, 0:S].rearrange("p k (t n) -> p t k n", t=2).bitcast(F32), ALU.subtract).then_inc(ut_lo, 1)
            for n in range(2):
                lo(2 * P_PLE + n + 4)
            dve.wait_ge(stat, 9)
            link(dve.reciprocal(st[:, 4:6], st[:, 4:6]))
            dve.wait_ge(gain_loaded[0], 16 * 5)
            for t in range(NT):
                STT(e_row[:, t, :], acc[:, 2 * t:2 * t + 2, :].rearrange("p b n -> p (b n)"), st[:, 4 + t:5 + t], gain[:, 0, :],
                    ALU.mult, ALU.mult).then_inc(e_out, 1)
            norm_lo(10, 0)
            for n in range(8):
                lo(2 * P_PGATE + n + 4)
            for t in range(NT):
                dve.wait_ge(fin_sig, t + 1)
                dve.wait_ge(e_out, t + 1)
                link(TT(u[:, t, :], u[:, t, :], e_row[:, t, :], ALU.mult))
                TT(u[:, t, :], u[:, t, :], h[:, t, :], ALU.add).then_inc(fin_out, 1)

        @block.tensor
        def _(pe):
            mm = pe.matmul

            def unit_ready(pu, stride=0, i=0):
                pe.wait_ge(w_lo, i * stride + (pu + 1))

            def bank_ready(j, pu, stride=0, i=0):
                n = along((EMPTIED0, EMPTIED1)[j], pu, stride, i)
                if not isinstance(n, int) or n > 0:
                    pe.wait_ge(emptied[j], n)

            def three(out, wh_, wl_, xh, xl, first, last):
                mm(out, wh_, xh, start=first, stop=False)
                mm(out, wh_, xl, start=False, stop=False)
                return mm(out, wl_, xh, start=False, stop=last)

            def three_tok(out, xh, xl, wh_, wl_, first, last, group=True):
                mm(out, xh, wh_, start=first, stop=False, skip_group_check=not group)
                mm(out, xh, wl_, start=False, stop=False, skip_group_check=not group)
                return mm(out, xl, wh_, start=False, stop=last, skip_group_check=not group)

            def fm_steps(pu, xh, xl, off, n, col=0, stride=0, i=0):
                unit_ready(pu, stride, i)
                bank_ready(pu % 2, pu, stride, i)
                a, b = (split_view(w, pu % UNITS, "cols") for w in (wh, wl))
                for k in range(KC):
                    last = three(fm[:, pu % 2, col:col + n], a[:, k, :], b[:, k, :], xh[:, k, off:off + n], xl[:, k, off:off + n],
                                 k == 0, k == KC - 1)
                    if k == KC - 1:
                        last.then_inc(unit_done, 1)
                    yield

            def tok_steps(pu, off, stride=0, i=0):
                unit_ready(pu, stride, i)
                j = pu % 2
                if j == 0:
                    bank_ready(0, pu, stride, i)
                    bank_ready(1, pu, stride, i)
                a, b = (w[:, pu % UNITS, :].rearrange("p (k n) -> p k n", k=4) for w in (wh, wl))
                for kk in range(4):
                    for t in range(NT):
                        k = 4 * j + kk
                        last = three_tok(fm[:, t, 0:S], xTh[:, k, off + t * P:off + (t + 1) * P], xTl[:, k, off + t * P:off + (t + 1) * P],
                                         a[:, kk, :], b[:, kk, :], k == 0, k == KC - 1)
                        if kk == 3 and t == NT - 1:
                            last.then_inc(unit_done, 1)
                        yield

            def run(steps):
                for _ in steps:
                    pass

            def acc_unit(pu, xh, xl, first, last_, stride=0, i=0):
                unit_ready(pu, stride, i)
                a, b = wh[:, pu % UNITS, :], wl[:, pu % UNITS, :]
                for t in range(NT):
                    for half in range(2):
                        last = three_tok(acc[:, 2 * t + half, :], xh[:, t * P:(t + 1) * P], xl[:, t * P:(t + 1) * P],
                                         a[:, half * 512:(half + 1) * 512], b[:, half * 512:(half + 1) * 512], first, last_, group=False)
                last.then_inc(unit_done, 1)

            def transposes(base, u_base, rows_):
                for t in range(NT):
                    pe.wait_ge(u_ready, u_base + t + 1)
                    for k in range(KC):
                        last = pe.transpose(acc[:, 2 * t + k // 4, (k % 4) * P:(k % 4 + 1) * P], rows_[:, t, k * P:(k + 1) * P], ident)
                    last.then_inc(ut_ps, 1)

            pe.wait_ge(cst_loaded, 16)
            pe.wait_ge(u_ready, 1)
            for k in range(KC):
                last = pe.transpose(ma[:, k * META:(k + 1) * META], meta[0:META, k * P:(k + 1) * P], ident[0:META, 0:META])
            last.then_inc(ut_ps, 1)
            transposes(1, 1, u)
            pe.wait_ge(ut_lo, 3)
            run(fm_steps(0, xTh, xTl, 0, T1))
            unit_ready(1)
            a, b = (split_view(w, 1, "cols") for w in (wh, wl))
            for t, (off, n) in enumerate(((META, P), (META + P, P), (0, META))):
                for k in range(KC):
                    last = three_tok(ma[0:n, t * P:(t + 1) * P], xTh[:, k, off:off + n], xTl[:, k, off:off + n], a[:, k, :], b[:, k, :],
                                     k == 0, k == KC - 1)
            last.then_inc(unit_done, 1)
            for m in range(LT):
                run(fm_steps(2 + m, xTh, xTl, 0, T1))
            for m in range(2):
                run(fm_steps(6 + m, xTh, xTl, META, S))
            pe.wait_ge(small3, 64)
            pe.wait_ge(v1_out, 1)
            for m in range(LT):
                pe.wait_ge(xc_ready, m // 2 + 1)
                if m >= 2:
                    pe.wait_ge(r_act, m - 1)
                mm(acc[:, m, 0:T1], wa_bd[:, m, :], xc[:, m, :], start=True, stop=True)
                mm((ma, mb)[m % 2][:, 0:T1], wx_bd[:, m, :], xc[:, m, :], start=True, stop=True).then_inc(r_ps, 1)
            for m in range(4):
                run(fm_steps(8 + m, xTh, xTl, META, S))
            for m in range(2):
                run(fm_steps(12 + m, xTh, xTl, META, S))
            pe.wait_ge(r_act, LT)
            pe.wait_ge(emptied[0], EMPTIED0[12])
            pe.wait_ge(emptied[1], EMPTIED1[12])
            for b in range(2):
                nk, k0 = ((P + META, 0), (2 * P, META))[b]
                if b:
                    pe.wait_ge(p1T_out, 2 * b)
                for hh in range(QH):
                    at_ = (hh % 2) * 4 + hh // 2
                    part = slice(64 * (hh % 2), 64 * (hh % 2) + 64)
                    last = mm(acc[:, at_ // 2, (at_ % 2) * 256:(at_ % 2) * 256 + nk], qT1[part, hh // 2, b * P:(b + 1) * P],
                              kT1[part, hh // 4, k0:k0 + nk], start=True, stop=True)
                last.then_inc(s1_ps, 1)
                chunks = (((0, META, 2), (META, P, 0)), ((0, P, 0), (P, P, 1)))[b]
                pe.wait_ge(s1_exp, QH * (b + 1))
                for hh in range(QH):
                    for c, (at, n, _) in enumerate(chunks):
                        last = pe.transpose(acc[0:n, hh // 2, (hh % 2) * 256 + c * P:(hh % 2) * 256 + c * P + P], p1[:, hh, at:at + n], ident)
                    if hh % 4 == 3:
                        last.then_inc(p1T_ps, 1)
                pe.wait_ge(p1T_out, 2 * b + 2)
                if b:
                    pe.wait_ge(o1_out, b)
                for hh in range(QH):
                    at_ = (hh % 2) * 4 + hh // 2
                    kv = slice(64 * (hh // 4), 64 * (hh // 4) + 64)
                    for c, (at, n, vt) in enumerate(chunks):
                        last = mm(ma[:, hh * HD1:(hh + 1) * HD1], pT1[0:n, at_, c, :], v1[0:n, vt, kv], start=c == 0, stop=c == 1)
                last.then_inc(o1_ps, 1)
                pe.wait_ge(o1_out, b + 1)
                if b:
                    pe.wait_ge(o1T_lo, b)
                for k in range(4):
                    last = pe.transpose(mb[:, k * P:(k + 1) * P], o1[:, k * P:(k + 1) * P], ident)
                last.then_inc(o1T_ps, 1)
            pe.wait_ge(rec_lo, 1)
            pe.wait_ge(o1T_lo, 2)
            for n in range(8):
                k = (4 + n) % 8
                acc_unit(2 * P_OUT1 + n, yTh[:, k, :], yTl[:, k, :], n == 0, n == 7)
            transposes(3, 3, u)
            pe.wait_ge(ut_lo, 5)

            F = 2 * P_FF1

            def ffn1_up(fu, stride=0, i=0):
                for j in range(2):
                    run(fm_steps(fu + j, xTh, xTl, 0, S, stride=stride, i=i))

            def ffn1_down(fu, par, n0, stride=0, i=0, last_=False):
                pe.wait_ge(hid_lo, i * (stride // 2) + 2 * n0 + 2)
                for j in range(2):
                    acc_unit(fu + j, hid_h[:, par, j, :], hid_l[:, par, j, :], False, last_ and j == 1, stride, i)

            def open_acc():
                for q in range(4):
                    mm(acc[:, q, :], zero_r[:, :], junk0, start=True, stop=False, skip_group_check=True)

            junk0 = cst[:, 0:512]
            open_acc()
            ffn1_up(F)
            for i in rounds(pe, 7):
                ffn1_up(F + 2, 8, i)
                ffn1_down(F + 4, 0, 0, 8, i)
                ffn1_up(F + 6, 8, i)
                ffn1_down(F + 8, 1, 1, 8, i)
            ffn1_up(F + 58)
            ffn1_down(F + 60, 0, 14)
            ffn1_down(F + 62, 1, 15, last_=True)
            transposes(5, 5, u)
            pe.wait_ge(ut_lo, 7)
            pe.wait_ge(ab_lo, 1)
            for t in range(NT):
                for k in range(KC):
                    last = three_tok(ma[:, t * 16:(t + 1) * 16], xTh[:, k, t * P:(t + 1) * P], xTl[:, k, t * P:(t + 1) * P],
                                     ab_h[:, k, :], ab_l[:, k, :], k == 0, k == KC - 1)
            last.then_inc(ab_ps, 1)
            M, G = 2 * P_MOBA, 2 * P_GDN

            def pair_steps(kinds, fu, stride, i):
                for c in range(8):
                    if kinds[c] == "t":
                        yield from tok_steps(fu + c, 0, stride, i)
                    else:
                        yield from fm_steps(fu + c, xTh, xTl, 0, S, stride=stride, i=i)

            run(pair_steps("ffffff" + "tt", M, 0, 0))
            pe.wait_ge(g_ready, 1)
            for c in range(2):
                mm(mb[:, c * 8:(c + 1) * 8], tri, g_all[:, 5, c, :], start=True, stop=True)
            for c in range(2):
                last = mm(mb[:, 16 + c * 8:16 + (c + 1) * 8], ones[:, :], g_all[:, 5, c, :], start=True, stop=True)
            last.then_inc(gc_ps, 1)

            def moba_stage(s, a):
                if s == 1:
                    pe.wait_ge(rope_out, a + 1)
                    for j in range(2):
                        mm(acc[:, j, 0:256], qr[:, j, P:2 * P], qr[:, 2 + j, :], start=True, stop=True)
                        last = mm(acc[:, j, 256:384], qr[:, j, 0:P], qr[:, 2 + j, 0:P], start=True, stop=True)
                    last.then_inc(s2_ps, 1)
                if s == 3:
                    pe.wait_ge(s2_p, a + 1)
                    for j in range(2):
                        for c in range(3):
                            last = pe.transpose(acc[:, 2 + j, c * P:(c + 1) * P], p2[:, j, c * P:(c + 1) * P], ident)
                    last.then_inc(p2T_ps, 1)
                if s == 4:
                    pe.wait_ge(p2T_a, a + 1)
                    pe.wait_ge(p2T_v, a + 1)
                    for j in range(2):
                        hd = slice(j * P, (j + 1) * P)
                        mm(ma[:, j * 256:j * 256 + P], va[:, 0, hd], pT2[:, j, 256:384], start=True, stop=True)
                        mm(ma[:, j * 256 + P:(j + 1) * 256], va[:, 0, hd], pT2[:, j, 0:P], start=True, stop=False)
                        last = mm(ma[:, j * 256 + P:(j + 1) * 256], va[:, 1, hd], pT2[:, j, P:2 * P], start=False, stop=True)
                    last.then_inc(o2_ps, 1)

            def gdn_stage(s, a):
                if s == 1:
                    for n, q in enumerate((1, 0)):
                        pe.wait_ge(sq_out, a * 2 + (n + 1))
                        mm(acc[:, q, :], ones[:, :], sq[:, q * 512:(q + 1) * 512], start=True, stop=True).then_inc(ssq_ps, 1)
                if s == 2:
                    for pr in range(4):
                        c, j = pr // 2, pr % 2
                        last = pe.transpose(acc[:, 3, pr * P:(pr + 1) * P], cv[:, 4 + j, c * P:(c + 1) * P], ident)
                    last.then_inc(vT_ps, 1)
                if s == 3:
                    pe.wait_ge(qkn_out, a * 2 + 2)
                    for pr in range(4):
                        c, j = pr // 2, pr % 2
                        k = cv[:, 2 + j, c * P:(c + 1) * P]
                        last = mm(acc[:, 1, pr * P:(pr + 1) * P], k, k, start=True, stop=True)
                    last.then_inc(kk_ps, 1)
                    for pr in range(4):
                        c, j = pr // 2, pr % 2
                        last = pe.transpose(acc[:, 0, pr * P:(pr + 1) * P], cv[:, 2 + j, c * P:(c + 1) * P], ident)
                    last.then_inc(kT_ps, 1)
                    for pr in range(4):
                        c, j = pr // 2, pr % 2
                        last = mm(acc[:, 2, pr * P:(pr + 1) * P], cv[:, 2 + j, c * P:(c + 1) * P], cv[:, j, c * P:(c + 1) * P], start=True, stop=True)
                    last.then_inc(kq_ps, 1)
                if s == 4:
                    pe.wait_ge(x0_out, a + 1)
                    pe.wait_ge(vb_out, a + 1)
                    for pr in range(4):
                        last = pe.transpose(acc[:, 3, pr * P:(pr + 1) * P], X_[:, pr, :], ident)
                    last.then_inc(xt0_ps, 1)
                if 5 <= s < 17 and s % 2 == 1:
                    lv = (s - 5) // 2 + 1
                    if lv == 1:
                        pe.wait_ge(xt0_out, a + 1)
                        pe.wait_ge(kv_out, a + 1)
                        pe.wait_ge(attn_out, a + 1)
                    for g in range(2):
                        if lv > 1:
                            pe.wait_ge(lv_xt[g], a * 6 + (lv - 1))
                        for j in range(2):
                            last = mm(acc[:, 3 * g, j * P:(j + 1) * P], A_[:, 2 * g + j, :], XT_[:, 2 * g + j, :], start=True, stop=True)
                        last.then_inc(lv_p[g], 1)
                if 5 <= s < 17 and s % 2 == 0:
                    lv = (s - 5) // 2 + 1
                    for g in range(2):
                        pe.wait_ge(lv_pm[g], a * 6 + lv)
                        if lv > 1:
                            pe.wait_ge(lv_x[g], a * 5 + (lv - 1))
                        for j in range(2):
                            pr = 2 * g + j
                            last = mm(acc[:, 1 + g, j * P:(j + 1) * P], X_[:, pr, :], PM_[:, pr, :], start=True, stop=True)
                        if lv < 6:
                            for j in range(2):
                                pr = 2 * g + j
                                last = mm(acc[:, 1 + g, (2 + j) * P:(3 + j) * P], PM_[:, pr, :], X_[:, pr, :], start=True, stop=True)
                        last.then_inc(lv_z[g], 1)
                if s == 17:
                    for g in range(2):
                        pe.wait_ge(lv_xt[g], a * 6 + 6)
                    for j in range(2):
                        mm(acc[:, 3, j * P:(j + 1) * P], XT_[:, j, :], vb[:, j, :], start=True, stop=True)
                    for j in range(2):
                        last = mm(acc[:, 0, j * P:(j + 1) * P], kbe[:, j, :], XT_[:, 2 + j, :], start=True, stop=True)
                    last.then_inc(uw_ps, 1)
                if s == 18:
                    pe.wait_ge(u0_out, a + 1)
                    for j in range(2):
                        last = mm(acc[:, 1, j * P:(j + 1) * P], kdec[:, j, :], u0[:, j, :], start=True, stop=True)
                    last.then_inc(so_ps, 1)
                    for j in range(2):
                        mm(acc[:, 2, j * P:(j + 1) * P], attnT[:, j, :], u0[:, j, :], start=True, stop=True)
                if s == 19:
                    pe.wait_ge(S1_out, a + 1)
                    pe.wait_ge(nw_out, a + 1)
                    for j in range(2):
                        out = acc[:, 3, (2 + j) * P:(3 + j) * P]
                        mm(out, XT_[:, 2 + j, :], vb[:, 2 + j, :], start=True, stop=False)
                        last = mm(out, nwT[:, j, :], S1[:, j, :], start=False, stop=True)
                    last.then_inc(vn_ps, 1)
                if s == 20:
                    pe.wait_ge(vn_out, a + 1)
                    for j in range(2):
                        out = acc[:, 2, (2 + j) * P:(3 + j) * P]
                        mm(out, qeg[:, j, :], S1[:, j, :], start=True, stop=False)
                        last = mm(out, attnT[:, 2 + j, :], vn[:, j, :], start=False, stop=True)
                    last.then_inc(o_ps, 1)
                if s == 9 and not (isinstance(a, int) and a == PAIRS - 1):
                    g_rows(a + 1)
                if s == 13 and not (isinstance(a, int) and a == 0):
                    out_transposes(a - 1)

            def g_rows(b):
                pe.wait_ge(gb_out, b + 1)
                for pr in range(4):
                    last = mm(mb[:, pr * P:(pr + 1) * P], gb[:, pr, :], tri, start=True, stop=True)
                last.then_inc(gcb_ps, 1)

            def out_transposes(b):
                pe.wait_ge(y_out, b + 1)
                for pr in range(4):
                    last = pe.transpose(ma[:, pr * P:(pr + 1) * P], y_[:, pr, :], ident)
                last.then_inc(yT_ps, 1)

            def pair_round(weave, stage, kinds, fu, a):
                steps = pair_steps(kinds, fu, 8, a)
                for s, n in enumerate(weave):
                    stage(s, a)
                    for _ in range(n):
                        next(steps)

            for i in rounds(pe, 3):
                pair_round(MOBA_WEAVE, moba_stage, "fffffftt", M + 8, i)
            pair_round(MOBA_WEAVE, moba_stage, "fffffftt", M + 8, 3)
            g_rows(0)
            pair_round(GDN_WEAVE, gdn_stage, "fffffftt", G + 8, 0)
            for i in rounds(pe, 2):
                pair_round(GDN_WEAVE, gdn_stage, "fffffftt", G + 8, i + 1)
            pair_round(GDN_WEAVE, gdn_stage, "ffffffff", G + 8, 3)
            pe.wait_ge(o2_lo, PAIRS)
            for m in range(KC):
                run(fm_steps(2 * P_PROJA + m, yTh, yTl, 0, S))
                if m == 1:
                    out_transposes(3)
            pe.wait_ge(yb_lo, PAIRS)
            for m in range(KC):
                run(fm_steps(2 * P_PROJB + m, ybh, ybl, 0, S))
            for k in range(KC):
                pe.wait_ge(mg_lo, k // 4 + 1)
                acc_unit(2 * P_OUT2 + k, yTh[:, k, :], yTl[:, k, :], k == 0, k == KC - 1)
            transposes(7, 7, u)
            pe.wait_ge(ut_lo, 9)
            F2 = 2 * P_FF2

            def slice_up(fu, banks, read, need, stride=0, i=0):
                for j in range(2):
                    unit_ready(fu + j, stride, i)
                    if need is not None:
                        pe.wait_ge(read, i * (stride // 3) + need + j)
                    a, b = (split_view(w, (fu + j) % UNITS, "cols") for w in (wh, wl))
                    for k in range(KC):
                        last = three(banks[j], a[:, k, :], b[:, k, :], xTh[:, k, 0:S], xTl[:, k, 0:S], k == 0, k == KC - 1)
                    last.then_inc(unit_done, 1)

            def ffn2_down(fu, k, stride=0, i=0, last_=False):
                pe.wait_ge(swi_lo, i * (stride // 3) + 2 * k + 2)
                for j in range(2):
                    acc_unit(fu + j, hid2_h[:, j, :], hid2_l[:, j, :], False, last_ and j == 1, stride, i)

            pe.wait_ge(emptied[0], EMPTIED0[F2])
            pe.wait_ge(emptied[1], EMPTIED1[F2])
            open_acc()
            gates, ups = (fm[:, 0, 0:S], fm[:, 1, 0:S]), (ma[:, 0:S], mb[:, 0:S])
            slice_up(F2, gates, swi_a, None)
            slice_up(F2 + 2, ups, swi_m, None)
            for i in rounds(pe, 5):
                for n in range(2):
                    slice_up(F2 + 4 + 6 * n, gates, swi_a, 2 * n + 1, 12, i)
                    ffn2_down(F2 + 6 + 6 * n, n, 12, i)
                    slice_up(F2 + 8 + 6 * n, ups, swi_m, 2 * n + 1, 12, i)
            ffn2_down(F2 + 64, 10, last_=True)
            pe.wait_ge(p_loaded, 16)
            for t in range(NT):
                for k in range(2):
                    last = pe.transpose(ma[:, (2 * t + k) * P:(2 * t + k + 1) * P], p_in[:, t, k * P:(k + 1) * P], ident)
            last.then_inc(ut_ps, 1)
            pe.wait_ge(ut_lo, 10)
            pe.wait_ge(h_ready, 8)
            for k in range(2):
                acc_unit(2 * P_PLE + k, xTh[:, k, 0:S], xTl[:, k, 0:S], k == 0, k == 1)
            pe.wait_ge(e_out, NT)
            for t in range(NT):
                for k in range(KC):
                    last = pe.transpose(acc[:, 2 * t + k // 4, (k % 4) * P:(k % 4 + 1) * P], h[:, t, k * P:(k + 1) * P], ident)
                last.then_inc(ut_ps, 1)
            pe.wait_ge(ut_lo, 12)
            for k in range(KC):
                acc_unit(2 * P_PGATE + k, xTh[:, k, 0:S], xTl[:, k, 0:S], k == 0, k == KC - 1)


_INS = ["x", "meta_tokens", "g_pre_mix", "w_in", "conv_w", "conv_b", "w_a", "b_a", "w_x", "b_x", "lru_lambda",
        "attn_sinks", "w_out", "g_post_mix", "g_pre_ffn", "w_ff1", "w_ff2", "g_post_ffn", "p_2", "ln_pre_mix_2",
        "w_in_2", "conv_w_2", "a_log_2", "dt_bias_2", "gdn_norm_2", "w_proj_a_2", "w_proj_b_2", "w_out_2",
        "ln_post_mix_2", "ln_pre_ffn_2", "w_ffn_gate_2", "w_ffn_up_2", "w_ffn_down_2", "ln_post_ffn_2", "w_ple_2",
        "ln_ple_2", "w_ple_gate_2"]


def kernel(**inputs):
    import concourse.bacc as _bacc
    from concourse.bass_utils import run_bass_kernel_spmd as _run

    nc = _bacc.Bacc("TRN2", target_bir_lowering=False, num_devices=1)
    arrays, aps = {}, {}
    for name in _INS:
        a = np.ascontiguousarray(inputs[name])
        arrays[f"in_{name}_dram"] = a
        aps[name] = nc.dram_tensor(f"in_{name}_dram", a.shape, mybir.dt.from_np(a.dtype), kind="ExternalInput").ap()
    table = constant_table()
    arrays["constants_dram"] = table
    aps["cst"] = nc.dram_tensor("constants_dram", table.shape, F32, kind="ExternalInput").ap()
    aps["out"] = nc.dram_tensor("out_0_dram", (1, S, D), F32, kind="ExternalOutput").ap()
    build(nc, aps)
    r = _run(nc, [arrays], core_ids=[0])
    return r.results[0]["out_0_dram"]
```

```python
from contextlib import ExitStack

import numpy as np

import concourse.bass as bass
from concourse import mybir

F32 = mybir.dt.float32
F32R = mybir.dt.float32r
ALU = mybir.AluOpType
ACT = mybir.ActivationFunctionType
AX = mybir.AxisListType.X

P = 128
D = 1024
KC = D // P
S = 256
META = 16
T1 = S + META
NT = S // P
EPS = 1e-6
NEG = -1e30
QH, KVH, HD1 = 8, 2, 64
WINDOW = 128
LRU = 512
LT = LRU // P
FF1_TILES = 16
HEADS2 = 8
PAIRS = HEADS2 // 2
LEVELS = 7
FF2_TILES = 11
PLE = 256
REGION = 16128
SC1 = HD1 ** -0.5
SC2 = P ** -0.5
IN2_Q, IN2_K, IN2_V, IN2_CONV, IN2_Z, IN2_B, IN2_GA, IN2_GB = (
    0, 1024, 2048, 3072, 6144, 7168, 7184, 8208)

C_IDENT, C_TRI, C_MUP, C_MLOW, C_LEV, C_MOBA, C_WIN0, C_WIN1, C_COS, C_SIN, C_END = (
    0, 128, 256, 384, 512, 1408, 1792, 1936, 2192, 2448, 2704)


def constant_table():
    c = np.zeros((P, C_END), np.float32)
    r, k = np.arange(P)[:, None], np.arange(P)[None, :]
    c[:, C_IDENT:C_TRI] = r == k
    c[:, C_TRI:C_MUP] = r <= k
    c[:, C_MUP:C_MLOW] = np.where(r <= k, 0.0, NEG)
    c[:, C_MLOW:C_LEV] = np.where(k < r, 0.0, NEG)
    for n in range(LEVELS):
        b = 1 << n
        low = (r // (2 * b) == k // (2 * b)) & (r % (2 * b) >= b) & (k % (2 * b) < b)
        at = C_LEV + n * P
        if n:
            c[:, at:at + P] = low.T
        else:
            c[:, at:at + P // 2] = low[:, 0::2]
    diag = np.where(k <= r, 0.0, NEG)
    c[:, C_MOBA + P:C_MOBA + 2 * P] = diag
    c[:, C_MOBA + 2 * P:C_MOBA + 3 * P] = diag
    k0 = np.arange(P + META)[None, :]
    gap = META + r - k0
    c[:, C_WIN0:C_WIN1] = np.where((gap >= 0) & (gap < WINDOW), 0.0, NEG)
    gap = P + r - np.arange(2 * P)[None, :]
    c[:, C_WIN1:C_COS] = np.where((gap >= 0) & (gap < WINDOW), 0.0, NEG)
    half = P // 2
    inv = (1.0 / (np.float32(10000.0) ** (np.arange(0, P, 2, dtype=np.float32) / np.float32(P)))).astype(np.float32)
    ang = (np.arange(S, dtype=np.float32)[None, :] * inv[:, None]).astype(np.float32)
    c[:half, C_COS:C_SIN] = c[half:, C_COS:C_SIN] = np.cos(ang)
    c[:half, C_SIN:C_END] = -np.sin(ang)
    c[half:, C_SIN:C_END] = np.sin(ang)
    return c


RING = 4
UNITS = 4
(P_KV, P_Q, P_XR, P_YR, P_OUT1, P_FF1, P_MOBA, P_GDN, P_GATEB, P_PROJA, P_PROJB, P_OUT2, P_PLE, P_FF2,
 P_PGATE, P_ALL) = (0, 1, 3, 5, 7, 11, 43, 59, 75, 79, 83, 87, 91, 92, 125, 129)


GATE_UNIT = 2 * P_YR + 2


def panel_plan():
    plan = [("cols", "kv")] + [("cols", "fm")] * 6 + [("rows", "acc")] * 4
    plan += [("cols", "fm")] + [("cols", "fm"), ("rows", "acc")] * 15 + [("rows", "acc")]
    plan += ([("cols", "fm")] * 3 + [("rows", "tok")]) * PAIRS
    plan += ([("cols", "fm")] * 3 + [("rows", "tok")]) * PAIRS
    plan += [("cols", "fm")] * 12 + [("rows", "acc")] * 4 + [("rows", "high")]
    plan += [("cols", "fm")] * 2 + [("cols", "fm"), ("rows", "acc"), ("cols", "fm")] * 10 + [("rows", "acc")]
    plan += [("rows", "acc")] * 4
    assert len(plan) == P_ALL
    return plan


PLAN = panel_plan()
SLOT = [p % RING if p < P_FF2 else (0, 1, 3)[(p - P_FF2) % 3] if p < P_PGATE else (p - P_PGATE) % RING for p in range(P_ALL)]
LOADS = [16 * sum(SLOT[q] == SLOT[p] for q in range(p + 1)) for p in range(P_ALL)]
REUSE = [max((q for q in range(p) if SLOT[q] == SLOT[p]), default=-1) for p in range(P_ALL)]


def bank_counts():
    n, before = [0, 0], []
    for layout, to in PLAN:
        for j in range(2):
            if len(before) == GATE_UNIT:
                n = [n[0] + LT // 2, n[1] + LT // 2]
            before.append(tuple(n))
            if to == "fm":
                n[j] += 1
            elif to == "kv" and j == 0:
                n[0] += 1
            elif to in ("tok", "high") and j == 1:
                n[0] += 1
                n[1] += 1
    return before


EMPTIED = bank_counts()
AFTER = [[EMPTIED[min(n + 1, 2 * P_ALL - 1)][b] for n in range(2 * P_ALL)] for b in range(2)]
EMPTIED0 = [e[0] for e in EMPTIED] + [0] * 64
EMPTIED1 = [e[1] for e in EMPTIED] + [0] * 64


def along(table, at, stride, i):
    if isinstance(i, int):
        return table[at + stride * i]
    step = table[at + stride] - table[at]
    assert table[at + 2 * stride] - table[at + stride] == step
    return i * step + table[at]


class Chain:

    def __init__(self, eng, sem):
        self.eng, self.sem, self.n, self.links = eng, sem, 0, 0

    def mark(self, ins):
        ins.then_inc(self.sem, 1)
        self.n, self.links = self.n + 1, self.links + 1

    def wait(self):
        self.eng.wait_ge(self.sem, self.n)

    def link(self, ins):
        self.mark(ins)
        self.wait()


def rounds(eng, n, chain=None, per=0):
    base, links = (chain.n, chain.links) if chain else (0, 0)
    with eng.Fori(0, n) as i:
        if chain:
            chain.n = i * per + base
        yield i
    if chain:
        assert chain.links - links == per, chain.links - links
        chain.n = base + n * per


MOBA_WEAVE = [18, 8, 16, 8, 14]
GDN_WEAVE = [9, 8, 4, 6, 4] + [1] * 12 + [4, 3, 3, 11]
assert sum(MOBA_WEAVE) == 64 and sum(GDN_WEAVE) == 64


def finished(weave):
    done, out = 0, []
    for n in weave:
        out.append(range(done // 8, (done + n) // 8))
        done += n
    return out


def build(nc, A):
    ctx = ExitStack()
    with ctx:
        def sb(name, shape, dt=F32):
            return ctx.enter_context(nc.sbuf_tensor(name, shape, dt))

        def sem(name):
            return ctx.enter_context(nc.semaphore(name))

        ps = ctx.enter_context(nc.psum_tensor("ps", [P, 8, 512], F32))
        acc, fm, ma, mb = ps[:, 0:4, :], ps[:, 4:6, :], ps[:, 6, :], ps[:, 7, :]
        high = ps[:, 4:8, :]

        w_raw = sb("w_raw", [P, RING, 2048])
        wh = sb("wh", [P, UNITS, 1024], F32R)
        wl = sb("wl", [P, UNITS, 1024], F32R)
        h = sb("h", [P, NT, D])
        xTh = sb("xTh", [P, KC, T1], F32R)
        xTl = sb("xTl", [P, KC, T1], F32R)
        yTh = sb("yTh", [P, KC, S], F32R)
        yTl = sb("yTl", [P, KC, S], F32R)
        y2 = sb("y2", [P, 2 * KC * S], F32R)
        gain = sb("gain", [P, 2, D])
        cst = sb("cst", [P, C_END])
        ones = sb("ones", [P, P])
        zero_r = sb("zero_r", [P, P])
        eps = sb("eps", [P, 1])
        st = sb("st", [P, 32])
        R = sb("R", [P, REGION])

        def carve(state, *shape):
            n = int(np.prod(shape))
            a = R[:, state[0]:state[0] + n]
            state[0] += n
            assert state[0] <= REGION, state
            if len(shape) == 2:
                return a.rearrange("p (a b) -> p a b", a=shape[0])
            if len(shape) == 3:
                return a.rearrange("p (a b c) -> p a b c", a=shape[0], b=shape[1])
            return a

        c1 = [0]
        u = carve(c1, NT, D)
        meta = carve(c1, D)
        xr_pad = carve(c1, LT, T1 + 3)
        xc = carve(c1, LT, T1)
        r_g = carve(c1, LT, T1)
        i_g = carve(c1, LT, T1)
        th_ = carve(c1, LT, T1)
        a_ = carve(c1, LT, T1)
        a2 = carve(c1, LT, T1)
        gy = carve(c1, LT, S)
        qT1 = carve(c1, 4, S)
        kT1 = carve(c1, KVH, T1)
        v1 = carve(c1, 3, P)
        wa_bd = carve(c1, LT, P)
        wx_bd = carve(c1, LT, P)
        cwb = carve(c1, LT, 8)
        lam_t = carve(c1, 8, LT)
        sink = carve(c1, QH)
        p1 = R[:, 0:NT * D].rearrange("p (a b) -> p a b", a=QH)
        junk = sb("junk", [P, D])
        pT1 = [x.rearrange("p (a b c) -> p a b c", a=4, b=2) for x in (meta, junk[:, :])]
        cf = [NT * D + D]
        hid_t = carve(cf, 2, S)
        hid_q = carve(cf, 2, S)
        hid_h = y2[:, 0:4 * S].rearrange("p (a b c) -> p a b c", a=2, b=2)
        hid_l = y2[:, 4 * S:8 * S].rearrange("p (a b c) -> p a b c", a=2, b=2)
        c2 = [NT * D]
        ybh = y2[:, 0:KC * S].rearrange("p (k n) -> p k n", k=KC)
        ybl = y2[:, KC * S:2 * KC * S].rearrange("p (k n) -> p k n", k=KC)
        ga = carve(c2, KC, S)
        g_all = carve(c2, 7, 2, HEADS2)
        cw_all = carve(c2, 4, 24)
        ab_w = carve(c2, KC, 16)
        ab_h = y2[:, 0:KC * 16].rearrange("p (k n) -> p k n", k=KC)
        ab_l = y2[:, KC * 16:2 * KC * 16].rearrange("p (k n) -> p k n", k=KC)
        ab = carve(c2, 2, 16)
        dt_row = carve(c2, 2, HEADS2)
        tmp16 = carve(c2, 8, 16)
        gnorm = carve(c2, P)
        sc = carve(c2, 6, 2, 2)
        cw = carve(c2, 4, 6)
        raw = carve(c2, 6, S + 3)
        zr = carve(c2, NT, S)
        cvn = carve(c2, 6, S)
        cvt = gain[:, 0, 0:2 * S].rearrange("p (m n) -> p m n", m=2)
        c3 = [c2[0]]
        qk = carve(c3, 4, S)
        qr = carve(c3, 4, S)
        rot = carve(c3, 4, S)
        va = carve(c3, NT, S)
        sm2 = carve(c3, 2, 384)
        p2 = carve(c3, 2, 384)
        pT2 = carve(c3, 2, 384)
        c4 = [c2[0]]
        cv = carve(c4, 6, S)
        c5 = [0]
        rk = carve(c5, 4 * S)
        sq = rk
        kbe = carve(c5, 2, P)
        kdec = carve(c5, 2, P)
        vb = carve(c5, 4, P)
        dt_ = carve(c4, 4, P)
        dl_ = carve(c4, 4, P)
        eg = carve(c4, 2, P)
        attnT = carve(c4, 4, P)
        A_ = carve(c4, 4, P)
        gb = carve(c4, 4, P)
        X_ = carve(c4, 4, P)
        XT_ = carve(c4, 4, P)
        PM_ = carve(c4, 4, P)
        u0 = carve(c4, 2, P)
        nwT = carve(c4, 2, P)
        S1 = carve(c4, 2, P)
        vn = carve(c4, 2, P)
        qeg = carve(c4, 2, P)
        y_ = gb
        sz = carve(c4, NT, S)
        c6 = [c2[0]]
        gate_s = carve(c6, 2, S)
        hid2 = carve(c6, 2, S)
        hid2_h = y2[:, 0:2 * S].rearrange("p (j n) -> p j n", j=2)
        hid2_l = y2[:, 2 * S:4 * S].rearrange("p (j n) -> p j n", j=2)
        gb_s = gain[:, :, :].rearrange("p a (m n) -> p (a m) n", n=S)
        p_in = carve(c6, NT, PLE)
        pT_h = y2[:, 0:2 * S].rearrange("p (k n) -> p k n", k=2)
        pT_l = y2[:, 2 * S:4 * S].rearrange("p (k n) -> p k n", k=2)
        e_row = ga.rearrange("p a b -> p (a b)").rearrange("p (t n) -> p t n", t=NT)
        o_s = junk[:, 0:512].rearrange("p (r n) -> p r n", r=4)

        ident = cst[:, C_IDENT:C_TRI]
        tri = cst[:, C_TRI:C_MUP]

        w_loaded = [sem(f"w_loaded{n}") for n in range(RING)]
        w_hi, w_lo, unit_done = sem("w_hi"), sem("w_lo"), sem("unit_done")
        emptied = [sem("fm0_emptied"), sem("fm1_emptied")]
        x_loaded = [sem("x0_loaded"), sem("x1_loaded")]
        meta_loaded, ident_loaded = sem("meta_loaded"), sem("identity_loaded")
        cst_loaded, small1, small2 = (sem(n) for n in ("cst_loaded", "small1_loaded", "small2_loaded"))
        small3 = sem("block_diag_loaded")
        gain_loaded = [sem("gain0_loaded"), sem("gain1_loaded")]
        gain_first = sem("first_gain_loaded")
        gain_used = sem("gain_used")
        filled = sem("pool_filled")
        act_chain, dve_chain, pool_chain = sem("act_chain"), sem("dve_chain"), sem("pool_chain")
        rows0_done = sem("rows0_done")
        stat = sem("norm_root_ready")
        u_ready = sem("u_ready")
        ut_ps = sem("uT_in_psum")
        ut_hi, ut_lo = sem("uT_hi_ready"), sem("uT_lo_ready")
        h_ready = sem("h_ready")
        v1_out = sem("v1_ready")
        lam_e, sp_ready, xc_ready = sem("lam_exp_ready"), sem("softplus_ready"), sem("conv_ready")
        r_ps, tanh_out, a_out, m2_out, mult_out = (
            sem(n) for n in ("lru_gates_in_psum", "lru_tanh_ready", "lru_a_ready",
                             "lru_mult2_ready", "lru_mult_ready"))
        rec_out, rec_hi, rec_lo = sem("rec_ready"), sem("rec_hi_ready"), sem("rec_lo_ready")
        s1_ps, s1_max, s1_exp, p1T_ps, p1T_out, o1T_ps, o1T_hi, o1T_lo = (
            sem(n) for n in ("attn1_scores", "attn1_max", "attn1_exp", "attn1_pT", "attn1_pT_ready", "attn1_oT", "attn1_oT_hi", "attn1_oT_lo"))
        i_act, p_ready = sem("lru_input_gate_ready"), sem("attn1_p_ready")
        s1_sink, gelu_out = sem("attn1_sink_exp"), sem("gelu_ready")
        hid_s, hid_hi, hid_lo = (sem(n) for n in ("hid_square", "hid_hi", "hid_lo"))
        ab_sb, abT_ps = sem("ab_copied"), sem("ab_rows")
        ab_hi, ab_ps, ab_out, ab_act, g_ready, gc_ps, gc_act, gc_ready = (
            sem(n) for n in ("ab_w_hi", "ab_in_psum", "ab_ready", "ab_act", "g_ready", "gc_in_psum", "gc_exp", "gc_ready"))
        ab_lo = sem("ab_w_lo")
        rot_out, rope_out, s2_ps, s2_max, s2_exp, s2_p, p2T_ps, p2T_a, p2T_v, o2_ps, o2_hi, o2_lo = (
            sem(n) for n in ("rope_halves", "rope_ready", "moba_scores", "moba_max", "moba_exp", "moba_p", "moba_pT",
                             "moba_pT0_ready", "moba_pT1_ready", "moba_o", "moba_o_hi", "moba_o_lo"))
        cv_out, silu_out, sq_out, ssq_ps, rk_out, qkn_out, gb_out, gcb_ps, t12_out, dt_out, dl_out = (
            sem(n) for n in ("gdn_conv", "gdn_silu", "gdn_squares", "gdn_square_sums", "gdn_inv_norms", "gdn_qk_ready",
                             "gdn_g_rows", "gdn_gc_rows", "gdn_exponents", "gdn_decay_up", "gdn_decay_low"))
        vT_ps, kT_ps, kk_ps, kq_ps, attn_out, qeg_out, kv_out, A_out, inv_start, x0_out, xt0_ps, xt0_out = (
            sem(n) for n in ("gdn_v_rows", "gdn_k_rows", "gdn_kk_products", "gdn_kq_products", "gdn_attn_ready", "gdn_q_scaled", "gdn_kv_scaled", "gdn_A_ready", "inv_identity_ready",
                             "inv_x0_ready", "inv_xt0_in_psum", "inv_xt0_ready"))
        lv_p, lv_pm, lv_z, lv_x, lv_xt = ([sem(f"{n}{g}") for g in range(2)] for n in (
            "inv_p_in_psum", "inv_p_ready", "inv_z_in_psum", "inv_x_ready", "inv_xt_ready"))
        vb_out, sz_out, os_out = sem("gdn_vb_ready"), sem("gdn_gate_ready"), sem("gdn_o_copied")
        uw_ps, u0_out, nw_out, so_ps, S1_out, vn_ps, vn_out, o_ps, og_out, y_out, yT_ps, yb_hi, yb_lo = (
            sem(n) for n in ("gdn_u_w", "gdn_u0", "gdn_nwT", "gdn_state_ps", "gdn_state", "gdn_vnew_ps", "gdn_vnew",
                             "gdn_o_ps", "gdn_o_root", "gdn_y", "gdn_yT_ps", "gdn_yT_hi", "gdn_yT_lo"))
        sig_a, sig_b, mg_out, mg_hi, mg_lo = (sem(n) for n in ("gate_a_sig", "gate_b_sig", "merged", "merged_hi", "merged_lo"))
        swi_a, swi_m, swi_hi, swi_lo = (sem(n) for n in ("ffn2_silu", "ffn2_hidden", "ffn2_hid_hi", "ffn2_hid_lo"))
        p_loaded, pT_ps, pT_hi, pT_lo, e_root, e_out = (sem(n) for n in (
            "ple_loaded", "ple_pT", "ple_pT_hi", "ple_pT_lo", "ple_root", "ple_rows_ready"))
        fin_sig, fin_out, stored = sem("final_sigmoid"), sem("out_ready"), sem("out_stored")

        def raw_unit(slot, j, layout):
            if layout == "cols":
                return w_raw[:, slot, :].rearrange("p (k n) -> p k n", k=KC)[:, :, j * P:(j + 1) * P]
            return w_raw[:, slot, j * 1024:(j + 1) * 1024]

        def split_view(buf, ring, layout):
            if layout == "cols":
                return buf[:, ring, :].rearrange("p (k n) -> p k n", k=KC)
            return buf[:, ring, :]

        block = ctx.enter_context(nc.Block())

        @block.sync
        def _(sp):
            w_in, w_in2 = A["w_in"][0], A["w_in_2"][0]

            def cols(w, off, n, m):
                src = w[:, off:off + 256 * n].rearrange("(k p) (m n) -> m p k n", p=P, n=256)
                return src[bass.ds(m, 1)].rearrange("a p k n -> p (a k) n")

            def rows(w, m):
                src = w.rearrange("(m k p) n -> m p k n", k=2, p=P)
                return src[bass.ds(m, 1)].rearrange("a p k n -> p (a k) n")

            def load(p, src, stride=0, i=0):
                if isinstance(i, int):
                    last = REUSE[p + stride * i]
                    if last >= 0:
                        sp.wait_ge(w_lo, 2 * last + 2)
                else:
                    sp.wait_ge(w_lo, along([2 * q + 2 for q in REUSE], p, stride, i))
                k = 8 if src.shape[-1] == 256 else 2
                dst = w_raw[:, SLOT[p], :].rearrange("p (k n) -> p k n", k=k)
                sp.dma_start(dst, src).then_inc(w_loaded[SLOT[p]], 16)

            for t in range(NT):
                sp.dma_start(h[:, t, :], A["x"][0].rearrange("(t p) d -> t p d", p=P)[t]).then_inc(x_loaded[t], 16)
            load(P_KV, cols(w_in, 512, 1, 0))
            for m in range(2):
                load(P_Q + m, cols(w_in, 0, 2, m))
            for m in range(2):
                load(P_XR + m, cols(w_in, 768, 2, m))
            for m in range(2):
                load(P_YR + m, cols(w_in, 1280, 2, m))
            for n, m in enumerate((2, 3, 0, 1)):
                load(P_OUT1 + n, rows(A["w_out"][0], m))
            w1, w2 = A["w_ff1"][0], A["w_ff2"][0]
            load(P_FF1, cols(w1, 0, 16, 0))
            for i in rounds(sp, 7):
                load(P_FF1 + 1, cols(w1, 0, 16, i * 2 + 1), 4, i)
                load(P_FF1 + 2, rows(w2, i * 2), 4, i)
                load(P_FF1 + 3, cols(w1, 0, 16, i * 2 + 2), 4, i)
                load(P_FF1 + 4, rows(w2, i * 2 + 1), 4, i)
            load(P_FF1 + 29, cols(w1, 0, 16, 15))
            load(P_FF1 + 30, rows(w2, 14))
            load(P_FF1 + 31, rows(w2, 15))
            for i in rounds(sp, PAIRS):
                for n, off in enumerate((IN2_Q, IN2_K, IN2_GA, IN2_V)):
                    load(P_MOBA + n, cols(w_in2, off, 4, i), 4, i)
            for i in rounds(sp, PAIRS):
                for n, off in enumerate((IN2_CONV, IN2_CONV + D, IN2_CONV + 2 * D, IN2_Z)):
                    load(P_GDN + n, cols(w_in2, off, 4, i), 4, i)
            for m in range(4):
                load(P_GATEB + m, cols(w_in2, IN2_GB, 4, m))
            for n, w in enumerate((A["w_proj_a_2"][0], A["w_proj_b_2"][0])):
                for m in range(4):
                    load(P_PROJA + 4 * n + m, cols(w, 0, 4, m))
            for m in range(4):
                load(P_OUT2 + m, rows(A["w_out_2"][0], m))
            load(P_PLE, rows(A["w_ple_2"][0], 0))
            wg, wu, wd = A["w_ffn_gate_2"][0], A["w_ffn_up_2"][0], A["w_ffn_down_2"][0]
            load(P_FF2, cols(wg, 0, 11, 0))
            load(P_FF2 + 1, cols(wu, 0, 11, 0))
            for i in rounds(sp, 5):
                for n in range(2):
                    load(P_FF2 + 2 + 3 * n, cols(wg, 0, 11, i * 2 + (n + 1)), 6, i)
                    load(P_FF2 + 3 + 3 * n, rows(wd, i * 2 + n), 6, i)
                    load(P_FF2 + 4 + 3 * n, cols(wu, 0, 11, i * 2 + (n + 1)), 6, i)
            load(P_FF2 + 32, rows(wd, 10))
            for m in range(4):
                load(P_PGATE + m, rows(A["w_ple_gate_2"][0], m))
            for n in range(2 * NT):
                t, cols_ = n // 2, slice(n % 2 * 512, n % 2 * 512 + 512)
                sp.wait_ge(fin_out, n + 1)
                sp.dma_start(A["out"][0].rearrange("(t p) d -> t p d", p=P)[t][:, cols_], u[:, t, cols_]).then_inc(stored, 16)
            sp.wait_ge(stored, 32 * NT)

        GAINS = ["g_pre_mix", "g_post_mix", "g_pre_ffn", "g_post_ffn", "ln_pre_mix_2", "ln_post_mix_2",
                 "ln_pre_ffn_2", "ln_post_ffn_2", "ln_ple_2"]

        @block.gpsimd
        def _(pool):
            pool.memset(eps[:, :], EPS).then_inc(filled, 1)
            pool.memset(ones[:, :], 1.0).then_inc(filled, 1)
            pool.memset(zero_r[:, :], 0.0).then_inc(filled, 1)
            pool.memset(xr_pad[:, :, 0:3], 0.0).then_inc(filled, 1)
            pool.memset(wa_bd[:, :, :], 0.0).then_inc(filled, 1)
            pool.memset(wx_bd[:, :, :], 0.0).then_inc(filled, 1)
            pool.dma_start(cst[:, C_TRI:C_END], A["cst"][:, C_TRI:C_END]).then_inc(cst_loaded, 16)
            pool.dma_start(gain[:, 1, :], A[GAINS[1]][0].partition_broadcast(P)).then_inc(gain_loaded[1], 16)
            with nc.allow_non_contiguous_dma(reason="per-channel vectors"):
                for tap in range(4):
                    pool.dma_start(cwb[:, :, tap], A["conv_w"][0, tap].rearrange("(m p) -> p m", p=P)).then_inc(small1, 16)
                for n, name in enumerate(("conv_b", "b_a", "b_x", "lru_lambda")):
                    pool.dma_start(cwb[:, :, 4 + n], A[name][0].rearrange("(m p) -> p m", p=P)).then_inc(small1, 16)
                for b in range(2):
                    sinks = A["attn_sinks"][0].rearrange("(m b) -> b m", b=2)[b].partition_broadcast(P)
                    pool.dma_start(sink[:, 4 * b:4 * b + 4], sinks).then_inc(small1, 16)
            pool.wait_ge(filled, 6)
            for dst, name in ((wa_bd, "w_a"), (wx_bd, "w_x")):
                src = A[name][0].rearrange("(m b) c d -> b c m d", b=2)
                for b in range(2):
                    pool.dma_start(dst[64 * b:64 * b + 64, :, 64 * b:64 * b + 64], src[b]).then_inc(small3, 16)
            def gain_free(n):
                if n % 2 == 0:
                    pool.wait_ge(u_ready, n + 1)
                else:
                    pool.wait_ge(gain_used, n // 2)

            for n in range(2, 5):
                gain_free(n)
                pool.dma_start(gain[:, n % 2, :], A[GAINS[n]][0].partition_broadcast(P)).then_inc(gain_loaded[n % 2], 16)
            pool.wait_ge(h_ready, 2)
            with nc.allow_non_contiguous_dma(reason="per-channel vectors"):
                for tap in range(4):
                    pool.dma_start(cw_all[:, tap, :], A["conv_w_2"][0, tap].rearrange("(m p) -> p m", p=P)).then_inc(small2, 16)
                pool.dma_start(ab_w, A["w_in_2"][0][:, IN2_B:IN2_B + 16].rearrange("(k p) n -> p k n", p=P)).then_inc(small2, 16)
            pool.dma_start(dt_row[:, 0, :], A["dt_bias_2"][0].partition_broadcast(P)).then_inc(small2, 16)
            pool.dma_start(dt_row[:, 1, :], A["a_log_2"][0].partition_broadcast(P)).then_inc(small2, 16)
            pool.dma_start(gnorm, A["gdn_norm_2"][0].partition_broadcast(P)).then_inc(small2, 16)
            pool.memset(raw[:, :, 0:3], 0.0).then_inc(filled, 1)
            chp = Chain(pool, pool_chain)
            pool.wait_ge(small2, 16 * 8)
            pool.wait_ge(filled, 7)

            def convolve(fu, stride, a, pair):
                if not (isinstance(pair, int) and pair == 0):
                    pool.wait_ge(cv_out, pair * 3)
                chp.link(pool.tensor_copy(cw.rearrange("p t (k j) -> p t k j", k=3),
                                          cw_all.rearrange("p t (k h) -> p t k h", k=3)[:, :, :, bass.ds(pair * 2, 2)]))
                for c in (1, 3, 5):
                    for b in range(2):
                        pool.wait_ge(emptied[b], along(AFTER[b], fu + c, stride, a))
                    if not (isinstance(pair, int) and pair == 0):
                        pool.wait_ge(silu_out, pair)
                    y = cvn[:, c - 1:c + 1, :]
                    for tap in range(4):
                        x = raw[:, c - 1:c + 1, tap:tap + S]
                        w = cw[:, tap, c - 1:c + 1].unsqueeze(2).to_broadcast([P, 2, S])
                        ins = pool.tensor_tensor(cvt if tap else y, x, w, ALU.mult)
                        if tap:
                            chp.link(ins)
                            ins = pool.tensor_tensor(y, y, cvt, ALU.add)
                        if tap < 3:
                            chp.link(ins)
                    ins.then_inc(cv_out, 1)

            convolve(2 * P_MOBA + 32, 8, 0, 0)
            for i in rounds(pool, 3, chp, 19):
                convolve(2 * P_GDN + 8, 8, i, i + 1)
            pool.wait_ge(mg_lo, 2)
            pool.dma_start(p_in, A["p_2"][0, 0].rearrange("(t p) n -> p t n", p=P)).then_inc(p_loaded, 16)
            for n in range(5, 9):
                gain_free(n)
                pool.dma_start(gain[:, n % 2, :], A[GAINS[n]][0].partition_broadcast(P)).then_inc(gain_loaded[n % 2], 16)
        @block.scalar
        def _(act):
            ch = Chain(act, act_chain)

            def hi(pu, stride=0, i=0):
                p, j = pu // 2, pu % 2
                if p >= P_ALL:
                    return
                layout = PLAN[p][0]
                if not isinstance(i, int):
                    assert stride % (2 * UNITS) == 0 or stride == 12
                    assert PLAN[(pu + stride) // 2] == PLAN[p]
                if isinstance(i, int):
                    pu, i, stride = pu + stride * i, 0, 0
                    p, layout = pu // 2, PLAN[pu // 2][0]
                if j == 0:
                    act.wait_ge(w_loaded[SLOT[p]], along(LOADS, p, stride // 2, i))
                if pu >= UNITS or not isinstance(i, int):
                    act.wait_ge(unit_done, i * stride + (pu - UNITS + 1))
                act.activation(split_view(wh, pu % UNITS, layout), raw_unit(SLOT[p], j, layout), ACT.Copy).then_inc(w_hi, 1)

            def unit_wait(pu, stride=0, i=0):
                act.wait_ge(unit_done, i * stride + (pu + 1))

            def root(src, at):
                n = src.shape[0]
                ch.link(act.activation(junk[0:n, :], src, ACT.Square, accum_out=st[0:n, at:at + 1]))
                act.activation(st[0:n, at + 4:at + 5], st[0:n, at:at + 1], ACT.Sqrt, bias=eps[0:n, 0:1], scale=1.0 / D).then_inc(stat, 1)

            pieces = [1]

            def pieces_hi(off):
                for n in range(4):
                    t, ks = n // 2, slice(4 * (n % 2), 4 * (n % 2) + 4)
                    pieces[0] += 1
                    act.wait_ge(ut_ps, pieces[0])
                    act.activation(xTh[:, ks, off + t * P:off + (t + 1) * P], acc[:, n, :].rearrange("p (k n) -> p k n", n=P),
                                   ACT.Copy).then_inc(ut_hi, 1)

            def turn(n, last_unit, split, then=None, norm=True):
                split = list(split)
                act.preload_act_table(ACT.Sqrt)
                for t in range(NT):
                    if t == 0:
                        act.wait_ge(rows0_done, n + 1)
                    else:
                        act.wait_ge(unit_done, last_unit + 1)
                    root(acc[:, 2 * t:2 * t + 2, :].rearrange("p b n -> p (b n)"), t)
                while len(split) > 2:
                    hi(split.pop(0))
                if norm:
                    for t in range(NT):
                        act.wait_ge(h_ready, 2 * n + t + 1)
                        root(h[:, t, :], 8 + t)
                while split:
                    hi(split.pop(0))
                if then:
                    then()
                pieces_hi(0)

            act.dma_start(meta[0:META, :], A["meta_tokens"]).then_inc(meta_loaded, 16)
            act.dma_start(ident, A["cst"][:, C_IDENT:C_TRI]).then_inc(ident_loaded, 16)
            act.dma_start(gain[:, 0, :], A["g_pre_mix"][0].partition_broadcast(P)).then_inc(gain_first, 16)
            act.preload_act_table(ACT.Sqrt)
            act.wait_ge(filled, 4)
            for t in range(NT):
                act.wait_ge(x_loaded[t], 16)
                root(h[:, t, :], t)
                if t == 0:
                    act.wait_ge(meta_loaded, 16)
                    root(meta[0:META, :], 2)
            for n in range(4):
                hi(n)
            act.wait_ge(ut_ps, 1)
            act.activation(xTh[:, :, 0:META], ma[:, 0:KC * META].rearrange("p (k n) -> p k n", k=KC), ACT.Copy).then_inc(ut_hi, 1)
            pieces_hi(META)
            unit_wait(0)
            for v in range(KVH):
                for half in range(2):
                    ins = act.activation(kT1[64 * half:64 * half + 64, v, :], fm[64 * v:64 * v + 64, 0, 0:T1], ACT.Copy)
            ins.then_inc(emptied[0], 1)
            hi(4)
            act.wait_ge(small1, 16 * 10)
            ch.link(act.activation(lam_t[:, 0, :], cwb[:, :, 7], ACT.Abs))
            act.activation(lam_t[:, 1, :], lam_t[:, 0, :], ACT.Exp, scale=-1.0).then_inc(lam_e, 1)
            unit_wait(1)
            act.activation(v1[:, 0:2, :], ma[:, 0:256].rearrange("p (a b) -> p a b", a=2), ACT.Copy)
            act.activation(v1[0:META, 2, :], ma[0:META, 256:384], ACT.Copy).then_inc(v1_out, 1)
            hi(5)
            act.wait_ge(filled, 4)
            for m in range(4):
                unit_wait(2 + m)
                act.activation(qT1[:, m, :], fm[:, m % 2, 0:S], ACT.Copy).then_inc(emptied[m % 2], 1)
                hi(6 + m)

            def soft(b):
                nk = (P + META, 2 * P)[b]
                act.wait_ge(s1_max, b + 1)
                for hh in range(QH):
                    act.activation(p1[:, hh, 0:nk], p1[:, hh, 0:nk], ACT.Exp, bias=st[:, 16 + hh:17 + hh],
                                   accum_out=st[:, 8 + hh:9 + hh]).then_inc(s1_exp, 1)
                act.activation(st[:, 24:32], st[:, 24:32], ACT.Exp).then_inc(s1_sink, 1)

            def pT_copy(b):
                act.wait_ge(p1T_ps, 2 * b + 1)
                act.activation(pT1[0], ps[:, 4 * b:4 * b + 2, :].rearrange("p b (h c n) -> p (b h) c n", h=2, c=2), ACT.Copy).then_inc(p1T_out, 1)

            def oT_hi(b):
                act.wait_ge(o1T_ps, b + 1)
                act.activation(yTh[:, 0:4, b * P:(b + 1) * P], ma[:, :].rearrange("p (k n) -> p k n", k=4), ACT.Copy).then_inc(o1T_hi, 1)

            act.wait_ge(filled, 4)
            for m in range(LT):
                unit_wait(6 + m)
                act.activation(xr_pad[:, m, 3:3 + T1], fm[:, m % 2, 0:T1], ACT.Copy).then_inc(emptied[m % 2], 1)
                hi(10 + m)
                if m == 1:
                    soft(0)
            for m in range(2):
                unit_wait(10 + m)
                act.activation(gy[:, m, :], fm[:, m % 2, 0:S], ACT.Copy).then_inc(emptied[m % 2], 1)
                hi(14 + m)
            act.preload_act_table(ACT.Sigmoid)
            for m in range(LT):
                act.wait_ge(r_ps, m + 1)
                act.activation(r_g[:, m, :], fm[:, m % 2, 0:T1], ACT.Sigmoid, bias=cwb[:, m, 5:6]).then_inc(emptied[m % 2], 1)
                act.activation(i_g[:, m, :], (ma, mb)[m % 2][:, 0:T1], ACT.Sigmoid, bias=cwb[:, m, 6:7]).then_inc(i_act, 1)
            pT_copy(0)
            act.wait_ge(sp_ready, 1)
            for b in range(2):
                act.wait_ge(emptied[b], EMPTIED[GATE_UNIT][b])
            for m in range(LT):
                act.activation(th_[:, m, :], r_g[:, m, :], ACT.Tanh, scale=lam_t[:, 6, m:m + 1]).then_inc(tanh_out, 1)
            for m in range(LT):
                act.activation(a_[:, m, :], r_g[:, m, :], ACT.Exp, scale=lam_t[:, 7, m:m + 1]).then_inc(a_out, 1)
            act.wait_ge(a_out, LT)
            act.activation(a2, a_, ACT.Square).then_inc(a_out, 1)
            for m in range(2):
                unit_wait(12 + m)
                act.activation(gy[:, 2 + m, :], fm[:, m % 2, 0:S], ACT.Copy).then_inc(emptied[m % 2], 1)
                hi(16 + m)
            act.preload_act_table(ACT.Sqrt)
            oT_hi(0)
            act.wait_ge(m2_out, 1)
            act.activation(a2, th_, ACT.Sqrt).then_inc(mult_out, 1)
            for b in range(2):
                act.wait_ge(emptied[b], EMPTIED[14][b])
            act.activation(gy, gy, ACT.Gelu_apprx_tanh).then_inc(gelu_out, 1)
            act.wait_ge(rec_out, 1)
            act.activation(yTh[:, 4:8, :], gy, ACT.Copy).then_inc(rec_hi, 1)
            soft(1)
            for n in range(14, 18):
                hi(n + 4)
            pT_copy(1)
            oT_hi(1)
            turn(0, 21, range(22, 26))

            def ffn1_hidden(fu, par, n0, stride=0, i=0):
                for j in range(2):
                    unit_wait(fu + j, stride, i)
                    act.activation(hid_t[:, j, :], fm[:, j, 0:S], ACT.Relu).then_inc(emptied[j], 1)
                    hi(fu + j + 4, stride, i)
                for j in range(2):
                    act.wait_ge(hid_s, i * (stride // 2) + (2 * n0 + j + 1))
                    act.activation(hid_h[:, par, j, :], hid_q[:, j, :], ACT.Copy).then_inc(hid_hi, 1)

            def acc_units(fu, stride=0, i=0):
                for j in range(2):
                    hi(fu + j + 4, stride, i)

            F = 2 * P_FF1
            ffn1_hidden(F, 0, 0)
            for i in rounds(act, 7):
                ffn1_hidden(F + 2, 1, 1, 8, i)
                acc_units(F + 4, 8, i)
                ffn1_hidden(F + 6, 0, 2, 8, i)
                acc_units(F + 8, 8, i)
            ffn1_hidden(F + 58, 1, 15)
            acc_units(F + 60)
            turn(1, F + 63, (F + 66, F + 67))
            act.wait_ge(small2, 16 * 8)
            act.activation(ab_h, ab_w, ACT.Copy).then_inc(ab_hi, 1)
            act.activation(dt_row[:, 1, :], dt_row[:, 1, :], ACT.Exp).then_inc(ab_act, 1)
            act.wait_ge(ab_ps, 1)
            act.activation(junk[0:16, 0:S], ma[0:16, 0:S], ACT.Copy).then_inc(ab_sb, 1)

            def moba_unit(c, fu, stride, a, pair):
                unit_wait(fu, stride, a)
                if c < 4:
                    act.wait_ge(rope_out, pair) if not (isinstance(pair, int) and pair == 0) else None
                    act.activation(qk[:, c, :], fm[:, c % 2, 0:S], ACT.Copy).then_inc(emptied[c % 2], 1)
                elif c < 6:
                    act.activation(ga[:, bass.ds(pair * 2 + (c - 4), 1), :].rearrange("p a n -> p (a n)"),
                                   fm[:, c % 2, 0:S], ACT.Copy).then_inc(emptied[c % 2], 1)
                elif c == 7:
                    for t in range(NT):
                        act.activation(va[:, t, :], fm[:, t, 0:S], ACT.Copy).then_inc(emptied[t], 1)
                hi(fu + 4, stride, a)

            def gdn_unit(c, fu, stride, a, pair):
                unit_wait(fu, stride, a)
                later = not (isinstance(pair, int) and pair == 0)
                if c < 6:
                    if later:
                        act.wait_ge(cv_out, (pair - 1) * 3 + (c // 2 + 1))
                    act.activation(raw[:, c, 3:3 + S], fm[:, c % 2, 0:S], ACT.Copy).then_inc(emptied[c % 2], 1)
                elif c == 7:
                    if later:
                        act.wait_ge(sz_out, pair)
                    for t in range(NT):
                        act.activation(zr[:, t, :], fm[:, t, 0:S], ACT.Copy).then_inc(emptied[t], 1)
                hi(fu + 4, stride, a)

            def gateb_unit(c, fu, stride, a, pair):
                unit_wait(fu, stride, a)
                act.activation(gb_s[:, c, :], fm[:, c % 2, 0:S], ACT.Copy).then_inc(emptied[c % 2], 1)
                hi(fu + 4, stride, a)

            def moba_stage(s, a):
                if s == 0:
                    act.wait_ge(emptied[0], along(EMPTIED0, 2 * P_MOBA + 4, 8, a))
                    act.wait_ge(emptied[1], along(EMPTIED1, 2 * P_MOBA + 4, 8, a))
                    act.activation(rot[0:64, :, :], qk[64:128, :, :], ACT.Copy)
                    act.activation(rot[64:128, :, :], qk[0:64, :, :], ACT.Copy).then_inc(rot_out, 1)
                if s == 2:
                    act.wait_ge(s2_max, a + 1)
                    for n, (lo_, hi_) in enumerate(((0, 256), (256, 384))):
                        for j in range(2):
                            ins = act.activation(p2[:, j, lo_:hi_], sm2[:, j, lo_:hi_], ACT.Exp,
                                                 bias=st[:, 16 + 2 * n + j:17 + 2 * n + j], accum_out=st[:, 8 + 2 * n + j:9 + 2 * n + j])
                    ins.then_inc(s2_exp, 1)
                if s == 3:
                    act.wait_ge(p2T_ps, a + 1)
                    act.activation(pT2[:, 0, :], acc[:, 2, 0:384], ACT.Copy).then_inc(p2T_a, 1)
                if s == 4:
                    act.wait_ge(o2_ps, a + 1)
                    act.activation(yTh[:, bass.ds(a * 2, 2), :], ma[:, :].rearrange("p (j n) -> p j n", j=2), ACT.Copy).then_inc(o2_hi, 1)

            def start_inverse():
                act.activation(X_, ident.unsqueeze(1).to_broadcast([P, 4, P]), ACT.Copy).then_inc(inv_start, 1)

            def gdn_stage(s, a):
                if s == 0:
                    act.wait_ge(cv_out, a * 3 + 3)
                    act.activation(cv, cvn, ACT.Silu).then_inc(silu_out, 1)
                    act.wait_ge(silu_out, a + 1)
                    for q in (1, 0):
                        act.activation(sq[:, q * 512:(q + 1) * 512], cv[:, 2 * q:2 * q + 2, :].rearrange("p a b -> p (a b)"),
                                       ACT.Square).then_inc(sq_out, 1)
                if s == 1:
                    act.preload_act_table_set("natural_log_exp_and_others")
                    for n, q in enumerate((1, 0)):
                        act.wait_ge(ssq_ps, a * 2 + (n + 1))
                        rq = rk[:, q * 512:(q + 1) * 512]
                        ch.link(act.activation(rq, acc[:, q, :], ACT.Ln, bias=eps[:, 0:1]))
                        act.activation(rq, rq, ACT.Exp, scale=-0.5).then_inc(rk_out, 1)
                if s == 2:
                    act.wait_ge(vT_ps, a + 1)
                    for pr in range(4):
                        c, j = pr // 2, pr % 2
                        ins = act.activation(vb[:, pr, :], acc[:, 3, pr * P:(pr + 1) * P], ACT.Copy, scale=sc[:, 0, c, j:j + 1])
                    ins.then_inc(vb_out, 1)
                if s == 3:
                    act.wait_ge(kT_ps, a + 1)
                    for j in range(2):
                        act.activation(kdec[:, j, :], acc[:, 0, j * P:(j + 1) * P], ACT.Copy, scale=sc[:, 4, 0, j:j + 1])
                        ins = act.activation(kbe[:, j, :], acc[:, 0, (2 + j) * P:(3 + j) * P], ACT.Copy, scale=sc[:, 3, 1, j:j + 1])
                    ins.then_inc(kv_out, 1)
                if s == 4:
                    act.wait_ge(xt0_ps, a + 1)
                    act.activation(XT_, acc[:, 3, :].rearrange("p (r n) -> p r n", r=4), ACT.Copy).then_inc(xt0_out, 1)
                if s == 17:
                    act.wait_ge(uw_ps, a + 1)
                    act.activation(u0, acc[:, 3, 0:256].rearrange("p (j n) -> p j n", j=2), ACT.Copy).then_inc(u0_out, 1)
                if s == 18:
                    act.wait_ge(so_ps, a + 1)
                    act.activation(S1, acc[:, 1, 0:256].rearrange("p (j n) -> p j n", j=2), ACT.Copy).then_inc(S1_out, 1)
                if s == 19:
                    act.wait_ge(vn_ps, a + 1)
                    act.activation(vn, acc[:, 3, 256:512].rearrange("p (j n) -> p j n", j=2), ACT.Copy).then_inc(vn_out, 1)
                if s == 7 and not (isinstance(a, int) and a == 0):
                    out_root(a - 1)
                if s == 14 and not (isinstance(a, int) and a == 0):
                    out_hi(a - 1)
                if s == 13 and not (isinstance(a, int) and a == PAIRS - 1):
                    decays(a + 1)
                if s == 15:
                    act.wait_ge(emptied[0], along(EMPTIED0, 2 * P_GDN + 8, 8, a))
                    act.wait_ge(emptied[1], along(EMPTIED1, 2 * P_GDN + 8, 8, a))
                    if not (isinstance(a, int) and a == 0):
                        act.wait_ge(y_out, a)
                    act.activation(sz, zr, ACT.Silu).then_inc(sz_out, 1)
                if s == 20:
                    act.wait_ge(o_ps, a + 1)
                    act.activation(o_s, acc[:, 2, :].rearrange("p (r n) -> p r n", r=4), ACT.Copy).then_inc(os_out, 1)
                    if not (isinstance(a, int) and a == PAIRS - 1):
                        start_inverse()

            def decays(b):
                act.wait_ge(t12_out, b + 1)
                act.activation(eg, mb[:, 256:512].rearrange("p (j n) -> p j n", j=2), ACT.Exp)
                for pr in range(4):
                    c, j = pr // 2, pr % 2
                    act.activation(dt_[:, pr, :], dt_[:, pr, :], ACT.Exp, bias=sc[:, 2, c, j:j + 1])
                    ins = act.activation(dl_[:, pr, :], dl_[:, pr, :], ACT.Exp, bias=sc[:, 1, c, j:j + 1])
                ins.then_inc(dt_out, 1)

            def out_root(b):
                act.wait_ge(os_out, b + 1)
                for pr in range(4):
                    ins = act.activation(junk[:, 512 + pr * P:640 + pr * P], o_s[:, pr, :], ACT.Square, accum_out=st[:, pr:pr + 1])
                ch.link(ins)
                ch.link(act.activation(st[:, 4:8], st[:, 0:4], ACT.Ln, bias=eps[:, 0:1], scale=1.0 / P))
                act.activation(st[:, 4:8], st[:, 4:8], ACT.Exp, scale=-0.5).then_inc(og_out, 1)

            def out_hi(b):
                act.wait_ge(yT_ps, b + 1)
                dst = ybh[:, bass.ds(b * 2, 2), :].rearrange("p j (c n) -> p j c n", c=2)
                act.activation(dst, ma[:, :].rearrange("p (c j n) -> p j c n", c=2, j=2), ACT.Copy).then_inc(yb_hi, 1)

            def pair_round(weave, stage, unit, fu, a, pair, mine=0):
                before = ch.n
                for s, done in enumerate(finished(weave)):
                    stage(s, a)
                    for c in done:
                        unit(c, fu + c, 8, a, pair)
                return ch.n - before if isinstance(ch.n, int) else None

            M, G = 2 * P_MOBA, 2 * P_GDN
            for c in range(8):
                moba_unit(c, M + c, 8, 0, 0)
                if c == 1:
                    act.wait_ge(ab_out, 1)
                    act.activation(g_all[:, 0, :, :], ma[:, 256:288].rearrange("p (t n) -> p t n", t=2)[:, :, 0:8], ACT.Sigmoid).then_inc(ab_act, 1)
                    ch.link(act.activation(tmp16[:, 1, :], tmp16[:, 0, :], ACT.Abs))
                    act.activation(tmp16[:, 2, :], tmp16[:, 1, :], ACT.Exp, scale=-1.0).then_inc(ab_act, 1)
            act.wait_ge(gc_ps, 1)
            gcs = mb[:, 0:32].rearrange("p (v c h) -> p v c h", v=2, c=2)
            act.activation(g_all[:, 1, :, :], gcs[:, 0], ACT.Copy)
            act.activation(g_all[:, 2, :, :], gcs[:, 0], ACT.Copy, scale=-1.0)
            act.activation(g_all[:, 3, :, :], gcs[:, 0], ACT.Exp).then_inc(gc_act, 1)
            act.wait_ge(gc_ready, 1)
            act.activation(g_all[:, 4, :, :], g_all[:, 6, :, :], ACT.Exp).then_inc(gc_act, 1)
            for i in rounds(act, 3, ch, 0):
                pair_round(MOBA_WEAVE, moba_stage, moba_unit, M + 8, i, i + 1)
            pair_round(MOBA_WEAVE, moba_stage, gdn_unit, M + 8, 3, 0)
            start_inverse()
            decays(0)
            pair_round(GDN_WEAVE, gdn_stage, gdn_unit, G + 8, 0, 1)
            for i in rounds(act, 2, ch, 4):
                pair_round(GDN_WEAVE, gdn_stage, gdn_unit, G + 8, i + 1, i + 2)
            pair_round(GDN_WEAVE, gdn_stage, gateb_unit, G + 8, 3, 0)
            out_root(3)
            act.activation(ga, ga, ACT.Sigmoid).then_inc(sig_a, 1)
            act.wait_ge(emptied[0], EMPTIED0[2 * P_PROJA])
            act.wait_ge(emptied[1], EMPTIED1[2 * P_PROJA])
            act.activation(gb_s, gb_s, ACT.Sigmoid).then_inc(sig_b, 1)
            for n in range(16):
                hi(2 * P_PROJA + n + 4)
                if n == 2:
                    out_hi(3)
            for q in range(2):
                act.wait_ge(mg_out, 4 * q + 4)
                act.activation(yTh[:, 4 * q:4 * q + 4, :], gb_s[:, 4 * q:4 * q + 4, :], ACT.Copy).then_inc(mg_hi, 1)
            for n in range(6):
                hi(2 * P_OUT2 + n + 4)
            act.wait_ge(pT_ps, 1)
            act.activation(pT_h.rearrange("p k (t n) -> p t k n", t=2), ma[:, :].rearrange("p (t k n) -> p t k n", t=2, k=2),
                           ACT.Copy).then_inc(pT_hi, 1)

            def ple_rows():
                unit_wait(2 * P_PLE + 1)
                for t in range(NT):
                    ins = act.activation(e_row[:, t, :], high[:, 2 * t:2 * t + 2, :].rearrange("p b n -> p (b n)"), ACT.Copy)
                    if t == 0:
                        ins.then_inc(emptied[0], 1)
                ins.then_inc(emptied[1], 1)
                hi(2 * P_FF2 + 2)
                hi(2 * P_FF2 + 3)

            turn(2, 2 * P_OUT2 + 7, (2 * P_FF2, 2 * P_FF2 + 1), ple_rows)
            F2 = 2 * P_FF2

            def silu_gate(fu, stride=0, i=0, k=0):
                for j in range(2):
                    unit_wait(fu + j, stride, i)
                    if k > 0:
                        act.wait_ge(swi_m, i * (stride // 3) + 2 * (k - 1) + j + 1)
                    act.activation(gate_s[:, j, :], fm[:, j, 0:S], ACT.Silu).then_inc(swi_a, 1)
                    hi(fu + j + 4, stride, i)

            def hid2_hi(fu, stride=0, i=0, k=0):
                for j in range(2):
                    act.wait_ge(swi_m, i * (stride // 3) + 2 * k + j + 1)
                    act.activation(hid2_h[:, j, :], hid2[:, j, :], ACT.Copy).then_inc(swi_hi, 1)
                    hi(fu + j + 4, stride, i)

            silu_gate(F2)
            for t in range(NT):
                ch.link(act.activation(junk[:, :], e_row[:, t, :], ACT.Square, accum_out=st[:, 16 + t:17 + t]))
            hid2_hi(F2 + 2)
            for i in rounds(act, 4):
                for n in range(2):
                    silu_gate(F2 + 4 + 6 * n, 12, i, n + 1)
                    acc_units(F2 + 6 + 6 * n, 12, i)
                    hid2_hi(F2 + 8 + 6 * n, 12, i, n + 1)
            for n in range(2):
                silu_gate(F2 + 4 + 6 * n + 48, 0, 0, n + 9)
                acc_units(F2 + 6 + 6 * n + 48)
                hid2_hi(F2 + 8 + 6 * n + 48, 0, 0, n + 9)
            act.activation(st[:, 20:22], st[:, 16:18], ACT.Sqrt, bias=eps[:, 0:1], scale=1.0 / D).then_inc(e_root, 1)
            turn(3, F2 + 65, (F2 + 68, F2 + 69), norm=False)
            for n in range(4):
                hi(2 * P_PGATE + n + 4)
            act.preload_act_table(ACT.Sigmoid)
            for n in range(2 * NT):
                if n == 0:
                    act.wait_ge(rows0_done, 5)
                if n == 2:
                    act.wait_ge(unit_done, 2 * P_ALL)
                act.activation(u[:, n // 2, n % 2 * 512:n % 2 * 512 + 512], acc[:, n, :], ACT.Sigmoid).then_inc(fin_sig, 1)

        @block.vector
        def _(dve):
            ch = Chain(dve, dve_chain)
            link = ch.link
            TT, TS, STT = dve.tensor_tensor, dve.tensor_scalar, dve.scalar_tensor_tensor

            def lo(pu, stride=0, i=0):
                p, j = pu // 2, pu % 2
                if p >= P_ALL:
                    return
                if isinstance(i, int):
                    pu, i, stride = pu + stride * i, 0, 0
                    p = pu // 2
                layout = PLAN[p][0]
                dve.wait_ge(w_hi, i * stride + (pu + 1))
                TT(split_view(wl, pu % UNITS, layout), raw_unit(SLOT[p], j, layout),
                   split_view(wh, pu % UNITS, layout).bitcast(F32), ALU.subtract).then_inc(w_lo, 1)

            def log1p(y, z, t, out):
                link(TS(t, y, 2.0, None, ALU.add))
                link(dve.reciprocal(t, t))
                link(TT(z, y, t, ALU.mult))
                link(TT(t, z, z, ALU.mult))
                link(TS(out, t, 1.0 / 19, None, ALU.mult))
                for c in (17, 15, 13, 11, 9, 7, 5, 3):
                    link(STT(out, out, 1.0 / c, t, ALU.add, ALU.mult))
                link(STT(out, out, 1.0, z, ALU.add, ALU.mult))
                link(TS(out, out, 2.0, None, ALU.mult))

            roots, pieces = [0], [1]

            def inverse(at, n=P):
                roots[0] += 1
                dve.wait_ge(stat, roots[0])
                link(dve.reciprocal(st[0:n, at:at + 1], st[0:n, at:at + 1]))

            def pieces_lo(off):
                for n in range(4):
                    t, ks = n // 2, slice(4 * (n % 2), 4 * (n % 2) + 4)
                    pieces[0] += 1
                    dve.wait_ge(ut_hi, pieces[0])
                    TT(xTl[:, ks, off + t * P:off + (t + 1) * P], acc[:, n, :].rearrange("p (k n) -> p k n", n=P),
                       xTh[:, ks, off + t * P:off + (t + 1) * P].bitcast(F32), ALU.subtract).then_inc(ut_lo, 1)

            def turn(g, split, norm=True):
                dve.wait_ge(gain_loaded[1], 16 * (g // 2 + 1))
                for t in range(NT):
                    inverse(4 + t)
                    ins = STT(u[:, t, :], acc[:, 2 * t:2 * t + 2, :].rearrange("p b n -> p (b n)"), st[:, 4 + t:5 + t],
                              gain[:, g % 2, :], ALU.mult, ALU.mult)
                    if t == 0:
                        link(ins)
                    else:
                        ins.then_inc(gain_used, 1)
                        dve.wait_ge(gain_used, g // 2 + 1)
                    TT(h[:, t, :], h[:, t, :], u[:, t, :], ALU.add).then_inc(h_ready, 1)
                if norm:
                    dve.wait_ge(gain_loaded[0], 16 * ((g + 1) // 2))
                    for t in range(NT):
                        inverse(12 + t)
                        STT(u[:, t, :], h[:, t, :], st[:, 12 + t:13 + t], gain[:, (g + 1) % 2, :], ALU.mult, ALU.mult).then_inc(u_ready, 1)
                for n in split[:2]:
                    lo(n)
                pieces_lo(0)
                for n in split[2:]:
                    lo(n)

            dve.wait_ge(filled, 4)
            dve.wait_ge(gain_first, 16)
            inverse(4)
            STT(u[:, 0, :], h[:, 0, :], st[:, 4:5], gain[:, 0, :], ALU.mult, ALU.mult).then_inc(u_ready, 1)
            inverse(6, META)
            STT(meta[0:META, :], meta[0:META, :], st[0:META, 6:7], gain[0:META, 0, :], ALU.mult, ALU.mult).then_inc(u_ready, 1)
            inverse(5)
            STT(u[:, 1, :], h[:, 1, :], st[:, 5:6], gain[:, 0, :], ALU.mult, ALU.mult).then_inc(u_ready, 1)
            for n in range(4):
                lo(n)
            dve.wait_ge(ut_hi, 1)
            TT(xTl[:, :, 0:META], ma[:, 0:KC * META].rearrange("p (k n) -> p k n", k=KC), xTh[:, :, 0:META].bitcast(F32),
               ALU.subtract).then_inc(ut_lo, 1)
            pieces_lo(META)
            lo(4)
            lo(5)
            lo(6)
            dve.wait_ge(lam_e, 1)
            log1p(lam_t[:, 1, :], lam_t[:, 2, :], lam_t[:, 3, :], lam_t[:, 4, :])
            link(TS(lam_t[:, 5, :], cwb[:, :, 7], -1.0, 0.0, ALU.mult, ALU.max))
            link(TT(lam_t[:, 4, :], lam_t[:, 4, :], lam_t[:, 5, :], ALU.add))
            TS(lam_t[:, 6, :], lam_t[:, 4, :], 8.0, None, ALU.mult)
            TS(lam_t[:, 7, :], lam_t[:, 4, :], -8.0, None, ALU.mult).then_inc(sp_ready, 1)
            for n in range(7, 10):
                lo(n)

            def soft_scores(b):
                nk = (P + META, 2 * P)[b]
                mask = cst[:, (C_WIN0, C_WIN1)[b]:(C_WIN0, C_WIN1)[b] + nk]
                dve.wait_ge(s1_ps, b + 1)
                dve.wait_ge(cst_loaded, 16)
                dve.wait_ge(small1, 16 * 10)
                sc_ps = ps[:, 4 * b:4 * b + 4, :].rearrange("p b (h n) -> p (b h) n", h=2)
                link(STT(p1[:, :, 0:nk], sc_ps[:, :, 0:nk], SC1, mask.unsqueeze(1).to_broadcast([P, QH, nk]), ALU.mult, ALU.add))
                if b:
                    dve.wait_ge(s1_exp, QH * b)
                link(dve.tensor_reduce(st[:, 16:24], p1[:, :, 0:nk], AX, ALU.max))
                link(TT(st[:, 16:24], st[:, 16:24], sink, ALU.max))
                link(TT(st[:, 24:32], sink, st[:, 16:24], ALU.subtract))
                TS(st[:, 16:24], st[:, 16:24], -1.0, None, ALU.mult).then_inc(s1_max, 1)

            def soft_sums(b):
                dve.wait_ge(s1_sink, b + 1)
                dve.wait_ge(s1_exp, QH * (b + 1))
                link(TT(st[:, 8:16], st[:, 8:16], st[:, 24:32], ALU.add))
                link(dve.reciprocal(st[:, 8:16], st[:, 8:16]))
                nk = (P + META, 2 * P)[b]
                for hh in range(QH):
                    ins = TS(p1[:, hh, 0:nk], p1[:, hh, 0:nk], st[:, 8 + hh:9 + hh], None, ALU.mult)
                ins.then_inc(p_ready, 1)

            def pT_copy(b):
                dve.wait_ge(p1T_ps, 2 * b + 2)
                dve.tensor_copy(pT1[1], ps[:, 4 * b + 2:4 * b + 4, :].rearrange("p b (h c n) -> p (b h) c n", h=2, c=2)).then_inc(p1T_out, 1)

            def oT_lo(b):
                dve.wait_ge(o1T_hi, b + 1)
                TT(yTl[:, 0:4, b * P:(b + 1) * P], ma[:, :].rearrange("p (k n) -> p k n", k=4),
                   yTh[:, 0:4, b * P:(b + 1) * P].bitcast(F32), ALU.subtract).then_inc(o1T_lo, 1)

            def convolve(q):
                for b in range(2):
                    dve.wait_ge(emptied[b], AFTER[b][7 + 2 * q])
                for m in (2 * q, 2 * q + 1):
                    ins = TS(xc[:, m, :], xr_pad[:, m, 0:T1], cwb[:, m, 0:1], cwb[:, m, 4:5], ALU.mult, ALU.add)
                link(ins)
                for tap in range(1, 4):
                    for m in (2 * q, 2 * q + 1):
                        ins = STT(xc[:, m, :], xr_pad[:, m, tap:tap + T1], cwb[:, m, tap:tap + 1], xc[:, m, :], ALU.mult, ALU.add)
                    if tap < 3:
                        link(ins)
                ins.then_inc(xc_ready, 1)

            soft_scores(0)
            lo(10)
            lo(11)
            convolve(0)
            lo(12)
            lo(13)
            convolve(1)
            lo(14)
            soft_sums(0)
            lo(15)
            dve.wait_ge(i_act, LT)
            dve.wait_ge(xc_ready, 2)
            link(TT(xc, i_g, xc, ALU.mult))
            pT_copy(0)
            dve.wait_ge(tanh_out, LT)
            dve.wait_ge(a_out, LT + 1)
            STT(th_, a2, 1.0, th_, ALU.add, ALU.mult).then_inc(m2_out, 1)
            lo(16)
            lo(17)
            oT_lo(0)
            dve.wait_ge(mult_out, 1)
            link(TT(xc, a2, xc, ALU.mult))
            for m in range(LT):
                ins = dve.tensor_tensor_scan(r_g[:, m, :], a_[:, m, :], xc[:, m, :], 0.0, ALU.mult, ALU.add)
            link(ins)
            dve.wait_ge(gelu_out, 1)
            TT(gy, gy, r_g[:, :, META:T1], ALU.mult).then_inc(rec_out, 1)
            dve.wait_ge(rec_hi, 1)
            TT(yTl[:, 4:8, :], gy, yTh[:, 4:8, :].bitcast(F32), ALU.subtract).then_inc(rec_lo, 1)
            soft_scores(1)
            lo(18)
            soft_sums(1)
            for n in range(19, 22):
                lo(n)
            pT_copy(1)
            oT_lo(1)
            turn(1, range(22, 26))

            def ffn1_hidden(fu, par, n0, stride=0, i=0):
                for j in range(2):
                    lo(fu + j + 4, stride, i)
                    dve.wait_ge(emptied[j], along(AFTER[j], fu + j, stride, i))
                    if n0:
                        dve.wait_ge(hid_lo, i * (stride // 2) + 2 * n0 + j - 1)
                    TT(hid_q[:, j, :], hid_t[:, j, :], hid_t[:, j, :], ALU.mult).then_inc(hid_s, 1)
                for j in range(2):
                    k = i * (stride // 2) + 2 * n0 + j + 1
                    dve.wait_ge(hid_hi, k)
                    TT(hid_l[:, par, j, :], hid_q[:, j, :], hid_h[:, par, j, :].bitcast(F32), ALU.subtract).then_inc(hid_lo, 1)

            def acc_units(fu, stride=0, i=0):
                for j in range(2):
                    lo(fu + j + 4, stride, i)

            F = 2 * P_FF1
            ffn1_hidden(F, 0, 0)
            for i in rounds(dve, 7):
                ffn1_hidden(F + 2, 1, 1, 8, i)
                acc_units(F + 4, 8, i)
                ffn1_hidden(F + 6, 0, 2, 8, i)
                acc_units(F + 8, 8, i)
            ffn1_hidden(F + 58, 1, 15)
            acc_units(F + 60)
            turn(3, (F + 66, F + 67))
            dve.wait_ge(ab_hi, 1)
            TT(ab_l, ab_w, ab_h.bitcast(F32), ALU.subtract).then_inc(ab_lo, 1)
            def pair_unit(c, fu, stride, a, pair):
                lo(fu + 4, stride, a)

            def moba_stage(s, a):
                if s == 0:
                    cosb = cst[:, C_COS:C_SIN].unsqueeze(1).to_broadcast([P, 4, S])
                    sinb = cst[:, C_SIN:C_END].unsqueeze(1).to_broadcast([P, 4, S])
                    dve.wait_ge(rot_out, a + 1)
                    TT(qr, qk, cosb, ALU.mult)
                    link(TT(rot, rot, sinb, ALU.mult))
                    TT(qr, qr, rot, ALU.add).then_inc(rope_out, 1)
                if s == 1:
                    dve.wait_ge(s2_ps, a + 1)
                    mask = cst[:, C_MOBA:C_WIN0].unsqueeze(1).to_broadcast([P, 2, 384])
                    link(STT(sm2, acc[:, 0:2, 0:384], SC2, mask, ALU.mult, ALU.add))
                    dve.tensor_reduce(st[:, 16:18], sm2[:, :, 0:256], AX, ALU.max)
                    link(dve.tensor_reduce(st[:, 18:20], sm2[:, :, 256:384], AX, ALU.max))
                    TS(st[:, 16:20], st[:, 16:20], -1.0, None, ALU.mult).then_inc(s2_max, 1)
                if s == 2:
                    dve.wait_ge(s2_exp, a + 1)
                    link(dve.reciprocal(st[:, 8:12], st[:, 8:12]))
                    for n, (lo_, hi_) in enumerate(((0, 256), (256, 384))):
                        for j in range(2):
                            ins = TS(p2[:, j, lo_:hi_], p2[:, j, lo_:hi_], st[:, 8 + 2 * n + j:9 + 2 * n + j], None, ALU.mult)
                    ins.then_inc(s2_p, 1)
                if s == 3:
                    dve.wait_ge(p2T_ps, a + 1)
                    dve.tensor_copy(pT2[:, 1, :], acc[:, 3, 0:384]).then_inc(p2T_v, 1)
                if s == 4:
                    dve.wait_ge(o2_hi, a + 1)
                    TT(yTl[:, bass.ds(a * 2, 2), :], ma[:, :].rearrange("p (j n) -> p j n", j=2),
                       yTh[:, bass.ds(a * 2, 2), :].bitcast(F32), ALU.subtract).then_inc(o2_lo, 1)

            def rows4(x):
                return x.rearrange("p (r n) -> p r n", r=4)

            def spread(x):
                return x.unsqueeze(1).to_broadcast([P, 4, P])

            def half_blocks(x, n, odd):
                return x.rearrange("p r (q two b) -> p (r q) two b", two=2, b=1 << n)[:, :, odd, :]

            def grow(x, n, odd, z):
                v = half_blocks(x, n, odd)
                return TT(v, v, z, ALU.subtract)

            def gdn_stage(s, a):
                if s == 1:
                    for n, q in enumerate((1, 0)):
                        dve.wait_ge(rk_out, a * 2 + (n + 1))
                        x = cv[:, 2 * q:2 * q + 2, :].rearrange("p a b -> p (a b)")
                        TT(x, x, rk[:, q * 512:(q + 1) * 512], ALU.mult).then_inc(qkn_out, 1)
                if s == 3:
                    dve.wait_ge(kk_ps, a + 1)
                    dve.wait_ge(dt_out, a + 1)
                    for pr in range(4):
                        ins = STT(A_[:, pr, :], acc[:, 1, pr * P:(pr + 1) * P], sc[:, 0, pr // 2, pr % 2:pr % 2 + 1], dl_[:, pr, :], ALU.mult, ALU.mult)
                    ins.then_inc(A_out, 1)
                    dve.wait_ge(A_out, a + 1)
                    dve.wait_ge(inv_start, a + 1)
                    low = PM_.rearrange("p r n -> p (r n)")[:, 0:4 * 64]
                    first = cst[:, C_LEV:C_LEV + 64].unsqueeze(1).to_broadcast([P, 4, 64])
                    link(TT(rows4(low), A_.rearrange("p r (q two) -> p r q two", two=2)[:, :, :, 0], first, ALU.mult))
                    grow(X_, 0, 0, low.rearrange("p (m b) -> p m b", b=1)).then_inc(x0_out, 1)
                if s == 4:
                    dve.wait_ge(kq_ps, a + 1)
                    STT(attnT, rows4(acc[:, 2, :]), SC2, dt_, ALU.mult, ALU.mult).then_inc(attn_out, 1)
                    STT(qeg, cv[:, 0:2, P:2 * P], SC2, eg, ALU.mult, ALU.mult).then_inc(qeg_out, 1)
                if s == 8 and not (isinstance(a, int) and a == PAIRS - 1):
                    dve.wait_ge(kv_out, a + 1)
                    dve.wait_ge(qeg_out, a + 1)
                    prepare(a + 1)
                if s == 10 and not (isinstance(a, int) and a == PAIRS - 1):
                    exponents(a + 1)
                if 5 <= s < 17 and s % 2 == 1:
                    lv = (s - 5) // 2 + 1
                    for g in range(2):
                        dve.wait_ge(lv_p[g], a * 6 + lv)
                        mask = cst[:, C_LEV + lv * P:C_LEV + (lv + 1) * P].unsqueeze(1).to_broadcast([P, 2, P])
                        TT(PM_[:, 2 * g:2 * g + 2, :], acc[:, 3 * g, 0:256].rearrange("p (j n) -> p j n", j=2), mask,
                           ALU.mult).then_inc(lv_pm[g], 1)
                if 5 <= s < 17 and s % 2 == 0:
                    lv = (s - 5) // 2 + 1
                    for g in range(2):
                        dve.wait_ge(lv_z[g], a * 6 + lv)
                        z = acc[:, 1 + g, :].rearrange("p (r n) -> p r n", r=4)
                        grow(XT_[:, 2 * g:2 * g + 2, :], lv, 1, half_blocks(z[:, 0:2, :], lv, 1)).then_inc(lv_xt[g], 1)
                        if lv < 6:
                            grow(X_[:, 2 * g:2 * g + 2, :], lv, 0, half_blocks(z[:, 2:4, :], lv, 0)).then_inc(lv_x[g], 1)
                if s == 17:
                    dve.wait_ge(uw_ps, a + 1)
                    TS(nwT, acc[:, 0, 0:256].rearrange("p (j n) -> p j n", j=2), -1.0, None, ALU.mult).then_inc(nw_out, 1)
                if s == 11 and not (isinstance(a, int) and a == 0):
                    out_rows(a - 1)
                if s == 14 and not (isinstance(a, int) and a == 0):
                    out_lo(a - 1)

            def prepare(b):
                link(dve.tensor_copy(sc, g_all[:, 0:6, :, bass.ds(b * 2, 2)]))
                gsrc = sc[:, 5, :, :].rearrange("p c j -> p (c j)").unsqueeze(2).to_broadcast([P, 4, P])
                dve.tensor_copy(gb, gsrc).then_inc(gb_out, 1)

            def exponents(b):
                dve.wait_ge(gcb_ps, b + 1)
                TT(dt_, rows4(mb[:, :]), spread(cst[:, C_MUP:C_MLOW]), ALU.add)
                TT(dl_, spread(cst[:, C_MLOW:C_LEV]), rows4(mb[:, :]), ALU.subtract).then_inc(t12_out, 1)

            def out_rows(b):
                dve.wait_ge(og_out, b + 1)
                dve.wait_ge(sz_out, b + 1)
                for pr in range(4):
                    ins = STT(y_[:, pr, :], o_s[:, pr, :], st[:, 4 + pr:5 + pr], gnorm, ALU.mult, ALU.mult)
                link(ins)
                TT(y_, y_, sz.rearrange("p t (j n) -> p (t j) n", j=2), ALU.mult).then_inc(y_out, 1)

            def out_lo(b):
                dve.wait_ge(yb_hi, b + 1)
                dst = ybl[:, bass.ds(b * 2, 2), :].rearrange("p j (c n) -> p j c n", c=2)
                hi_ = ybh[:, bass.ds(b * 2, 2), :].rearrange("p j (c n) -> p j c n", c=2).bitcast(F32)
                TT(dst, ma[:, :].rearrange("p (c j n) -> p j c n", c=2, j=2), hi_, ALU.subtract).then_inc(yb_lo, 1)

            def pair_round(weave, stage, unit, fu, a, pair):
                for s, done in enumerate(finished(weave)):
                    stage(s, a)
                    for c in done:
                        unit(c, fu + c, 8, a, pair)

            M, G = 2 * P_MOBA, 2 * P_GDN
            for c in range(8):
                pair_unit(c, M + c, 8, 0, 0)
                if c == 1:
                    dve.wait_ge(abT_ps, 1)
                    x_dt = tmp16[:, 0, :].rearrange("p (t n) -> p t n", t=2)
                    TT(x_dt, ma[:, 256:288].rearrange("p (t n) -> p t n", t=2)[:, :, 8:16],
                       dt_row[:, 0, :].unsqueeze(1).to_broadcast([P, 2, 8]), ALU.add).then_inc(ab_out, 1)
                    dve.wait_ge(ab_act, 3)
                    log1p(tmp16[:, 2, :], tmp16[:, 3, :], tmp16[:, 4, :], tmp16[:, 5, :])
                    link(STT(tmp16[:, 5, :], tmp16[:, 0, :], 0.0, tmp16[:, 5, :], ALU.max, ALU.add))
                    STT(g_all[:, 5, :, :], tmp16[:, 5, :].rearrange("p (t n) -> p t n", t=2), -1.0,
                        dt_row[:, 1, :].unsqueeze(1).to_broadcast([P, 2, 8]), ALU.mult, ALU.mult).then_inc(g_ready, 1)
            dve.wait_ge(gc_act, 1)
            gcs = mb[:, 0:32].rearrange("p (v c h) -> p v c h", v=2, c=2)
            TT(g_all[:, 3, :, :], g_all[:, 3, :, :], g_all[:, 0, :, :], ALU.mult)
            TT(g_all[:, 6, :, :], gcs[:, 1], g_all[:, 1, :, :], ALU.subtract).then_inc(gc_ready, 1)
            for i in rounds(dve, 3, ch, 4):
                pair_round(MOBA_WEAVE, moba_stage, pair_unit, M + 8, i, i + 1)
            pair_round(MOBA_WEAVE, moba_stage, pair_unit, M + 8, 3, 0)
            dve.wait_ge(gc_act, 2)
            prepare(0)
            exponents(0)
            pair_round(GDN_WEAVE, gdn_stage, pair_unit, G + 8, 0, 1)
            for i in rounds(dve, 2, ch, 3):
                pair_round(GDN_WEAVE, gdn_stage, pair_unit, G + 8, i + 1, i + 2)
            pair_round(GDN_WEAVE, gdn_stage, pair_unit, G + 8, 3, 0)
            out_rows(3)
            dve.wait_ge(sig_a, 1)
            for m in range(KC):
                pu = 2 * P_PROJA + m
                dve.wait_ge(unit_done, pu + 1)
                TT(ga[:, m, :], ga[:, m, :], fm[:, m % 2, 0:S], ALU.mult).then_inc(emptied[m % 2], 1)
                lo(pu + 4)
                if m == 2:
                    out_lo(3)
            dve.wait_ge(sig_b, 1)
            dve.wait_ge(emptied[0], EMPTIED0[2 * P_PROJB])
            dve.wait_ge(emptied[1], EMPTIED1[2 * P_PROJB])
            for m in range(KC):
                pu = 2 * P_PROJB + m
                dve.wait_ge(unit_done, pu + 1)
                ins = TT(gb_s[:, m, :], gb_s[:, m, :], fm[:, m % 2, 0:S], ALU.mult)
                ins.then_inc(emptied[m % 2], 1)
                dve.wait_ge(emptied[m % 2], AFTER[m % 2][pu])
                TT(gb_s[:, m, :], gb_s[:, m, :], ga[:, m, :], ALU.add).then_inc(mg_out, 1)
                lo(pu + 4)
            for q in range(2):
                dve.wait_ge(mg_hi, q + 1)
                TT(yTl[:, 4 * q:4 * q + 4, :], gb_s[:, 4 * q:4 * q + 4, :], yTh[:, 4 * q:4 * q + 4, :].bitcast(F32), ALU.subtract).then_inc(mg_lo, 1)
            for n in range(6):
                lo(2 * P_OUT2 + n + 4)
            dve.wait_ge(pT_hi, 1)
            TT(pT_l.rearrange("p k (t n) -> p t k n", t=2), ma[:, :].rearrange("p (t k n) -> p t k n", t=2, k=2),
               pT_h.rearrange("p k (t n) -> p t k n", t=2).bitcast(F32), ALU.subtract).then_inc(pT_lo, 1)
            turn(5, (2 * P_FF2, 2 * P_FF2 + 1))
            lo(2 * P_FF2 + 2)
            lo(2 * P_FF2 + 3)
            F2 = 2 * P_FF2

            def gate_units(fu, stride=0, i=0):
                for j in range(2):
                    lo(fu + j + 4, stride, i)

            def hid2_mul(fu, stride=0, i=0, k=0):
                for j in range(2):
                    n = i * (stride // 3) + 2 * k + j + 1
                    dve.wait_ge(swi_a, n)
                    dve.wait_ge(unit_done, i * stride + (fu + j + 1))
                    if k:
                        dve.wait_ge(swi_lo, n - 2)
                    TT(hid2[:, j, :], gate_s[:, j, :], (ma, mb)[j][:, 0:S], ALU.mult).then_inc(swi_m, 1)
                    lo(fu + j + 4, stride, i)
                for j in range(2):
                    n = i * (stride // 3) + 2 * k + j + 1
                    dve.wait_ge(swi_hi, n)
                    TT(hid2_l[:, j, :], hid2[:, j, :], hid2_h[:, j, :].bitcast(F32), ALU.subtract).then_inc(swi_lo, 1)

            gate_units(F2)
            hid2_mul(F2 + 2)
            for i in rounds(dve, 4):
                for n in range(2):
                    gate_units(F2 + 4 + 6 * n, 12, i)
                    acc_units(F2 + 6 + 6 * n, 12, i)
                    hid2_mul(F2 + 8 + 6 * n, 12, i, n + 1)
            for n in range(2):
                gate_units(F2 + 52 + 6 * n)
                acc_units(F2 + 54 + 6 * n)
                hid2_mul(F2 + 56 + 6 * n, 0, 0, n + 9)
            turn(7, (F2 + 68, F2 + 69), norm=False)
            for n in range(4):
                lo(2 * P_PGATE + n + 4)
            dve.wait_ge(e_root, 1)
            link(dve.reciprocal(st[:, 20:22], st[:, 20:22]))
            dve.wait_ge(gain_loaded[0], 16 * 4)
            for t in range(NT):
                STT(e_row[:, t, :], e_row[:, t, :], st[:, 20 + t:21 + t], gain[:, 0, :], ALU.mult, ALU.mult).then_inc(e_out, 1)
            dve.wait_ge(e_out, NT)
            for n in range(2 * NT):
                t, at = n // 2, slice(n % 2 * 512, n % 2 * 512 + 512)
                dve.wait_ge(fin_sig, n + 1)
                link(TT(u[:, t, at], u[:, t, at], e_row[:, t, at], ALU.mult))
                TT(u[:, t, at], u[:, t, at], h[:, t, at], ALU.add).then_inc(fin_out, 1)

        @block.tensor
        def _(pe):
            mm = pe.matmul

            def unit_ready(pu, stride=0, i=0):
                pe.wait_ge(w_lo, i * stride + (pu + 1))

            def bank_ready(j, pu, stride=0, i=0):
                n = along((EMPTIED0, EMPTIED1)[j], pu, stride, i)
                if not isinstance(n, int) or n > 0:
                    pe.wait_ge(emptied[j], n)

            def three(out, wh_, wl_, xh, xl, first, last):
                mm(out, wh_, xh, start=first, stop=False)
                mm(out, wh_, xl, start=False, stop=False)
                return mm(out, wl_, xh, start=False, stop=last)

            def three_tok(out, xh, xl, wh_, wl_, first, last, group=True):
                mm(out, xh, wh_, start=first, stop=False, skip_group_check=not group)
                mm(out, xh, wl_, start=False, stop=False, skip_group_check=not group)
                return mm(out, xl, wh_, start=False, stop=last, skip_group_check=not group)

            def fm_steps(pu, xh, xl, off, n, col=0, stride=0, i=0):
                unit_ready(pu, stride, i)
                bank_ready(pu % 2, pu, stride, i)
                a, b = (split_view(w, pu % UNITS, "cols") for w in (wh, wl))
                for k in range(KC):
                    last = three(fm[:, pu % 2, col:col + n], a[:, k, :], b[:, k, :], xh[:, k, off:off + n], xl[:, k, off:off + n],
                                 k == 0, k == KC - 1)
                    if k == KC - 1:
                        last.then_inc(unit_done, 1)
                    yield

            def tok_steps(pu, off, stride=0, i=0):
                unit_ready(pu, stride, i)
                j = pu % 2
                if j == 0:
                    bank_ready(0, pu, stride, i)
                    bank_ready(1, pu, stride, i)
                a, b = (w[:, pu % UNITS, :].rearrange("p (k n) -> p k n", k=4) for w in (wh, wl))
                for kk in range(4):
                    for t in range(NT):
                        k = 4 * j + kk
                        last = three_tok(fm[:, t, 0:S], xTh[:, k, off + t * P:off + (t + 1) * P], xTl[:, k, off + t * P:off + (t + 1) * P],
                                         a[:, kk, :], b[:, kk, :], k == 0, k == KC - 1)
                        if kk == 3 and t == NT - 1:
                            last.then_inc(unit_done, 1)
                        yield

            def run(steps):
                for _ in steps:
                    pass

            def acc_unit(pu, xh, xl, first, last_, stride=0, i=0, into=acc):
                unit_ready(pu, stride, i)
                a, b = wh[:, pu % UNITS, :], wl[:, pu % UNITS, :]
                for t in range(NT):
                    for half in range(2):
                        last = three_tok(into[:, 2 * t + half, :], xh[:, t * P:(t + 1) * P], xl[:, t * P:(t + 1) * P],
                                         a[:, half * 512:(half + 1) * 512], b[:, half * 512:(half + 1) * 512], first, last_, group=False)
                last.then_inc(unit_done, 1)

            def acc_tail(pus, xs, last_=True, opens=False):
                for t in range(NT):
                    for n, (pu, (xh, xl)) in enumerate(zip(pus, xs)):
                        if t == 0:
                            unit_ready(pu)
                        a, b = wh[:, pu % UNITS, :], wl[:, pu % UNITS, :]
                        for half in range(2):
                            last = three_tok(acc[:, 2 * t + half, :], xh[:, t * P:(t + 1) * P], xl[:, t * P:(t + 1) * P],
                                             a[:, half * 512:(half + 1) * 512], b[:, half * 512:(half + 1) * 512], False,
                                             n == len(pus) - 1, group=False)
                        if t == 1:
                            last.then_inc(unit_done, 1)
                        elif n == len(pus) - 1:
                            last.then_inc(rows0_done, 1)

            pieces = [1]

            def transposes(rows_, ready, base):
                for n in range(4):
                    t = n // 2
                    if n % 2 == 0:
                        pe.wait_ge(ready, base + t + 1)
                    for k in range(4):
                        last = pe.transpose(acc[:, n, k * P:(k + 1) * P], rows_[:, t, (n % 2 * 4 + k) * P:(n % 2 * 4 + k + 1) * P], ident)
                    last.then_inc(ut_ps, 1)
                pieces[0] += 4

            def pieces_ready():
                pe.wait_ge(ut_lo, pieces[0])

            pe.wait_ge(ident_loaded, 16)
            pe.wait_ge(u_ready, 2)
            for k in range(KC):
                last = pe.transpose(ma[:, k * META:(k + 1) * META], meta[0:META, k * P:(k + 1) * P], ident[0:META, 0:META])
            last.then_inc(ut_ps, 1)
            transposes(u, u_ready, 1)
            pieces_ready()
            run(fm_steps(0, xTh, xTl, 0, T1))
            unit_ready(1)
            a, b = (split_view(w, 1, "cols") for w in (wh, wl))
            for t, (off, n) in enumerate(((META, P), (META + P, P), (0, META))):
                for k in range(KC):
                    last = three_tok(ma[0:n, t * P:(t + 1) * P], xTh[:, k, off:off + n], xTl[:, k, off:off + n], a[:, k, :], b[:, k, :],
                                     k == 0, k == KC - 1)
            last.then_inc(unit_done, 1)
            for m in range(4):
                run(fm_steps(2 + m, xTh, xTl, META, S))

            chunks = (((0, META, 2), (META, P, 0)), ((0, P, 0), (P, P, 1)))

            def scores(b):
                nk, k0 = ((P + META, 0), (2 * P, META))[b]
                for hh in range(QH):
                    at_ = (hh % 2) * 4 + hh // 2
                    part = slice(64 * (hh % 2), 64 * (hh % 2) + 64)
                    last = mm(ps[:, 4 * b + at_ // 2, (at_ % 2) * 256:(at_ % 2) * 256 + nk], qT1[part, hh // 2, b * P:(b + 1) * P],
                              kT1[part, hh // 4, k0:k0 + nk], start=True, stop=True)
                last.then_inc(s1_ps, 1)

            def p_transposes(b):
                pe.wait_ge(p_ready, b + 1)
                for hh in range(QH):
                    for c, (at, n, _) in enumerate(chunks[b]):
                        last = pe.transpose(ps[0:n, 4 * b + hh // 2, (hh % 2) * 256 + c * P:(hh % 2) * 256 + c * P + P], p1[:, hh, at:at + n], ident)
                    if hh % 4 == 3:
                        last.then_inc(p1T_ps, 1)

            def outputs(b):
                pe.wait_ge(p1T_out, 2 * b + 2)
                for odd in range(2):
                    for kv in range(KVH):
                        for c, (at, n, vt) in enumerate(chunks[b]):
                            last = mm(ma[64 * odd:64 * odd + 64, kv * 256:(kv + 1) * 256], v1[0:n, vt, 64 * kv:64 * kv + 64],
                                      pT1[odd][0:n, 2 * kv:2 * kv + 2, c, :], start=c == 0, stop=c == 1)
                last.then_inc(o1T_ps, 1)

            for b in range(2):
                pe.wait_ge(emptied[b], EMPTIED[6][b])
            scores(0)
            for m in range(LT):
                run(fm_steps(6 + m, xTh, xTl, 0, T1))
            for m in range(2):
                run(fm_steps(10 + m, xTh, xTl, META, S))
            pe.wait_ge(small3, 64)
            for m in range(LT):
                pe.wait_ge(xc_ready, m // 2 + 1)
                pe.wait_ge(emptied[m % 2], EMPTIED[GATE_UNIT][m % 2] - LT // 2 + m // 2)
                if m == 0:
                    pe.wait_ge(v1_out, 1)
                elif m > 1:
                    pe.wait_ge(i_act, m - 1)
                mm(fm[:, m % 2, 0:T1], wa_bd[:, m, :], xc[:, m, :], start=True, stop=True)
                mm((ma, mb)[m % 2][:, 0:T1], wx_bd[:, m, :], xc[:, m, :], start=True, stop=True).then_inc(r_ps, 1)
            p_transposes(0)
            for m in range(2):
                run(fm_steps(12 + m, xTh, xTl, META, S))
            pe.wait_ge(i_act, LT)
            outputs(0)
            pe.wait_ge(o1T_lo, 1)
            for b in range(2):
                pe.wait_ge(emptied[b], EMPTIED[14][b])
            scores(1)
            pe.wait_ge(rec_lo, 1)
            for n in range(4):
                acc_unit(2 * P_OUT1 + n, yTh[:, 4 + n, :], yTl[:, 4 + n, :], n == 0, False)
            p_transposes(1)
            outputs(1)
            pe.wait_ge(o1T_lo, 2)
            acc_tail(range(2 * P_OUT1 + 4, 2 * P_OUT1 + 8), [(yTh[:, k, :], yTl[:, k, :]) for k in range(4)])
            transposes(u, u_ready, 3)
            pieces_ready()

            F = 2 * P_FF1

            def ffn1_up(fu, stride=0, i=0):
                for j in range(2):
                    run(fm_steps(fu + j, xTh, xTl, 0, S, stride=stride, i=i))

            def ffn1_down(fu, par, n0, stride=0, i=0, last_=False):
                pe.wait_ge(hid_lo, i * (stride // 2) + 2 * n0 + 2)
                for j in range(2):
                    acc_unit(fu + j, hid_h[:, par, j, :], hid_l[:, par, j, :], False, last_ and j == 1, stride, i)

            def open_acc():
                for q in range(4):
                    mm(acc[:, q, :], zero_r[:, :], junk0, start=True, stop=False, skip_group_check=True)

            junk0 = cst[:, 0:512]
            open_acc()
            ffn1_up(F)
            for i in rounds(pe, 7):
                ffn1_up(F + 2, 8, i)
                ffn1_down(F + 4, 0, 0, 8, i)
                ffn1_up(F + 6, 8, i)
                ffn1_down(F + 8, 1, 1, 8, i)
            ffn1_up(F + 58)
            ffn1_down(F + 60, 0, 14)
            pe.wait_ge(hid_lo, 32)
            acc_tail((F + 62, F + 63), [(hid_h[:, 1, j, :], hid_l[:, 1, j, :]) for j in range(2)])
            transposes(u, u_ready, 5)
            pieces_ready()
            pe.wait_ge(ab_lo, 1)
            for k in range(KC):
                last = three(ma[0:16, 0:S], ab_h[:, k, :], ab_l[:, k, :], xTh[:, k, 0:S], xTl[:, k, 0:S], k == 0, k == KC - 1)
            last.then_inc(ab_ps, 1)
            M, G = 2 * P_MOBA, 2 * P_GDN

            def pair_steps(kinds, fu, stride, i):
                for c in range(8):
                    if kinds[c] == "t":
                        yield from tok_steps(fu + c, 0, stride, i)
                    else:
                        yield from fm_steps(fu + c, xTh, xTl, 0, S, stride=stride, i=i)

            steps = pair_steps("ffffff" + "tt", M, 0, 0)
            for _ in range(16):
                next(steps)
            pe.wait_ge(ab_sb, 1)
            for t in range(NT):
                last = pe.transpose(ma[:, 256 + t * 16:256 + (t + 1) * 16], junk[0:16, t * P:(t + 1) * P], ident[0:16, 0:16])
            last.then_inc(abT_ps, 1)
            run(steps)
            pe.wait_ge(g_ready, 1)
            for c in range(2):
                mm(mb[:, c * 8:(c + 1) * 8], tri, g_all[:, 5, c, :], start=True, stop=True)
            for c in range(2):
                last = mm(mb[:, 16 + c * 8:16 + (c + 1) * 8], ones[:, :], g_all[:, 5, c, :], start=True, stop=True)
            last.then_inc(gc_ps, 1)

            def moba_stage(s, a):
                if s == 1:
                    pe.wait_ge(rope_out, a + 1)
                    for j in range(2):
                        mm(acc[:, j, 0:256], qr[:, j, P:2 * P], qr[:, 2 + j, :], start=True, stop=True)
                        last = mm(acc[:, j, 256:384], qr[:, j, 0:P], qr[:, 2 + j, 0:P], start=True, stop=True)
                    last.then_inc(s2_ps, 1)
                if s == 3:
                    pe.wait_ge(s2_p, a + 1)
                    for j in range(2):
                        for c in range(3):
                            last = pe.transpose(acc[:, 2 + j, c * P:(c + 1) * P], p2[:, j, c * P:(c + 1) * P], ident)
                    last.then_inc(p2T_ps, 1)
                if s == 4:
                    pe.wait_ge(p2T_a, a + 1)
                    pe.wait_ge(p2T_v, a + 1)
                    for j in range(2):
                        hd = slice(j * P, (j + 1) * P)
                        mm(ma[:, j * 256:j * 256 + P], va[:, 0, hd], pT2[:, j, 256:384], start=True, stop=True)
                        mm(ma[:, j * 256 + P:(j + 1) * 256], va[:, 0, hd], pT2[:, j, 0:P], start=True, stop=False)
                        last = mm(ma[:, j * 256 + P:(j + 1) * 256], va[:, 1, hd], pT2[:, j, P:2 * P], start=False, stop=True)
                    last.then_inc(o2_ps, 1)

            def gdn_stage(s, a):
                if s == 1:
                    for n, q in enumerate((1, 0)):
                        pe.wait_ge(sq_out, a * 2 + (n + 1))
                        mm(acc[:, q, :], ones[:, :], sq[:, q * 512:(q + 1) * 512], start=True, stop=True).then_inc(ssq_ps, 1)
                if s == 2:
                    for pr in range(4):
                        c, j = pr // 2, pr % 2
                        last = pe.transpose(acc[:, 3, pr * P:(pr + 1) * P], cv[:, 4 + j, c * P:(c + 1) * P], ident)
                    last.then_inc(vT_ps, 1)
                if s == 3:
                    pe.wait_ge(qkn_out, a * 2 + 2)
                    for pr in range(4):
                        c, j = pr // 2, pr % 2
                        k = cv[:, 2 + j, c * P:(c + 1) * P]
                        last = mm(acc[:, 1, pr * P:(pr + 1) * P], k, k, start=True, stop=True)
                    last.then_inc(kk_ps, 1)
                    for pr in range(4):
                        c, j = pr // 2, pr % 2
                        last = pe.transpose(acc[:, 0, pr * P:(pr + 1) * P], cv[:, 2 + j, c * P:(c + 1) * P], ident)
                    last.then_inc(kT_ps, 1)
                    for pr in range(4):
                        c, j = pr // 2, pr % 2
                        last = mm(acc[:, 2, pr * P:(pr + 1) * P], cv[:, 2 + j, c * P:(c + 1) * P], cv[:, j, c * P:(c + 1) * P], start=True, stop=True)
                    last.then_inc(kq_ps, 1)
                if s == 4:
                    pe.wait_ge(x0_out, a + 1)
                    pe.wait_ge(vb_out, a + 1)
                    for pr in range(4):
                        last = pe.transpose(acc[:, 3, pr * P:(pr + 1) * P], X_[:, pr, :], ident)
                    last.then_inc(xt0_ps, 1)
                if 5 <= s < 17 and s % 2 == 1:
                    lv = (s - 5) // 2 + 1
                    if lv == 1:
                        pe.wait_ge(xt0_out, a + 1)
                        pe.wait_ge(kv_out, a + 1)
                        pe.wait_ge(attn_out, a + 1)
                    for g in range(2):
                        if lv > 1:
                            pe.wait_ge(lv_xt[g], a * 6 + (lv - 1))
                        for j in range(2):
                            last = mm(acc[:, 3 * g, j * P:(j + 1) * P], A_[:, 2 * g + j, :], XT_[:, 2 * g + j, :], start=True, stop=True)
                        last.then_inc(lv_p[g], 1)
                if 5 <= s < 17 and s % 2 == 0:
                    lv = (s - 5) // 2 + 1
                    for g in range(2):
                        pe.wait_ge(lv_pm[g], a * 6 + lv)
                        if lv > 1:
                            pe.wait_ge(lv_x[g], a * 5 + (lv - 1))
                        for j in range(2):
                            pr = 2 * g + j
                            last = mm(acc[:, 1 + g, j * P:(j + 1) * P], X_[:, pr, :], PM_[:, pr, :], start=True, stop=True)
                        if lv < 6:
                            for j in range(2):
                                pr = 2 * g + j
                                last = mm(acc[:, 1 + g, (2 + j) * P:(3 + j) * P], PM_[:, pr, :], X_[:, pr, :], start=True, stop=True)
                        last.then_inc(lv_z[g], 1)
                if s == 17:
                    for g in range(2):
                        pe.wait_ge(lv_xt[g], a * 6 + 6)
                    for j in range(2):
                        mm(acc[:, 3, j * P:(j + 1) * P], XT_[:, j, :], vb[:, j, :], start=True, stop=True)
                    for j in range(2):
                        last = mm(acc[:, 0, j * P:(j + 1) * P], kbe[:, j, :], XT_[:, 2 + j, :], start=True, stop=True)
                    last.then_inc(uw_ps, 1)
                if s == 18:
                    pe.wait_ge(u0_out, a + 1)
                    for j in range(2):
                        last = mm(acc[:, 1, j * P:(j + 1) * P], kdec[:, j, :], u0[:, j, :], start=True, stop=True)
                    last.then_inc(so_ps, 1)
                    for j in range(2):
                        mm(acc[:, 2, j * P:(j + 1) * P], attnT[:, j, :], u0[:, j, :], start=True, stop=True)
                if s == 19:
                    pe.wait_ge(S1_out, a + 1)
                    pe.wait_ge(nw_out, a + 1)
                    for j in range(2):
                        out = acc[:, 3, (2 + j) * P:(3 + j) * P]
                        mm(out, XT_[:, 2 + j, :], vb[:, 2 + j, :], start=True, stop=False)
                        last = mm(out, nwT[:, j, :], S1[:, j, :], start=False, stop=True)
                    last.then_inc(vn_ps, 1)
                if s == 20:
                    pe.wait_ge(vn_out, a + 1)
                    for j in range(2):
                        out = acc[:, 2, (2 + j) * P:(3 + j) * P]
                        mm(out, qeg[:, j, :], S1[:, j, :], start=True, stop=False)
                        last = mm(out, attnT[:, 2 + j, :], vn[:, j, :], start=False, stop=True)
                    last.then_inc(o_ps, 1)
                if s == 9 and not (isinstance(a, int) and a == PAIRS - 1):
                    g_rows(a + 1)
                if s == 13 and not (isinstance(a, int) and a == 0):
                    out_transposes(a - 1)

            def g_rows(b):
                pe.wait_ge(gb_out, b + 1)
                for pr in range(4):
                    last = mm(mb[:, pr * P:(pr + 1) * P], gb[:, pr, :], tri, start=True, stop=True)
                last.then_inc(gcb_ps, 1)

            def out_transposes(b):
                pe.wait_ge(y_out, b + 1)
                for pr in range(4):
                    last = pe.transpose(ma[:, pr * P:(pr + 1) * P], y_[:, pr, :], ident)
                last.then_inc(yT_ps, 1)

            def pair_round(weave, stage, kinds, fu, a):
                steps = pair_steps(kinds, fu, 8, a)
                for s, n in enumerate(weave):
                    stage(s, a)
                    for _ in range(n):
                        next(steps)

            for i in rounds(pe, 3):
                pair_round(MOBA_WEAVE, moba_stage, "fffffftt", M + 8, i)
            pair_round(MOBA_WEAVE, moba_stage, "fffffftt", M + 8, 3)
            g_rows(0)
            pair_round(GDN_WEAVE, gdn_stage, "fffffftt", G + 8, 0)
            for i in rounds(pe, 2):
                pair_round(GDN_WEAVE, gdn_stage, "fffffftt", G + 8, i + 1)
            pair_round(GDN_WEAVE, gdn_stage, "ffffffff", G + 8, 3)
            pe.wait_ge(o2_lo, PAIRS)
            for m in range(KC):
                run(fm_steps(2 * P_PROJA + m, yTh, yTl, 0, S))
                if m == 1:
                    out_transposes(3)
            pe.wait_ge(yb_lo, PAIRS)
            for m in range(KC):
                run(fm_steps(2 * P_PROJB + m, ybh, ybl, 0, S))
            pe.wait_ge(mg_lo, 1)
            for k in range(4):
                acc_unit(2 * P_OUT2 + k, yTh[:, k, :], yTl[:, k, :], k == 0, False)
            pe.wait_ge(mg_lo, 2)
            pe.wait_ge(p_loaded, 16)
            for t in range(NT):
                for k in range(2):
                    last = pe.transpose(ma[:, (2 * t + k) * P:(2 * t + k + 1) * P], p_in[:, t, k * P:(k + 1) * P], ident)
            last.then_inc(pT_ps, 1)
            for k in range(4, 6):
                acc_unit(2 * P_OUT2 + k, yTh[:, k, :], yTl[:, k, :], False, False)
            acc_tail(range(2 * P_OUT2 + 6, 2 * P_OUT2 + 8), [(yTh[:, k, :], yTl[:, k, :]) for k in range(6, 8)])
            pe.wait_ge(pT_lo, 1)
            pe.wait_ge(emptied[0], EMPTIED0[2 * P_PLE])
            pe.wait_ge(emptied[1], EMPTIED1[2 * P_PLE])
            for k in range(2):
                acc_unit(2 * P_PLE + k, pT_h[:, k, :], pT_l[:, k, :], k == 0, k == 1, into=high)
            transposes(u, u_ready, 7)
            pieces_ready()
            F2 = 2 * P_FF2

            def slice_up(fu, banks, read, need, stride=0, i=0):
                for j in range(2):
                    unit_ready(fu + j, stride, i)
                    if need is not None:
                        pe.wait_ge(read, i * (stride // 3) + need + j)
                    a, b = (split_view(w, (fu + j) % UNITS, "cols") for w in (wh, wl))
                    for k in range(KC):
                        last = three(banks[j], a[:, k, :], b[:, k, :], xTh[:, k, 0:S], xTl[:, k, 0:S], k == 0, k == KC - 1)
                    last.then_inc(unit_done, 1)

            def ffn2_down(fu, k, stride=0, i=0, last_=False):
                pe.wait_ge(swi_lo, i * (stride // 3) + 2 * k + 2)
                for j in range(2):
                    acc_unit(fu + j, hid2_h[:, j, :], hid2_l[:, j, :], False, last_ and j == 1, stride, i)

            pe.wait_ge(emptied[0], EMPTIED0[F2])
            pe.wait_ge(emptied[1], EMPTIED1[F2])
            open_acc()
            gates, ups = (fm[:, 0, 0:S], fm[:, 1, 0:S]), (ma[:, 0:S], mb[:, 0:S])
            slice_up(F2, gates, swi_a, None)
            slice_up(F2 + 2, ups, swi_m, None)
            for i in rounds(pe, 5):
                for n in range(2):
                    slice_up(F2 + 4 + 6 * n, gates, swi_a, 2 * n + 1, 12, i)
                    ffn2_down(F2 + 6 + 6 * n, n, 12, i)
                    slice_up(F2 + 8 + 6 * n, ups, swi_m, 2 * n + 1, 12, i)
            pe.wait_ge(swi_lo, 22)
            acc_tail((F2 + 64, F2 + 65), [(hid2_h[:, j, :], hid2_l[:, j, :]) for j in range(2)])
            transposes(h, h_ready, 6)
            pieces_ready()
            for k in range(4):
                acc_unit(2 * P_PGATE + k, xTh[:, k, 0:S], xTl[:, k, 0:S], k == 0, False)
            acc_tail(range(2 * P_PGATE + 4, 2 * P_PGATE + 8), [(xTh[:, k, 0:S], xTl[:, k, 0:S]) for k in range(4, 8)])


_INS = ["x", "meta_tokens", "g_pre_mix", "w_in", "conv_w", "conv_b", "w_a", "b_a", "w_x", "b_x", "lru_lambda",
        "attn_sinks", "w_out", "g_post_mix", "g_pre_ffn", "w_ff1", "w_ff2", "g_post_ffn", "p_2", "ln_pre_mix_2",
        "w_in_2", "conv_w_2", "a_log_2", "dt_bias_2", "gdn_norm_2", "w_proj_a_2", "w_proj_b_2", "w_out_2",
        "ln_post_mix_2", "ln_pre_ffn_2", "w_ffn_gate_2", "w_ffn_up_2", "w_ffn_down_2", "ln_post_ffn_2", "w_ple_2",
        "ln_ple_2", "w_ple_gate_2"]


def kernel(**inputs):
    import concourse.bacc as _bacc
    from concourse.bass_utils import run_bass_kernel_spmd as _run

    nc = _bacc.Bacc("TRN2", target_bir_lowering=False, num_devices=1)
    arrays, aps = {}, {}
    for name in _INS:
        a = np.ascontiguousarray(inputs[name])
        arrays[f"in_{name}_dram"] = a
        aps[name] = nc.dram_tensor(f"in_{name}_dram", a.shape, mybir.dt.from_np(a.dtype), kind="ExternalInput").ap()
    table = constant_table()
    arrays["constants_dram"] = table
    aps["cst"] = nc.dram_tensor("constants_dram", table.shape, F32, kind="ExternalInput").ap()
    aps["out"] = nc.dram_tensor("out_0_dram", (1, S, D), F32, kind="ExternalOutput").ap()
    build(nc, aps)
    r = _run(nc, [arrays], core_ids=[0])
    return r.results[0]["out_0_dram"]
```
